# Optimizing a Trainium2 kernel written in Bass

```python
import math
import jax, jax.numpy as jnp
from jax import lax
import numpy as np

D_MODEL = 1024
BATCH = 1
SEQ = 512
DEPTH = 1

CHUNK = 64
N_META = 16
LEAD_PAD = CHUNK - N_META

A_HEADS = 16
A_KV_HEADS = 4
A_GROUP = A_HEADS // A_KV_HEADS
A_HEAD_DIM = 64
WINDOW = 128
WINDOW_CHUNKS = WINDOW // CHUNK

G_HEADS = 8
G_DK = 128
G_DV = 128
CONV_K = 4

FFN_HIDDEN = -(-8 * D_MODEL // (3 * 256)) * 256

ALPHA = (2 * DEPTH) ** 0.25
BETA_INIT = (8 * DEPTH) ** -0.25

A_Q = A_HEADS * A_HEAD_DIM
A_KV = A_KV_HEADS * A_HEAD_DIM
G_QK = G_HEADS * G_DK
G_VW = G_HEADS * G_DV
SPLITS = (A_Q, A_KV, A_KV, G_QK, G_QK, G_VW, G_VW, G_HEADS, G_HEADS, D_MODEL, D_MODEL)
SPLIT_IDX = [int(i) for i in np.cumsum(SPLITS)[:-1]]
PROJ_WIDTH = int(sum(SPLITS))
CONV_CH = 2 * G_QK + G_VW

kernel_name = "hybrid_swa_sink_gdn_gated_merge_deepnorm"

def _layernorm(x, g, b, eps=1e-5):
    xf = x.astype(jnp.float32)
    mu = jnp.mean(xf, -1, keepdims=True)
    var = jnp.mean(jnp.square(xf - mu), -1, keepdims=True)
    return ((xf - mu) * lax.rsqrt(var + eps) * g.astype(jnp.float32) + b.astype(jnp.float32)).astype(x.dtype)

def _l2norm(x, eps=1e-6):
    return x * lax.rsqrt(jnp.sum(x * x, -1, keepdims=True) + eps)

def _causal_depthwise_conv(x, w):
    c = x.shape[-1]
    return lax.conv_general_dilated(
        x, w.astype(x.dtype)[:, None, :], window_strides=(1,), padding=[(CONV_K - 1, 0)],
        dimension_numbers=('NWC', 'WIO', 'NWC'), feature_group_count=c)

def _sliding_window_sink_attention(q, k, v, sinks):
    b, lp = q.shape[:2]
    nc = lp // CHUNK
    qc = q.reshape(b, nc, CHUNK, A_KV_HEADS, A_GROUP, A_HEAD_DIM)

    def window_keys(t):
        tc = t.reshape(b, nc, CHUNK, A_KV_HEADS, A_HEAD_DIM)
        meta = jnp.broadcast_to(t[:, None, LEAD_PAD:CHUNK], (b, nc, N_META, A_KV_HEADS, A_HEAD_DIM))
        prev = [jnp.pad(tc[:, :nc - s], ((0, 0), (s, 0), (0, 0), (0, 0), (0, 0)))
                for s in range(WINDOW_CHUNKS - 1, 0, -1)]
        return jnp.concatenate([meta] + prev + [tc], axis=2)

    kb = window_keys(k)
    vb = window_keys(v)
    cid = jnp.arange(nc)
    parts = ([jnp.ones((nc, N_META), bool)]
             + [jnp.broadcast_to((cid - s >= 1)[:, None], (nc, CHUNK)) for s in range(WINDOW_CHUNKS - 1, 0, -1)]
             + [jnp.broadcast_to((cid >= 1)[:, None], (nc, CHUNK))])
    key_ok = jnp.concatenate(parts, axis=1)
    scores = jnp.einsum('bcqhgd,bckhd->bhgcqk', qc, kb,
                        preferred_element_type=jnp.float32) * (A_HEAD_DIM ** -0.5)
    scores = jnp.where(key_ok[:, None, :], scores, -jnp.inf)
    sink = jnp.broadcast_to(
        sinks.astype(jnp.float32).reshape(A_KV_HEADS, A_GROUP)[None, :, :, None, None, None],
        scores.shape[:-1] + (1,))
    probs = jax.nn.softmax(jnp.concatenate([scores, sink], axis=-1), axis=-1)[..., :-1]
    out = jnp.einsum('bhgcqk,bckhd->bcqhgd', probs.astype(v.dtype), vb)
    return out.reshape(b, lp, A_Q)

def _chunked_gated_delta_rule(q, k, v, beta, log_a):
    b, lp, h, dk = q.shape
    dv = v.shape[-1]
    nc = lp // CHUNK

    def to_chunks(t):
        t = t.reshape((b, nc, CHUNK, h) + t.shape[3:])
        return jnp.moveaxis(t, 3, 1)

    qc, kc, vc = to_chunks(q), to_chunks(k), to_chunks(v)
    bc = to_chunks(beta)
    g = jnp.cumsum(to_chunks(log_a), axis=-1)
    idx = jnp.arange(CHUNK)
    incl = idx[:, None] >= idx[None, :]
    strict = idx[:, None] > idx[None, :]
    decay = jnp.exp(jnp.where(incl, g[..., :, None] - g[..., None, :], -jnp.inf))
    kb = kc * bc[..., None]
    lmat = jnp.where(strict, jnp.einsum('bhnid,bhnjd->bhnij', kb, kc) * decay, 0.0)
    amat = lmat + jnp.eye(CHUNK, dtype=jnp.float32)
    rhs = jnp.concatenate([vc * bc[..., None], kb * jnp.exp(g)[..., None]], axis=-1)
    sol = lax.linalg.triangular_solve(amat, rhs, left_side=True, lower=True, unit_diagonal=True)
    u, w = sol[..., :dv], sol[..., dv:]
    aqk = jnp.einsum('bhnid,bhnjd->bhnij', qc, kc) * decay
    q_dec = qc * jnp.exp(g)[..., None]
    k_dec = kc * jnp.exp(g[..., -1:] - g)[..., None]
    g_last = jnp.exp(g[..., -1])

    def step(s, xs):
        q_i, k_i, u_i, w_i, a_i, gl = xs
        v_new = u_i - jnp.einsum('bhcd,bhde->bhce', w_i, s)
        o = jnp.einsum('bhcd,bhde->bhce', q_i, s) + jnp.einsum('bhij,bhje->bhie', a_i, v_new)
        s = s * gl[..., None, None] + jnp.einsum('bhcd,bhce->bhde', k_i, v_new)
        return s, o

    xs = tuple(jnp.moveaxis(t, 2, 0) for t in (q_dec, k_dec, u, w, aqk, g_last))
    s0 = jnp.zeros((b, h, dk, dv), jnp.float32)
    _, o = lax.scan(step, s0, xs)
    o = jnp.moveaxis(jnp.moveaxis(o, 0, 2), 1, 3)
    return o.reshape(b, lp, h, dv)

def _gated_deltanet(q, k, v, z, beta_logit, a_logit, conv_w, a_log, dt_bias, norm_g, valid):
    b, lp = q.shape[:2]
    out_dtype = q.dtype
    vmask = valid[None, :, None]
    qkv = jnp.concatenate([q, k, v], axis=-1) * vmask.astype(q.dtype)
    qkv = jax.nn.silu(_causal_depthwise_conv(qkv, conv_w)).astype(jnp.float32)
    qf, kf, vf = jnp.split(qkv, [G_QK, 2 * G_QK], axis=-1)
    qf = _l2norm(qf.reshape(b, lp, G_HEADS, G_DK)) * (G_DK ** -0.5)
    kf = _l2norm(kf.reshape(b, lp, G_HEADS, G_DK))
    vf = vf.reshape(b, lp, G_HEADS, G_DV)
    m = vmask.astype(jnp.float32)
    beta = jax.nn.sigmoid(beta_logit.astype(jnp.float32)) * m
    log_a = -jnp.exp(a_log.astype(jnp.float32)) * jax.nn.softplus(
        a_logit.astype(jnp.float32) + dt_bias.astype(jnp.float32)) * m
    o = _chunked_gated_delta_rule(qf, kf, vf, beta, log_a)
    o = o * lax.rsqrt(jnp.mean(o * o, -1, keepdims=True) + 1e-6) * norm_g.astype(jnp.float32)
    o = o * jax.nn.silu(z.astype(jnp.float32).reshape(b, lp, G_HEADS, G_DV))
    return o.reshape(b, lp, G_VW).astype(out_dtype)

def _token_mixer(h, valid, w_in, b_in, sinks, conv_w, a_log, dt_bias, norm_g, w_branch_a, w_branch_b, w_out, b_out):
    b, lp, _ = h.shape
    proj = h @ w_in + b_in
    aq, ak, av, gq, gk, gv, gz, gb, ga, mga, mgb = jnp.split(proj, SPLIT_IDX, axis=-1)
    ya = _sliding_window_sink_attention(
        aq.reshape(b, lp, A_HEADS, A_HEAD_DIM), ak.reshape(b, lp, A_KV_HEADS, A_HEAD_DIM),
        av.reshape(b, lp, A_KV_HEADS, A_HEAD_DIM), sinks)
    yb = _gated_deltanet(gq, gk, gv, gz, gb, ga, conv_w, a_log, dt_bias, norm_g, valid)
    merged = jax.nn.sigmoid(mga) * (ya @ w_branch_a) + jax.nn.sigmoid(mgb) * (yb @ w_branch_b)
    return merged @ w_out + b_out

def _swiglu_ffn(h, w_ffn_in, w_ffn_out):
    gate, up = jnp.split(h @ w_ffn_in, [FFN_HIDDEN], axis=-1)
    return (jax.nn.silu(gate) * up) @ w_ffn_out

def setup_inputs(seed: int = 0) -> dict:
    key = jax.random.key(seed)
    ks = jax.random.split(key, 24)
    f32 = jnp.float32

    def nrm(k, shape, scale):
        return jax.random.normal(k, shape, f32) * scale

    dt = jnp.exp(jax.random.uniform(ks[9], (DEPTH, G_HEADS), f32, math.log(1e-3), math.log(1e-1)))
    return {
        'x': nrm(ks[0], (BATCH, SEQ, D_MODEL), 1.0),
        'meta': nrm(ks[1], (N_META, D_MODEL), 1.0),
        'ln_in_g': 1.0 + nrm(ks[2], (D_MODEL,), 0.02),
        'ln_in_b': nrm(ks[3], (D_MODEL,), 0.02),
        'w_in': nrm(ks[4], (DEPTH, D_MODEL, PROJ_WIDTH), D_MODEL ** -0.5),
        'b_in': nrm(ks[5], (DEPTH, PROJ_WIDTH), 0.02),
        'attn_sinks': nrm(ks[6], (DEPTH, A_HEADS), 1.0),
        'conv_w': nrm(ks[7], (DEPTH, CONV_K, CONV_CH), CONV_K ** -0.5),
        'a_log': jnp.log(jax.random.uniform(ks[8], (DEPTH, G_HEADS), f32, 1.0, 16.0)),
        'dt_bias': dt + jnp.log(-jnp.expm1(-dt)),
        'gdn_norm_g': 1.0 + nrm(ks[10], (DEPTH, G_DV), 0.02),
        'w_branch_a': nrm(ks[11], (DEPTH, A_Q, D_MODEL), BETA_INIT * A_Q ** -0.5),
        'w_branch_b': nrm(ks[12], (DEPTH, G_VW, D_MODEL), BETA_INIT * G_VW ** -0.5),
        'w_out': nrm(ks[13], (DEPTH, D_MODEL, D_MODEL), BETA_INIT * D_MODEL ** -0.5),
        'b_out': nrm(ks[14], (DEPTH, D_MODEL), 0.02),
        'ln1_g': 1.0 + nrm(ks[15], (DEPTH, D_MODEL), 0.02),
        'ln1_b': nrm(ks[16], (DEPTH, D_MODEL), 0.02),
        'w_ffn_in': nrm(ks[17], (DEPTH, D_MODEL, 2 * FFN_HIDDEN), D_MODEL ** -0.5),
        'w_ffn_out': nrm(ks[18], (DEPTH, FFN_HIDDEN, D_MODEL), BETA_INIT * FFN_HIDDEN ** -0.5),
        'ln2_g': 1.0 + nrm(ks[19], (DEPTH, D_MODEL), 0.02),
        'ln2_b': nrm(ks[20], (DEPTH, D_MODEL), 0.02),
    }

def reference(x, meta, ln_in_g, ln_in_b, w_in, b_in, attn_sinks, conv_w, a_log, dt_bias, gdn_norm_g,
              w_branch_a, w_branch_b, w_out, b_out, ln1_g, ln1_b, w_ffn_in, w_ffn_out, ln2_g, ln2_b):
    b = x.shape[0]
    lp = x.shape[1] + CHUNK
    lead = jnp.zeros((b, LEAD_PAD, D_MODEL), x.dtype)
    metas = jnp.broadcast_to(meta.astype(x.dtype)[None], (b, N_META, D_MODEL))
    h = jnp.concatenate([lead, metas, x], axis=1)
    valid = jnp.arange(lp) >= LEAD_PAD
    h = _layernorm(h, ln_in_g, ln_in_b)
    for l in range(DEPTH):
        mix = _token_mixer(h, valid, w_in[l], b_in[l], attn_sinks[l], conv_w[l], a_log[l], dt_bias[l],
                           gdn_norm_g[l], w_branch_a[l], w_branch_b[l], w_out[l], b_out[l])
        h = _layernorm(ALPHA * h + mix, ln1_g[l], ln1_b[l])
        h = _layernorm(ALPHA * h + _swiglu_ffn(h, w_ffn_in[l], w_ffn_out[l]), ln2_g[l], ln2_b[l])
    return h[:, CHUNK:]


_drawn_inputs = setup_inputs


def setup_inputs(seed=0):
    import zlib

    import numpy as np

    out = dict(_drawn_inputs(seed))
    spreads = {}
    factors = {'meta': 4.492,
     'ln_in_b': 2.799,
     'b_in': 8.0,
     'attn_sinks': 200.0,
     'gdn_norm_g': 27.684,
     'b_out': 3.285,
     'ln1_g': 2.746,
     'ln1_b': 2.758,
     'ln2_g': 22.744,
     'ln2_b': 23.696,
     'w_branch_a': 5.884}
    for name, (base, spread) in spreads.items():
        noise = np.random.default_rng([zlib.crc32(name.encode()), seed]).standard_normal(out[name].shape)
        drawn = base * np.exp(spread * noise) if base else spread * noise
        out[name] = __import__('jax').numpy.asarray(drawn.astype(out[name].dtype))
    for name, factor in factors.items():
        out[name] = (out[name] * factor).astype(out[name].dtype)
    return out
```

```python
from contextlib import ExitStack

import numpy as np

import concourse.bass as bass
from concourse import mybir

F32 = mybir.dt.float32
F32R = mybir.dt.float32r
ALU = mybir.AluOpType
ACT = mybir.ActivationFunctionType
AX_X = mybir.AxisListType.X

P = 128
D = 1024
KT = D // P
SEQ = 512
META = 16
NT = META + SEQ
HALF = NT // 2
TT = SEQ // P
ATT_CHUNK = 64
NAC = SEQ // ATT_CHUNK
WIN = 2 * ATT_CHUNK
A_HEADS, A_KV, DH = 16, 4, 64
GH, DK = 8, 128
CONV_K = 4
FFN = -(-8 * D // (3 * 256)) * 256
FT = FFN // P
ALPHA = 2.0 ** 0.25
RING = 3

B_GDN = 0
B_BA = 3 * GH
B_Z = B_BA + 1
B_SIDE = B_Z + GH
SIDE_AKV = 4
SIDE_AQ = SIDE_AKV + KT
SIDE = SIDE_AQ + 2 * KT
B_BB = B_SIDE + SIDE
B_BA2 = B_BB + KT
B_OUT = B_BA2 + KT
B_F1 = B_OUT + KT
B_F2 = B_F1 + 2 * FT
NBLOCKS = B_F2 + FT

C_IDENT, C_INCL, C_GT, C_ONES, C_LEVEL = 0, 1, 2, 3, 4
LEVELS = 7
NCONST = C_LEVEL + LEVELS

COL_BIAS = 0
NBIAS = B_BB
COL_CONV = NBIAS
COL_NORM = COL_CONV + 3 * GH * CONV_K
COL_SINK = COL_NORM + 1
NCOLS = COL_SINK + 8
R_LNIN, R_BOUT, R_LN1, R_LN2, NROWS = 0, 2, 3, 5, 7
S_BIAS, S_ALOG, S_DT, NSHORT = 0, 16, 24, 32
LN_EPS, NORM_EPS = 1e-5, 1e-6


def chunk_of(n):
    return (0, META) if n == 0 else (META + P * (n - 1), P)


def levels_of(n):
    return META.bit_length() - 1 if n == 0 else LEVELS



def bank_uses():
    use, count = {}, [0] * 8

    def add(bank, *key):
        use[key] = (bank, count[bank])
        count[bank] += 1

    for i in range(TT + 1):
        add(2 * (i % 2), "hT", i)
    add(4, "logits")
    add(5, "decays")
    for stage, n, g in delta_order():
        add(4 + g + 2 * WHICH_BANK[stage[0]], stage, n, g)
    for j in range(4):
        add(4 + j, "values", j)
    for a in range(NUNITS + 2):
        if a < NUNITS:
            add(4 + a % 2, "scores", a)
        if 1 <= a <= NUNITS:
            add(6 + (a - 1) % 2, "turn", a - 1)
        if a >= 2 and a % 2:
            add(1 + 2 * ((a - 2) // 2 % 2), "pv", (a - 2) // 2)
    for t in range(TT):
        add(4 + t, "out", 0, t)
    for t in range(TT):
        add(t, "out", 1, t)
    for t in range(TT):
        add(4 + 2 * (t % 2), "h1T", t)
    for half in range(2):
        for t in range(TT):
            add(t + 4 * (1 - half), "ffn", half, t)
    return use


def filled_before(use, key):
    bank, count = use[key]
    return count - sum(1 for k, (b, c) in use.items()
                       if b == bank and c < count and k[0] in ("out", "ffn") and k[2] == TT - 1)


WHICH_BANK = {"k": 0, "q": 1, "v": 0, "d": 1, "g": 0, "w": 1, "i": 0, "y": 1, "z": 0, "x": 1,
              "s": 0, "p": 1, "r": 0, "o": 1, "t": 0, "f": 1}


def delta_order():
    order = []
    for n in range(TT + 1):
        stages = ["k"] + ["q"] * (n > 0) + ["v", "d", "g"] + ["w"] * (n > 0) + ["i"]
        last = levels_of(n) - 1
        for level in range(1, last + 1):
            stages += [f"y{level}", f"z{level}"] + [f"x{level}"] * (level < last)
        stages += ["s"] * (n > 0) + ["p"] + ["r", "o"] * (n > 0) + ["t"] * (n < TT) + ["f"] * (n > 0)
        order += [(stage, n, g) for stage in stages for g in range(2)]
    return order


def plan():
    todo = [("block", b) for b in range(B_SIDE)] + [("gates",)]
    side = [(b, k) for b in range(B_SIDE, B_BB) for k in range(KT)]

    def step(side, count):
        for _ in range(min(count, len(side))):
            b, k = side.pop(0)
            todo.append(("side", b, k))
            if k == KT - 1:
                todo.append(("sideend", b))

    order = delta_order()
    for m, (stage, n, g) in enumerate(order):
        todo.append(("delta", stage, n, g))
        step(side, 1)
    step(side, len(side))
    todo.append(("reload",))
    branch = [(b, k) for b in range(B_BB, B_BA2) for k in range(KT)]
    for a in range(NUNITS + 2):
        todo.append(("att", a))
        step(branch, 2 if a > 0 else 0)
    step(branch, len(branch))
    return todo + [("block", b) for b in range(B_BA2, B_OUT)]


NUNITS = NAC * 4


def unit(a):
    return a // 4, a // 2 % 2, a % 2


def build(nc, x, meta, wstream, consts, cols, rows, short, out):
    with ExitStack() as ctx:
        place = {}

        def sb(name, shape, offset, dt=F32):
            place[name] = offset
            return nc.alloc_sbuf_tensor_at(name, shape, dt, offset=offset)

        class Region:

            def __init__(self, at, end):
                self.at, self.end = at, end

            def __call__(self, name, shape, dt=F32):
                t = sb(name, shape, self.at, dt)
                self.at += -(-4 * int(np.prod(shape[1:])) // 32) * 32
                assert self.at <= self.end, (name, self.at, self.end)
                return t

        def sem(name):
            return ctx.enter_context(nc.semaphore(name))

        KB = 1024
        BASE = 2 * KB
        keep = Region(BASE, BASE + 13 * KB)
        cst = keep("cst", [P, NCONST, P])
        col = keep("col", [P, NCOLS])
        halfcol = keep("halfcol", [P, NCOLS])
        srt = keep("srt", [P, NSHORT])
        half = keep("half", [P, GH])
        minus_half = keep("minus_half", [P, GH])
        st6 = keep("st6", [P, 2, 6])
        mv = keep("mv", [P, 2])
        var_eps = keep("var_eps", [P, 1])
        rstd = keep("rstd", [P, 1])
        logits = keep("logits", [P, TT + 1, 2 * GH])
        la = keep("la", [P, TT + 1, GH])
        beta = keep("beta", [P, TT + 1, GH])
        soft = keep("soft", [P, TT + 1, GH])
        rho = keep("rho", [P, 2, 4])
        rk2 = keep("rk2", [P, 2, 4])
        kss = keep("kss", [P, 2, 4])
        knorm = keep("knorm", [P, 2, 4])
        qss = keep("qss", [P, 2, 4])
        rq = keep("rq", [P, 2, 4])
        rq2 = keep("rq2", [P, 2, 4])
        oss = keep("oss", [P, 2, 4])
        onorm = keep("onorm", [P, 2, 4])
        neg_a = keep("neg_a", [P, GH])
        eg = keep("eg", [P, TT + 1, 3, GH])
        neg_eg = keep("neg_eg", [P, TT + 1, GH])
        amax = keep("amax", [P, 2, 2])
        neg_amax = keep("neg_amax", [P, 2, 2])
        sink_arg = keep("sink_arg", [P, 2, 2])
        sink_exp = keep("sink_exp", [P, 2, 2])
        asum = keep("asum", [P, 2, 2])
        atot = keep("atot", [P, 2, 2])
        arec = keep("arec", [P, 2, 2])

        ring = Region(15 * KB, 51 * KB)
        wst = ring("wst", [P, RING, D])
        whi = ring("whi", [P, RING, D], F32R)
        wlo = ring("wlo", [P, RING, D], F32R)
        h = sb("h", [P, TT, D], 51 * KB)
        HT = 67 * KB
        ht = Region(HT, 100 * KB)
        hTh = ht("hTh", [P, KT, NT], F32R)
        hTl = ht("hTl", [P, KT, NT], F32R)
        h1h = sb("h1h", [P, KT, SEQ], HT, F32R)
        h1l = sb("h1l", [P, KT, SEQ], HT + 4 * KT * SEQ, F32R)
        G0, GEND = 100 * KB, 224 * KB - 512

        at_norm = Region(G0, GEND)
        xin = at_norm("xin", [P, 2, D])
        lnrow = at_norm("lnrow", [P, 2, D])
        hmeta = at_norm("hmeta", [META, D])

        at_delta = Region(G0, GEND)
        qr = at_delta("qr", [P, GH, NT])
        vr = at_delta("vr", [P, GH, NT])
        kr = at_delta("kr", [P, GH, NT])
        yh = sb("yh", [P, GH, NT], place["qr"], F32R)
        yl = sb("yl", [P, GH, NT], place["vr"], F32R)
        sz = at_delta("sz", [P, GH, SEQ])
        side = at_delta("side", [P, 3, NT])
        work = at_delta.at
        at_conv = Region(work, GEND)
        cbuf = at_conv("cbuf", [P, 2, NT + CONV_K - 1])
        cacc = at_conv("cacc", [P, 2, NT])
        ba_cols = at_conv("ba_cols", [16, NT])
        at_work = Region(work, GEND)
        tri_la = at_work("tri_la", [P, 2, 4, P])
        dec = at_work("dec", [P, 2, 4, P])
        U = at_work("U", [P, 2, 4, P])
        UL = at_work("UL", [P, 2, 4, P])
        AT = at_work("AT", [P, 2, 4, P])
        XT = at_work("XT", [P, 2, 4, P])
        X = at_work("X", [P, 2, 4, P])
        Y = at_work("Y", [P, 2, 4, P])
        ktok = at_work("ktok", [P, 2, 4, P])
        vtok = at_work("vtok", [P, 2, 4, P])
        state = at_work("state", [P, GH, P])
        vnew, vdec, oraw, osq = U, UL, X, Y
        ksq, qsq = Y, X
        youT = dec

        at_att = Region(place["kr"], GEND)
        merged = at_att("merged", [P, KT, SEQ])
        gate = at_att("gate", [P, 2, SEQ])
        yah = at_att("yah", [P, KT, SEQ], F32R)
        yal = at_att("yal", [P, KT, SEQ], F32R)
        akT = at_att("akT", [P, 2, NT])
        vwin = at_att("vwin", [P, NAC - 1, 2, P])
        vmeta = at_att("vmeta", [META, 2, P])
        aqT = at_att("aqT", [P, NAC, KT, ATT_CHUNK])
        prob = at_att("prob", [P, 2, 2, META + WIN])
        pT = at_att("pT", [P, 2, 2, P])
        pTm = at_att("pTm", [META, 2, 2, P])
        avT = sb("avT", [P, 2, NT], place["yah"])
        prod = sb("prod", [P, 2, SEQ], place["aqT"])

        mgh = sb("mgh", [P, KT, SEQ], place["qr"], F32R)
        mgl = sb("mgl", [P, KT, SEQ], place["vr"], F32R)
        orow = sb("orow", [P, 3, D], place["yah"])
        at_ffn = Region(G0, GEND)
        hidh = at_ffn("hidh", [P, FT, SEQ], F32R)
        hidl = at_ffn("hidl", [P, FT, SEQ], F32R)
        sgate = at_ffn("sgate", [P, 2, SEQ])
        hid = at_ffn("hid", [P, 2, SEQ])
        frow = at_ffn("frow", [P, 2, D])
        res = sb("res", [P, TT, D], HT)

        ps = ctx.enter_context(nc.psum_tensor("ps", [P, 8, 512], F32))
        parked = nc.dram_tensor("parked", (SIDE, P, NT), F32).ap()

        x_landed = [sem(f"x_landed{i}") for i in range(2)]
        rows_landed = sem("rows_landed")
        const_landed = sem("const_landed")
        w_landed = [sem(f"w_landed{i}") for i in range(RING)]
        w_hi = sem("w_hi")
        w_lo = sem("w_lo")
        w_used = sem("w_used")
        freed = [sem(f"freed{i}") for i in range(2)]
        filled = [sem(f"filled{i}") for i in range(8)]
        taken = [sem(f"taken{i}") for i in range(8)]
        dve_step = sem("dve_step")
        act_step = sem("act_step")
        powers_ready = sem("powers_ready")
        var_ready = sem("var_ready")
        rstd_ready = sem("rstd_ready")
        h_ready = sem("h_ready")
        hT_hi = sem("hT_hi")
        conv_done = sem("conv_done")
        silu_done = sem("silu_done")
        prep = sem("prep")
        prep_act = sem("prep_act")
        tri_ready = sem("tri_ready")
        dec_ready = sem("dec_ready")
        kss_ready = [sem(f"kss_ready{g}") for g in range(2)]
        knorm_ready = [sem(f"knorm_ready{g}") for g in range(2)]
        qss_ready = [sem(f"qss_ready{g}") for g in range(2)]
        rq_ready = [sem(f"rq_ready{g}") for g in range(2)]
        u_ready = [sem(f"u_ready{g}") for g in range(2)]
        level_ready = [sem(f"level_ready{g}") for g in range(2)]
        xt_ready = [sem(f"xt_ready{g}") for g in range(2)]
        r_ready = [sem(f"r_ready{g}") for g in range(2)]
        vdec_ready = [sem(f"vdec_ready{g}") for g in range(2)]
        osq_ready = [sem(f"osq_ready{g}") for g in range(2)]
        oss_ready = [sem(f"oss_ready{g}") for g in range(2)]
        onorm_ready = [sem(f"onorm_ready{g}") for g in range(2)]
        o_ready = [sem(f"o_ready{g}") for g in range(2)]
        yh_ready = [sem(f"yh_ready{g}") for g in range(2)]
        yl_ready = [sem(f"yl_ready{g}") for g in range(2)]
        side_ready = sem("side_ready")
        side_stored = [sem(f"side_stored{i}") for i in range(3)]
        att_loaded = sem("att_loaded")
        gate_loaded = [sem(f"gate_loaded{i}") for i in range(2)]
        max_ready = sem("max_ready")
        prob_ready = sem("prob_ready")
        ya_hi = sem("ya_hi")
        merged_ready = sem("merged_ready")
        mg_hi = sem("mg_hi")
        mg_lo = sem("mg_lo")
        hid_hi = sem("hid_hi")
        hid_lo = sem("hid_lo")
        out_stored = sem("out_stored")

        steps = plan()
        use = bank_uses()

        def levels_before(n):
            return sum(levels_of(m) for m in range(n))

        def tile_index(b):
            return b if b < B_OUT else b - KT

        def slot_of(b):
            return tile_index(b) % 2, tile_index(b) // 2

        def wait_free(eng, *key):
            bank, before = use[key]
            if before:
                eng.wait_ge(taken[bank], before)

        def wait_filled(eng, *key):
            eng.wait_ge(filled[use[key][0]], filled_before(use, key) + 1)

        def wait_taken(eng, *key):
            bank, before = use[key]
            eng.wait_ge(taken[bank], before + 1)

        def heads(t, g, c, w):
            return t[:c, g, :, :w]

        def bank4(key, c, w):
            return ps[:c, use[key][0], :].rearrange("p (h t) -> p h t", h=4)[:, :, :w]

        def over_heads(i, c):
            return cst[:c, i, :c].unsqueeze(1).to_broadcast([c, 4, c])

        def per_head(t, c, w):
            return t.unsqueeze(2).to_broadcast([c, 4, w])

        def norm_tile(i):
            if i < TT:
                return xin[:, i % 2, :], h[:, i, :], P, lnrow
            if i == TT:
                return xin[:META, i % 2, :], hmeta[:, :], META, lnrow
            if i <= 2 * TT:
                t = i - TT - 1
                return h[:, t, :], h[:, t, :], P, orow[:, 1:3, :]
            t = i - 2 * TT - 1
            return res[:, t, :], res[:, t, :], P, frow

        def window_of(c):
            return META + ATT_CHUNK * max(c - 1, 0), ATT_CHUNK if c == 0 else WIN

        def pair_view(bank):
            return ps[:, bank:bank + 2, :].rearrange("p b (k t) -> p (b k) t", t=P)

        block = ctx.enter_context(nc.Block())

        @block.sync
        def _(sp):
            def load_x(i):
                src = x[P * i:P * (i + 1), :] if i < TT else meta
                sp.dma_start(xin[:src.shape[0], i % 2, :], src).then_inc(x_landed[i % 2], 16)

            load_x(0)
            sp.dma_start(lnrow[:], rows[R_LNIN:R_LNIN + 2, :].partition_broadcast(P)).then_inc(rows_landed, 16)
            load_x(1)
            sp.dma_start(cst[:], consts).then_inc(const_landed, 16)
            sp.dma_start(col[:], cols).then_inc(const_landed, 16)
            sp.dma_start(srt[:], short.partition_broadcast(P)).then_inc(const_landed, 16)
            for b in range(RING):
                sp.dma_start(wst[:, b, :], wstream[b]).then_inc(w_landed[b], 16)
            for i in range(2, TT + 1):
                sp.wait_ge(h_ready, i - 1)
                load_x(i)
            with sp.Fori(0, (NBLOCKS - RING) // RING) as turn:
                for j in range(RING):
                    sp.wait_ge(w_lo, turn * RING + (j + 1))
                    sp.dma_start(wst[:, j, :], wstream[turn * RING + (RING + j)]).then_inc(w_landed[j], 16)
            for b in range(NBLOCKS - NBLOCKS % RING, NBLOCKS):
                sp.wait_ge(w_lo, b - RING + 1)
                sp.dma_start(wst[:, b % RING, :], wstream[b]).then_inc(w_landed[b % RING], 16)

        @block.tensor
        def _(pe):
            ident = cst[:, C_IDENT, :]

            def tile_step(b, k, inh, inl, first):
                slot, before = slot_of(b)
                if k == 0:
                    pe.wait_ge(w_lo, b + 1)
                    if before:
                        pe.wait_ge(freed[slot], before)
                width = inh.shape[2] - first
                parts = [(0, width)] if width <= 512 else [(0, HALF), (HALF, HALF)]
                s = slice(k * P, (k + 1) * P)
                for m, (w, v) in enumerate(((whi, inh), (whi, inl), (wlo, inh))):
                    for j, (at, n) in enumerate(parts):
                        mm = nc.tensor.matmul(ps[:, 2 * slot + j, 0:n], w[:, b % RING, s],
                                              v[:, k, first + at:first + at + n],
                                              start=(k == 0 and m == 0), stop=(k == KT - 1 and m == 2))
                if k == KT - 1:
                    mm.then_inc(w_used, 1)

            def projection_step(b, k):
                narrow = b > B_BA and not B_SIDE <= b < B_SIDE + SIDE_AKV
                tile_step(b, k, hTh, hTl, META if narrow else 0)

            def branch_step(b, k):
                if b == B_BB and k == 0:
                    for g in range(2):
                        pe.wait_ge(yl_ready[g], TT)
                if b == B_BA2 and k == 0:
                    wait_taken(pe, "pv", NUNITS // 2 - 1)
                    wait_taken(pe, "pv", NUNITS // 2 - 2)
                if b < B_BA2:
                    tile_step(b, k, yh, yl, META)
                else:
                    tile_step(b, k, yah, yal, 0)

            def turn_tile(i, key, src, c):
                pe.wait_ge(h_ready, i + 1)
                wait_free(pe, *key)
                bank = use[key][0]
                for k in range(KT):
                    mm = nc.tensor.transpose(ps[:, bank + k // 4, (k % 4) * P:(k % 4) * P + c],
                                             src[:, k * P:(k + 1) * P], ident[:c, :c])
                mm.then_inc(filled[bank], 1)

            def logits_and_decays():
                slot, before = slot_of(B_BA)
                pe.wait_ge(freed[slot], before + 1)
                for n in range(TT + 1):
                    t0 = chunk_of(n)[0]
                    mm = nc.tensor.transpose(ps[:, 4, n * 16:n * 16 + 16], ba_cols[:, t0:t0 + P], ident[:16, :16])
                mm.then_inc(filled[4], 1)
                pe.wait_ge(prep, 4)
                for n in range(TT + 1):
                    c = chunk_of(n)[1]
                    for m, mat in enumerate((C_INCL, C_GT, C_ONES)):
                        at = (3 * n + m) * GH
                        mm = nc.tensor.matmul(ps[:, 5, at:at + GH], cst[:c, mat, :], la[:c, n, :],
                                              start=(n == 0 and m == 0), stop=(n == TT and m == 2),
                                              skip_group_check=True)
                mm.then_inc(filled[5], 1)

            def delta(stage, n, g):
                t0, c = chunk_of(n)
                key = (stage, n, g)
                bank = use[key][0]
                last = levels_of(n) - 1
                if key == ("k", 0, 0):
                    pe.wait_ge(silu_done, 3 * GH)
                wait_free(pe, *key)
                toks = slice(t0, t0 + c)
                kind, level = stage[0], int(stage[1:] or 0)
                if kind == "d":
                    pe.wait_ge(tri_ready, 2 * n + g + 1)
                    nc.tensor.matmul(bank4(key, c, c), cst[:c, C_GT, :c], heads(tri_la, g, c, c),
                                     start=True, stop=True).then_inc(filled[bank], 1)
                    return
                if kind == "i":
                    pe.wait_ge(xt_ready[g], n + 1)
                elif kind == "y":
                    pe.wait_ge(level_ready[g], levels_before(n) + level + 1)
                    wait_taken(pe, "i" if level == 1 else f"x{level - 1}", n, g)
                elif kind == "z":
                    wait_taken(pe, f"y{level}", n, g)
                elif kind == "x":
                    wait_taken(pe, f"z{level}", n, g)
                elif kind == "s" or kind == "r":
                    wait_taken(pe, "t", n - 1, g)
                elif kind == "p":
                    wait_taken(pe, f"z{last}", n, g)
                    if n:
                        pe.wait_ge(r_ready[g], n)
                    else:
                        wait_taken(pe, "v", n, g)
                elif kind == "o":
                    wait_taken(pe, "p", n, g)
                    wait_taken(pe, "w", n, g)
                elif kind == "t":
                    pe.wait_ge(vdec_ready[g], n + 1)
                    wait_taken(pe, "k", n, g)
                elif kind == "f":
                    pe.wait_ge(o_ready[g], n)
                for j in range(4):
                    head = 4 * g + j
                    wide = ps[:c, bank, j * P:(j + 1) * P]
                    square = ps[:c, bank, j * P:j * P + c]
                    full = ps[:, bank, j * P:(j + 1) * P]
                    if kind in "kqv":
                        mm = nc.tensor.transpose(wide, {"k": kr, "q": qr, "v": vr}[kind][:, head, toks], ident)
                    elif kind in "ix":
                        mm = nc.tensor.transpose(square, XT[:c, g, j, :c], ident[:c, :c])
                    elif kind == "f":
                        mm = nc.tensor.transpose(full, oraw[:, g, j, :], ident)
                    else:
                        dst, lhs, rhs = {
                            "g": (square, kr[:, head, toks], kr[:, head, toks]),
                            "w": (square, kr[:, head, toks], qr[:, head, toks]),
                            "y": (square, UL[:c, g, j, :c], X[:c, g, j, :c]),
                            "z": (square, Y[:c, g, j, :c], XT[:c, g, j, :c]),
                            "s": (wide, kr[:, head, toks], state[:, head, :]),
                            "p": (wide, XT[:c, g, j, :c], vtok[:c, g, j, :]),
                            "r": (wide, qr[:, head, toks], state[:, head, :]),
                            "o": (wide, AT[:c, g, j, :c], vnew[:c, g, j, :]),
                            "t": (full, ktok[:c, g, j, :], vdec[:c, g, j, :]),
                        }[kind]
                        mm = nc.tensor.matmul(dst, lhs, rhs, start=True, stop=True)
                mm.then_inc(filled[bank], 1)

            def values():
                pe.wait_ge(att_loaded, (2 + NAC) * 16)
                for j in range(4):
                    wait_free(pe, "values", j)
                    for m in range(4):
                        pr, w = divmod(4 * j + m, NAC)
                        rows_ = META if w == NAC - 1 else WIN
                        t0 = 0 if w == NAC - 1 else META + ATT_CHUNK * w
                        mm = nc.tensor.transpose(ps[:rows_, 4 + j, m * P:(m + 1) * P],
                                                 avT[:, pr, t0:t0 + rows_], ident)
                    mm.then_inc(filled[4 + j], 1)

            def scores(a):
                c, pr, e = unit(a)
                t0, w = window_of(c)
                wait_free(pe, "scores", a)
                part = slice(DH * e, DH * (e + 1))
                for ip in range(2):
                    q = aqT[part, c, 4 * pr + 2 * ip:4 * pr + 2 * ip + 2, :].rearrange("p i t -> p (i t)")
                    at = ip * (META + WIN)
                    bank = 4 + a % 2
                    nc.tensor.matmul(ps[:, bank, at:at + META], q, akT[part, pr, 0:META],
                                     start=(ip == 0), stop=False, skip_group_check=True)
                    mm = nc.tensor.matmul(ps[:, bank, at + META:at + META + w], q, akT[part, pr, t0:t0 + w],
                                          start=False, stop=(ip == 1), skip_group_check=True)
                mm.then_inc(filled[bank], 1)

            def turn_probs(a):
                w = window_of(unit(a)[0])[1]
                wait_free(pe, "turn", a)
                pe.wait_ge(prob_ready, a + 1)
                bank, s = 6 + a % 2, a % 2
                for ip in range(2):
                    nc.tensor.transpose(ps[:w, bank, ip * P:(ip + 1) * P], prob[:, s, ip, META:META + w], ident)
                    mm = nc.tensor.transpose(ps[:META, bank, (2 + ip) * P:(3 + ip) * P], prob[:, s, ip, 0:META], ident)
                mm.then_inc(filled[bank], 1)

            def weighted_values(a):
                c, pr, e = unit(a)
                w = window_of(c)[1]
                key = ("pv", a // 2)
                bank = use[key][0]
                if e == 0:
                    wait_free(pe, *key)
                wait_taken(pe, "turn", a)
                dst = ps[DH * e:DH * (e + 1), bank, 0:2 * P]
                part = slice(DH * e, DH * (e + 1))
                nc.tensor.matmul(dst, vwin[:w, max(c - 1, 0), pr, part],
                                 pT[:w, a % 2].rearrange("p i t -> p (i t)"), start=True, stop=False)
                mm = nc.tensor.matmul(dst, vmeta[:, pr, part], pTm[:, a % 2].rearrange("p i t -> p (i t)"),
                                      start=False, stop=True)
                if e:
                    mm.then_inc(filled[bank], 1)

            def output_blocks(first, name, half, blocks, acth, actl):
                for kb in range(blocks):
                    b = first + blocks * half + kb
                    pe.wait_ge(w_lo, b + 1)
                    for t in range(TT):
                        bank = use[(name, half, t)][0]
                        if kb == 0:
                            wait_free(pe, name, half, t)
                        toks = slice(P * t, P * (t + 1))
                        for kk in range(2):
                            k = 2 * kb + kk
                            for m, (v, w) in enumerate(((acth, whi), (actl, whi), (acth, wlo))):
                                mm = nc.tensor.matmul(ps[:, bank, :], v[:, k, toks],
                                                      w[:, b % RING, 512 * kk:512 * (kk + 1)],
                                                      start=(k == 0 and m == 0),
                                                      stop=(k == 2 * blocks - 1 and m == 2))
                        if t == TT - 1:
                            mm.then_inc(w_used, 1)
                        elif kb == blocks - 1:
                            mm.then_inc(filled[bank], 1)

            pe.wait_ge(const_landed, 3 * 16)
            for i in range(TT + 1):
                _, src, c, _ = norm_tile(i)
                turn_tile(i, ("hT", i), src, c)
            for i in range(TT + 1):
                wait_taken(pe, "hT", i)
            for what, *at in steps:
                if what == "block":
                    for k in range(KT):
                        (projection_step if at[0] < B_BB else branch_step)(at[0], k)
                elif what == "side":
                    (projection_step if at[0] < B_BB else branch_step)(*at)
                elif what == "gates":
                    logits_and_decays()
                elif what == "delta":
                    delta(*at)
                elif what == "reload":
                    values()
                elif what == "att":
                    a = at[0]
                    if a < NUNITS:
                        scores(a)
                    if 1 <= a <= NUNITS:
                        turn_probs(a - 1)
                    if a >= 2:
                        weighted_values(a - 2)
            pe.wait_ge(mg_lo, KT)
            output_blocks(B_OUT, "out", 0, KT // 2, mgh, mgl)
            for s in range(2):
                pe.wait_ge(freed[s], slot_of(B_OUT + KT + s)[1] if slot_of(B_OUT + KT + s)[0] == s
                           else slot_of(B_OUT + KT + 1 - s)[1])
            output_blocks(B_OUT, "out", 1, KT // 2, mgh, mgl)
            for t in range(TT):
                turn_tile(TT + 1 + t, ("h1T", t), h[:, t, :], P)
            for t in range(TT):
                wait_taken(pe, "h1T", t)
            for b in range(B_F1, B_F2):
                for k in range(KT):
                    tile_step(b, k, h1h, h1l, 0)
            pe.wait_ge(hid_lo, FT)
            output_blocks(B_F2, "ffn", 0, FT // 2, hidh, hidl)
            for s in range(2):
                pe.wait_ge(freed[s], sum(tile_index(b) % 2 == s for b in [*range(B_OUT), *range(B_F1, B_F2)]))
            output_blocks(B_F2, "ffn", 1, FT // 2, hidh, hidl)

        @block.scalar
        def _(act):
            own = [0]

            def step(ins):
                own[0] += 1
                ins.then_inc(act_step, 1)
                act.wait_ge(act_step, own[0])

            def split_hi(b):
                if b >= NBLOCKS:
                    return
                act.wait_ge(w_landed[b % RING], 16 * (b // RING + 1))
                if b >= RING:
                    act.wait_ge(w_used, b - RING + 1)
                nc.scalar.activation(whi[:, b % RING, :], wst[:, b % RING, :], ACT.Copy).then_inc(w_hi, 1)

            def hi_of_tile(i, key, dst, at, c):
                wait_filled(act, *key)
                src = pair_view(use[key][0])[:, :, :c]
                nc.scalar.activation(dst[:, :, at:at + c], src, ACT.Copy).then_inc(hT_hi, 1)

            def projection(b):
                slot, before = slot_of(b)
                act.wait_ge(w_used, b + 1)
                wide = ps[:, 2 * slot:2 * slot + 2, 0:HALF]
                narrow = ps[:, 2 * slot, :]
                bias = col[:, COL_BIAS + b:COL_BIAS + b + 1]
                if b < B_BA:
                    if b >= 2:
                        act.wait_ge(conv_done, b - 1)
                    dst = cbuf[:, b % 2, CONV_K - 1:].rearrange("p (j t) -> p j t", j=2)
                    nc.scalar.activation(dst, wide, ACT.Identity, bias=bias).then_inc(freed[slot], 1)
                elif b == B_BA:
                    dst = ba_cols[:, :].rearrange("p (j t) -> p j t", j=2)
                    nc.scalar.activation(dst, wide[:16], ACT.Copy).then_inc(freed[slot], 1)
                else:
                    nc.scalar.activation(sz[:, b - B_Z, :], narrow, ACT.Silu, bias=bias).then_inc(freed[slot], 1)

            def silu_of_conv(b):
                act.wait_ge(conv_done, b + 1)
                dst = (kr, vr, qr)[b // GH][:, b % GH, :]
                nc.scalar.activation(dst, cacc[:, b % 2, :], ACT.Silu).then_inc(silu_done, 1)

            def log_decay_terms():
                act.wait_ge(prep, 2)
                step(nc.scalar.activation(soft[:], soft[:], ACT.Exp, scale=-1.0))
                step(nc.scalar.activation(soft[:], soft[:], ACT.Ln, bias=1.0))
                step(nc.scalar.activation(neg_a[:], srt[:, S_ALOG:S_ALOG + GH], ACT.Exp))
                nc.scalar.activation(beta[:], logits[:, :, 0:GH], ACT.Tanh, scale=0.5).then_inc(prep_act, 1)
                wait_filled(act, "decays")
                src = ps[:, 5, 0:3 * GH * (TT + 1)].rearrange("p (n m h) -> p n m h", m=3, h=GH)
                nc.scalar.activation(eg[:], src, ACT.Exp).then_inc(taken[5], 1)

            def delta(stage, n, g):
                c = chunk_of(n)[1]
                key = (stage, n, g)
                bank = use[key][0]
                kind = stage[0]
                if kind == "k":
                    wait_filled(act, *key)
                    nc.scalar.activation(heads(ktok, g, c, P), bank4(key, c, P), ACT.Copy)
                    if n > 1:
                        act.wait_ge(oss_ready[g], n - 1)
                    nc.scalar.activation(heads(ksq, g, c, P), bank4(key, c, P), ACT.Square).then_inc(taken[bank], 1)
                elif kind == "q":
                    wait_filled(act, *key)
                    if n > 1:
                        wait_filled(act, "f", n - 1, g)
                    nc.scalar.activation(heads(qsq, g, c, P), bank4(key, c, P), ACT.Square).then_inc(taken[bank], 1)
                elif kind == "d":
                    wait_filled(act, *key)
                    if n > 1:
                        act.wait_ge(yl_ready[g], n - 1)
                    nc.scalar.activation(heads(dec, g, c, c), bank4(key, c, c), ACT.Exp).then_inc(taken[bank], 1)
                elif kind in "ixy":
                    wait_filled(act, *key)
                    dst = Y if kind == "y" else X
                    nc.scalar.activation(heads(dst, g, c, c), bank4(key, c, c), ACT.Copy).then_inc(taken[bank], 1)
                elif kind == "f":
                    wait_taken(act, *key)
                    t0 = chunk_of(n)[0]
                    nc.scalar.activation(yh[:, 4 * g:4 * g + 4, t0:t0 + P], youT[:, g], ACT.Copy).then_inc(yh_ready[g], 1)

            def store_side(j):
                if j < SIDE_AQ:
                    slot, before = slot_of(B_SIDE + j)
                    act.wait_ge(freed[slot], before + 1)
                else:
                    act.wait_ge(side_ready, j - SIDE_AQ + 1)
                w = NT if j < SIDE_AKV else SEQ
                act.dma_start(parked[j, :, 0:w], side[:, j % 3, 0:w]).then_inc(side_stored[j % 3], 16)

            def side_tile(b):
                j = b - B_SIDE
                slot, before = slot_of(b)
                act.wait_ge(w_used, b + 1)
                if j >= 3:
                    act.wait_ge(side_stored[j % 3], 16 * (j // 3))
                if j < SIDE_AKV:
                    dst = side[:, j % 3, :].rearrange("p (j t) -> p j t", j=2)
                    ins = nc.scalar.activation(dst, ps[:, 2 * slot:2 * slot + 2, 0:HALF], ACT.Identity,
                                               bias=col[:, COL_BIAS + b:COL_BIAS + b + 1])
                elif j < SIDE_AQ:
                    ins = nc.scalar.activation(side[:, j % 3, 0:SEQ], ps[:, 2 * slot, :], ACT.Identity,
                                               bias=col[:, COL_BIAS + b:COL_BIAS + b + 1])
                else:
                    ins = nc.scalar.activation(side[:, j % 3, 0:SEQ], ps[:, 2 * slot, :], ACT.Tanh, scale=0.5,
                                               bias=halfcol[:, COL_BIAS + b:COL_BIAS + b + 1])
                ins.then_inc(freed[slot], 1)
                if j:
                    store_side(j - 1)

            def load_gate(m):
                act.dma_start(gate[:, m % 2, :], parked[SIDE_AQ + m, :, 0:SEQ]).then_inc(gate_loaded[m % 2], 16)

            def reload():
                store_side(SIDE - 1)
                for i in range(3):
                    act.wait_ge(side_stored[i], 16 * len(range(i, SIDE, 3)))
                for g in range(2):
                    act.wait_ge(yl_ready[g], TT)
                act.dma_start(avT[:], parked[2:SIDE_AKV].rearrange("i p t -> p i t")).then_inc(att_loaded, 16)
                act.dma_start(akT[:], parked[0:2].rearrange("i p t -> p i t")).then_inc(att_loaded, 16)
                for c in range(NAC):
                    src = parked[SIDE_AKV:SIDE_AQ, :, ATT_CHUNK * c:ATT_CHUNK * (c + 1)]
                    act.dma_start(aqT[:, c], src.rearrange("i p t -> p i t")).then_inc(att_loaded, 16)
                load_gate(0)
                load_gate(1)
                for j in range(4):
                    wait_filled(act, "values", j)
                    pr, w0 = divmod(4 * j, NAC)
                    n = 3 if w0 else 4
                    src = ps[:, 4 + j, 0:n * P].rearrange("p (w t) -> p w t", w=n)
                    ins = nc.scalar.activation(vwin[:, w0:w0 + n, pr, :], src, ACT.Copy)
                    if w0:
                        ins = nc.scalar.activation(vmeta[:, pr, :], ps[:META, 4 + j, 3 * P:4 * P], ACT.Copy)
                    ins.then_inc(taken[4 + j], 1)

            def attention(a):
                if a < NUNITS:
                    w = META + window_of(unit(a)[0])[1]
                    s = a % 2
                    act.wait_ge(max_ready, a + 1)
                    if a >= 2:
                        wait_filled(act, "turn", a - 2)
                    nc.scalar.activation(sink_exp[:, s, :], sink_arg[:, s, :], ACT.Exp)
                    for ip in range(2):
                        at = ip * (META + WIN)
                        ins = nc.scalar.activation(prob[:, s, ip, 0:w], ps[:, 4 + s, at:at + w], ACT.Exp,
                                                   scale=DH ** -0.5, bias=neg_amax[:, s, ip:ip + 1],
                                                   accum_out=asum[:, s, ip:ip + 1])
                    ins.then_inc(taken[4 + s], 1)
                if 1 <= a <= NUNITS:
                    b = a - 1
                    w = window_of(unit(b)[0])[1]
                    wait_filled(act, "turn", b)
                    bank = 6 + b % 2
                    src = ps[:, bank, :].rearrange("p (i t) -> p i t", t=P)
                    nc.scalar.activation(pT[:w, b % 2], src[:w, 0:2], ACT.Copy)
                    nc.scalar.activation(pTm[:, b % 2], src[:META, 2:4], ACT.Copy).then_inc(taken[bank], 1)
                if a >= 2 and a % 2:
                    c, pr, _ = unit(a - 2)
                    key = ("pv", (a - 2) // 2)
                    wait_filled(act, *key)
                    src = ps[:, use[key][0], 0:2 * P].rearrange("p (i t) -> p i t", i=4)
                    nc.scalar.activation(yah[:, 4 * pr:4 * pr + 4, ATT_CHUNK * c:ATT_CHUNK * (c + 1)], src,
                                         ACT.Copy).then_inc(ya_hi, 1)

            def next_gate(m):
                if m + 2 < 2 * KT:
                    slot, before = slot_of(B_BB + m)
                    act.wait_ge(freed[slot], before + 1)
                    load_gate(m + 2)

            def merged_hi(m):
                act.wait_ge(merged_ready, m + 1)
                nc.scalar.activation(mgh[:, m, :], merged[:, m, :], ACT.Copy).then_inc(mg_hi, 1)

            for b in range(RING):
                split_hi(b)
            for i in range(TT + 1):
                at, c = (META + P * i, P) if i < TT else (0, META)
                hi_of_tile(i, ("hT", i), hTh, at, c)
            for what, *at in steps:
                if what == "block":
                    b = at[0]
                    if b < B_BB:
                        projection(b)
                        split_hi(b + RING)
                        if 1 <= b <= B_BA:
                            silu_of_conv(b - 1)
                    else:
                        split_hi(b + RING)
                        merged_hi(b - B_BA2)
                        next_gate(b - B_BB)
                elif what == "sideend":
                    b = at[0]
                    if b < B_BB:
                        side_tile(b)
                    split_hi(b + RING)
                    if b >= B_BB:
                        next_gate(b - B_BB)
                elif what == "gates":
                    log_decay_terms()
                elif what == "delta":
                    delta(*at)
                elif what == "reload":
                    reload()
                elif what == "att":
                    attention(at[0])
            act.dma_start(orow[:], rows[R_BOUT:R_BOUT + 3, :].partition_broadcast(P)).then_inc(rows_landed, 16)
            for b in range(B_OUT, B_F1):
                split_hi(b + RING)
            for t in range(TT):
                hi_of_tile(TT + 1 + t, ("h1T", t), h1h, P * t, P)
            for f in range(FT):
                b = B_F1 + 2 * f
                slot, before = slot_of(b)
                act.wait_ge(w_used, b + 1)
                nc.scalar.activation(sgate[:, f % 2, :], ps[:, 2 * slot, :], ACT.Silu).then_inc(freed[slot], 1)
                split_hi(b + RING)
                split_hi(b + 1 + RING)
                up, upbefore = slot_of(b + 1)
                act.wait_ge(freed[up], upbefore + 1)
                nc.scalar.activation(hidh[:, f, :], hid[:, f % 2, :], ACT.Copy).then_inc(hid_hi, 1)
                if f == 0:
                    act.dma_start(frow[:], rows[R_LN2:R_LN2 + 2, :].partition_broadcast(P)).then_inc(rows_landed, 16)
            for b in range(B_F2, NBLOCKS - RING):
                split_hi(b + RING)
            for t in range(TT):
                act.wait_ge(h_ready, 2 * TT + 2 + t)
                act.dma_start(out[P * t:P * (t + 1), :], res[:, t, :]).then_inc(out_stored, 16)
            act.wait_ge(out_stored, 16 * TT)

        @block.vector
        def _(dve):
            own = [0]

            def step(ins):
                own[0] += 1
                ins.then_inc(dve_step, 1)
                dve.wait_ge(dve_step, own[0])

            def tell(ins, semaphore, value):
                ins.then_inc(semaphore, 1)
                dve.wait_ge(semaphore, value)

            def take(ins, *key):
                bank, before = use[key]
                tell(ins, taken[bank], before + 1)

            def free_slot(ins, b):
                slot, before = slot_of(b)
                tell(ins, freed[slot], before + 1)

            def norm(i):
                src, dst, c, gain = norm_tile(i)
                for j in range(2):
                    step(nc.vector.bn_stats(st6[:c, j, :], src[:, 512 * j:512 * (j + 1)]))
                step(nc.vector.bn_aggr(mv[:c, :], st6[:c, :, :]))
                tell(nc.vector.tensor_scalar(var_eps[:c, :], mv[:c, 1:2], LN_EPS, None, ALU.add), var_ready, i + 1)
                dve.wait_ge(rstd_ready, i + 1)
                step(nc.vector.tensor_scalar(dst, src, mv[:c, 0:1], rstd[:c, 0:1], ALU.subtract, ALU.mult))
                step(nc.vector.tensor_tensor(dst, dst, gain[:c, 0, :], ALU.mult))
                tell(nc.vector.tensor_tensor(dst, dst, gain[:c, 1, :], ALU.add), h_ready, i + 1)

            def lo_of_tile(i, key, hi, lo, at, c, n):
                dve.wait_ge(hT_hi, n + 1)
                src = pair_view(use[key][0])[:, :, :c]
                s = slice(at, at + c)
                ins = nc.vector.tensor_tensor(lo[:, :, s], src, hi[:, :, s].bitcast(F32), ALU.subtract)
                bank, before = use[key]
                ins.then_inc(taken[bank], 1)
                dve.wait_ge(taken[bank], before + 1)

            def convolve(b):
                slot, before = slot_of(b)
                dve.wait_ge(freed[slot], before + 1)
                if b >= 2:
                    dve.wait_ge(silu_done, b - 1)
                acc = cacc[:, b % 2, :]
                for i in range(CONV_K):
                    tap = col[:, COL_CONV + CONV_K * b + i:COL_CONV + CONV_K * b + i + 1]
                    src = cbuf[:, b % 2, i:i + NT]
                    if i == 0:
                        step(nc.vector.tensor_scalar(acc, src, tap, None, ALU.mult))
                        continue
                    ins = nc.vector.scalar_tensor_tensor(out=acc, in0=src, scalar=tap, in1=acc,
                                                         op0=ALU.mult, op1=ALU.add)
                    if i < CONV_K - 1:
                        step(ins)
                    else:
                        tell(ins, conv_done, b + 1)

            def decay_logits():
                wait_filled(dve, "logits")
                n = TT + 1
                src = ps[:, 4, 0:16 * n].rearrange("p (n m) -> p n m", m=16)
                row = lambda at, w: srt[:, at:at + w].unsqueeze(1).to_broadcast([P, n, w])
                take(nc.vector.tensor_tensor(logits[:], src, row(S_BIAS, 16), ALU.add), "logits")
                tell(nc.vector.tensor_tensor(la[:], logits[:, :, GH:], row(S_DT, GH), ALU.add), prep, 1)
                tell(nc.vector.scalar_tensor_tensor(out=soft[:], in0=la[:], scalar=-1.0, in1=la[:],
                                                    op0=ALU.mult, op1=ALU.max), prep, 2)
                dve.wait_ge(prep_act, 1)
                step(nc.vector.scalar_tensor_tensor(out=la[:], in0=la[:], scalar=0.0, in1=soft[:],
                                                    op0=ALU.max, op1=ALU.add))
                step(nc.vector.tensor_scalar(neg_a[:], neg_a[:], -1.0, None, ALU.mult))
                tell(nc.vector.tensor_scalar(beta[:], beta[:], 0.5, 0.5, ALU.mult, ALU.add), prep, 3)
                tell(nc.vector.tensor_tensor(la[:], la[:], neg_a[:, :].unsqueeze(1).to_broadcast([P, n, GH]),
                                             ALU.mult), prep, 4)
                wait_taken(dve, "decays")
                step(nc.vector.tensor_scalar(neg_eg[:], eg[:, :, 0, :], -1.0, None, ALU.mult))

            def delta(stage, n, g):
                t0, c = chunk_of(n)
                key = (stage, n, g)
                kind = stage[0]
                hs = slice(4 * g, 4 * g + 4)
                tt = nc.vector.tensor_tensor
                if kind == "k":
                    step_la = per_head(la[:c, n, hs], c, c)
                    tell(tt(heads(tri_la, g, c, c), over_heads(C_INCL, c), step_la, ALU.mult), tri_ready, 2 * n + g + 1)
                    wait_taken(dve, *key)
                    step(nc.vector.tensor_reduce(kss[:c, g, :], heads(ksq, g, c, P), AX_X, ALU.add))
                    tell(nc.vector.tensor_scalar(kss[:c, g, :], kss[:c, g, :], NORM_EPS, None, ALU.add),
                         kss_ready[g], n + 1)
                    step(nc.vector.reciprocal(rk2[:c, g, :], kss[:c, g, :]))
                    step(tt(rho[:c, g, :], rk2[:c, g, :], beta[:c, n, hs], ALU.mult))
                elif kind == "q":
                    wait_taken(dve, *key)
                    step(nc.vector.tensor_reduce(qss[:c, g, :], heads(qsq, g, c, P), AX_X, ALU.add))
                    tell(nc.vector.tensor_scalar(qss[:c, g, :], qss[:c, g, :], NORM_EPS, None, ALU.add),
                         qss_ready[g], n)
                elif kind == "v":
                    wait_filled(dve, *key)
                    dve.wait_ge(knorm_ready[g], n + 1)
                    take(tt(heads(vtok, g, c, P), bank4(key, c, P), per_head(knorm[:c, g, :], c, P), ALU.mult), *key)
                elif kind == "g":
                    wait_filled(dve, *key)
                    dve.wait_ge(dec_ready, 2 * n + g + 1)
                    take(tt(heads(U, g, c, c), bank4(key, c, c), heads(dec, g, c, c), ALU.mult), *key)
                    tell(tt(heads(U, g, c, c), heads(U, g, c, c), per_head(rho[:c, g, :], c, c), ALU.mult),
                         u_ready[g], n + 1)
                elif kind == "w":
                    wait_filled(dve, *key)
                    take(tt(heads(AT, g, c, c), bank4(key, c, c), heads(dec, g, c, c), ALU.mult), *key)
                elif kind == "i":
                    dve.wait_ge(level_ready[g], levels_before(n) + 1)
                    tell(tt(heads(XT, g, c, c), over_heads(C_IDENT, c), heads(UL, g, c, c), ALU.subtract),
                         xt_ready[g], n + 1)
                elif kind == "z":
                    wait_filled(dve, *key)
                    take(tt(heads(XT, g, c, c), heads(XT, g, c, c), bank4(key, c, c), ALU.subtract), *key)
                elif kind == "s":
                    wait_filled(dve, *key)
                    take(tt(heads(Y, g, c, P), bank4(key, c, P), per_head(neg_eg[:c, n, hs], c, P), ALU.mult), *key)
                    tell(tt(heads(vtok, g, c, P), heads(vtok, g, c, P), heads(Y, g, c, P), ALU.add), r_ready[g], n)
                elif kind == "p":
                    wait_filled(dve, *key)
                    take(tt(heads(vnew, g, c, P), bank4(key, c, P), per_head(rho[:c, g, :], c, P), ALU.mult), *key)
                elif kind == "r":
                    wait_filled(dve, *key)
                    take(tt(heads(oraw, g, c, P), bank4(key, c, P), per_head(eg[:c, n, 0, hs], c, P), ALU.mult), *key)
                elif kind == "o":
                    wait_filled(dve, *key)
                    take(tt(heads(oraw, g, c, P), heads(oraw, g, c, P), bank4(key, c, P), ALU.add), *key)
                    dve.wait_ge(rq_ready[g], n)
                    step(nc.vector.tensor_scalar(rq[:, g, :], rq[:, g, :], DK ** -0.5, None, ALU.mult))
                    step(tt(rq2[:, g, :], rq[:, g, :], rq[:, g, :], ALU.mult))
                    dve.wait_ge(osq_ready[g], n)
                    step(nc.vector.tensor_reduce(oss[:, g, :], osq[:, g], AX_X, ALU.add))
                    step(nc.vector.scalar_tensor_tensor(out=oss[:, g, :], in0=oss[:, g, :], scalar=1.0 / DK,
                                                        in1=rq2[:, g, :], op0=ALU.mult, op1=ALU.mult))
                    tell(nc.vector.tensor_scalar(oss[:, g, :], oss[:, g, :], NORM_EPS, None, ALU.add), oss_ready[g], n)
                    if n == TT:
                        scale_output(n, g)
                elif kind == "t":
                    s = state[:, hs, :]
                    if n:
                        step(tt(s, s, per_head(eg[:, n, 2, hs], P, P), ALU.mult))
                    wait_filled(dve, *key)
                    if n:
                        take(tt(s, s, bank4(key, P, P), ALU.add), *key)
                        scale_output(n, g)
                    else:
                        take(nc.vector.tensor_copy(s, bank4(key, P, P)), *key)
                elif kind == "f":
                    wait_filled(dve, *key)
                    gated = sz[:, hs, t0 - META:t0 - META + P]
                    take(nc.vector.scalar_tensor_tensor(out=youT[:, g], in0=bank4(key, P, P),
                                                        scalar=col[:, COL_NORM:COL_NORM + 1], in1=gated,
                                                        op0=ALU.mult, op1=ALU.mult), *key)

            def scale_output(n, g):
                dve.wait_ge(onorm_ready[g], n)
                step(nc.vector.tensor_tensor(onorm[:, g, :], onorm[:, g, :], rq[:, g, :], ALU.mult))
                tell(nc.vector.tensor_tensor(oraw[:, g], oraw[:, g], per_head(onorm[:, g, :], P, P), ALU.mult),
                     o_ready[g], n)

            def gate_of_side(b):
                j = b - B_SIDE
                if j < SIDE_AQ:
                    return
                slot, before = slot_of(b)
                dve.wait_ge(freed[slot], before + 1)
                s = side[:, j % 3, 0:SEQ]
                tell(nc.vector.tensor_scalar(s, s, 0.5, 0.5, ALU.mult, ALU.add), side_ready, j - SIDE_AQ + 1)

            def branch(b):
                m = b - B_BB
                slot, _ = slot_of(b)
                dve.wait_ge(w_used, b + 1)
                dve.wait_ge(gate_loaded[m % 2], 16 * (m // 2 + 1))
                src = ps[:, 2 * slot, :]
                if m < KT:
                    free_slot(nc.vector.tensor_tensor(merged[:, m, :], src, gate[:, m % 2, :], ALU.mult), b)
                    return
                free_slot(nc.vector.tensor_tensor(prod[:, m % 2, :], src, gate[:, m % 2, :], ALU.mult), b)
                dst = merged[:, m - KT, :]
                tell(nc.vector.tensor_tensor(dst, dst, prod[:, m % 2, :], ALU.add), merged_ready, m - KT + 1)

            def attention(a):
                if a < NUNITS:
                    w = META + window_of(unit(a)[0])[1]
                    s, group = a % 2, a % 4
                    wait_filled(dve, "scores", a)
                    src = ps[:, 4 + s, 0:2 * (META + WIN)].rearrange("p (i t) -> p i t", i=2)[:, :, 0:w]
                    step(nc.vector.tensor_reduce(amax[:, s, :], src, AX_X, ALU.max))
                    sink = col[:, COL_SINK + 2 * group:COL_SINK + 2 * group + 2]
                    step(nc.vector.scalar_tensor_tensor(out=amax[:, s, :], in0=amax[:, s, :], scalar=DH ** -0.5,
                                                        in1=sink, op0=ALU.mult, op1=ALU.max))
                    step(nc.vector.tensor_scalar(neg_amax[:, s, :], amax[:, s, :], -1.0, None, ALU.mult))
                    tell(nc.vector.tensor_tensor(sink_arg[:, s, :], sink, amax[:, s, :], ALU.subtract),
                         max_ready, a + 1)
                if 1 <= a <= NUNITS:
                    b = a - 1
                    w = META + window_of(unit(b)[0])[1]
                    s = b % 2
                    wait_taken(dve, "scores", b)
                    step(nc.vector.tensor_tensor(atot[:, s, :], asum[:, s, :], sink_exp[:, s, :], ALU.add))
                    step(nc.vector.reciprocal(arec[:, s, :], atot[:, s, :]))
                    pr_ = prob[:, s, :, 0:w]
                    tell(nc.vector.tensor_tensor(pr_, pr_, arec[:, s, :].unsqueeze(2).to_broadcast([P, 2, w]),
                                                 ALU.mult), prob_ready, b + 1)
                if a >= 2 and a % 2:
                    c, pr, _ = unit(a - 2)
                    key = ("pv", (a - 2) // 2)
                    dve.wait_ge(ya_hi, (a - 2) // 2 + 1)
                    src = ps[:, use[key][0], 0:2 * P].rearrange("p (i t) -> p i t", i=4)
                    at = (slice(None), slice(4 * pr, 4 * pr + 4), slice(ATT_CHUNK * c, ATT_CHUNK * (c + 1)))
                    take(nc.vector.tensor_tensor(yal[at], src, yah[at].bitcast(F32), ALU.subtract), *key)

            def residual(name, half, t, first, dst):
                if t < TT - 1:
                    wait_filled(dve, name, half, t)
                else:
                    dve.wait_ge(w_used, first)
                cs = slice(512 * half, 512 * (half + 1))
                take(nc.vector.scalar_tensor_tensor(out=dst[:, t, cs], in0=h[:, t, cs], scalar=ALPHA,
                                                    in1=ps[:, use[(name, half, t)][0], :],
                                                    op0=ALU.mult, op1=ALU.add), name, half, t)

            step(nc.vector.memset(cbuf[:, :, 0:CONV_K - 1], 0.0))
            step(nc.vector.memset(half[:], 0.5))
            tell(nc.vector.memset(minus_half[:], -0.5), powers_ready, 1)
            dve.wait_ge(rows_landed, 16)
            for i in range(TT + 2):
                if i <= TT:
                    dve.wait_ge(x_landed[i % 2], 16 * (i // 2 + 1))
                    norm(i)
                if i:
                    j = i - 1
                    at, c = (META + P * j, P) if j < TT else (0, META)
                    lo_of_tile(j, ("hT", j), hTh, hTl, at, c, j)
                if i == 0:
                    dve.wait_ge(const_landed, 3 * 16)
                    step(nc.vector.tensor_scalar(halfcol[:], col[:], 0.5, None, ALU.mult))
            for what, *at in steps:
                if what == "block" and at[0] < B_BA:
                    convolve(at[0])
                elif what == "block" and at[0] >= B_BB or what == "sideend" and at[0] >= B_BB:
                    branch(at[0])
                elif what == "sideend":
                    gate_of_side(at[0])
                elif what == "gates":
                    decay_logits()
                elif what == "delta":
                    delta(*at)
                elif what == "att":
                    attention(at[0])
            dve.wait_ge(rows_landed, 2 * 16)
            for j in range(2):
                for t in range(TT):
                    residual("out", j, t, B_OUT + KT // 2 * (j + 1), h)
                    cs = slice(512 * j, 512 * (j + 1))
                    step(nc.vector.tensor_tensor(h[:, t, cs], h[:, t, cs], orow[:, 0, cs], ALU.add))
            for t in range(TT + 1):
                if t < TT:
                    norm(TT + 1 + t)
                if t:
                    lo_of_tile(t - 1, ("h1T", t - 1), h1h, h1l, P * (t - 1), P, TT + t)
            for f in range(FT):
                b = B_F1 + 2 * f + 1
                gslot, gbefore = slot_of(b - 1)
                dve.wait_ge(w_used, b + 1)
                dve.wait_ge(freed[gslot], gbefore + 1)
                if f >= 2:
                    dve.wait_ge(hid_lo, f - 1)
                free_slot(nc.vector.tensor_tensor(hid[:, f % 2, :], ps[:, 2 * slot_of(b)[0], :],
                                                  sgate[:, f % 2, :], ALU.mult), b)
            dve.wait_ge(rows_landed, 3 * 16)
            for j in range(2):
                for t in range(TT):
                    residual("ffn", j, t, B_F2 + FT // 2 * (j + 1), res)
            for t in range(TT):
                norm(2 * TT + 1 + t)

        @block.gpsimd
        def _(pool):
            def split_lo(b):
                if b >= NBLOCKS:
                    return
                s = b % RING
                pool.wait_ge(w_hi, b + 1)
                if b >= RING:
                    pool.wait_ge(w_used, b - RING + 1)
                nc.gpsimd.tensor_tensor(wlo[:, s, :], wst[:, s, :], whi[:, s, :].bitcast(F32),
                                        ALU.subtract).then_inc(w_lo, 1)

            def power(dst, src, exponent, semaphore, wait, value):
                pool.wait_ge(wait, value)
                nc.gpsimd.tensor_tensor(dst, src, exponent, ALU.pow).then_inc(semaphore, 1)

            def norm_power(i):
                c = META if i == TT else P
                power(rstd[:c, :], var_eps[:c, :], minus_half[:c, 0:1], rstd_ready, var_ready, i + 1)

            def delta(stage, n, g):
                c = chunk_of(n)[1]
                kind, level = stage[0], int(stage[1:] or 0)
                hs = slice(4 * g, 4 * g + 4)
                tt = nc.gpsimd.tensor_tensor
                small = (slice(0, c), g)
                if kind == "k":
                    power(knorm[small], kss[small], half[:c, 0:4], knorm_ready[g], kss_ready[g], n + 1)
                elif kind == "q":
                    power(rq[small], qss[small], minus_half[:c, 0:4], rq_ready[g], qss_ready[g], n)
                elif kind == "d":
                    wait_taken(pool, stage, n, g)
                    tt(heads(dec, g, c, c), heads(dec, g, c, c), over_heads(C_INCL, c), ALU.mult).then_inc(dec_ready, 1)
                elif kind == "i":
                    pool.wait_ge(u_ready[g], n + 1)
                    if n:
                        wait_filled(pool, "t", n - 1, g)
                    tt(heads(UL, g, c, c), heads(U, g, c, c), over_heads(C_LEVEL, c), ALU.mult).then_inc(level_ready[g], 1)
                elif kind == "y":
                    if level == 1:
                        pool.wait_ge(xt_ready[g], n + 1)
                    else:
                        wait_filled(pool, f"y{level - 1}", n, g)
                    tt(heads(UL, g, c, c), heads(U, g, c, c), over_heads(C_LEVEL + level, c),
                       ALU.mult).then_inc(level_ready[g], 1)
                elif kind == "p" and n < TT:
                    wait_taken(pool, stage, n, g)
                    tt(heads(vdec, g, c, P), heads(vnew, g, c, P), per_head(eg[:c, n, 1, hs], c, P),
                       ALU.mult).then_inc(vdec_ready[g], 1)
                elif kind == "o":
                    wait_taken(pool, stage, n, g)
                    tt(osq[:, g], oraw[:, g], oraw[:, g], ALU.mult).then_inc(osq_ready[g], 1)
                    power(onorm[small], oss[small], minus_half[:c, 0:4], onorm_ready[g], oss_ready[g], n)
                elif kind == "f":
                    t0 = chunk_of(n)[0]
                    pool.wait_ge(yh_ready[g], n)
                    at = (slice(None), hs, slice(t0, t0 + P))
                    tt(yl[at], youT[:, g], yh[at].bitcast(F32), ALU.subtract).then_inc(yl_ready[g], 1)

            for b in range(RING):
                split_lo(b)
            pool.wait_ge(powers_ready, 1)
            for i in range(TT + 1):
                norm_power(i)
            for what, *at in steps:
                if what in ("block", "sideend"):
                    b = at[0]
                    split_lo(b + RING)
                    if b >= B_BA2:
                        m = b - B_BA2
                        pool.wait_ge(mg_hi, m + 1)
                        nc.gpsimd.tensor_tensor(mgl[:, m, :], merged[:, m, :], mgh[:, m, :].bitcast(F32),
                                                ALU.subtract).then_inc(mg_lo, 1)
                elif what == "delta":
                    delta(*at)
            for b in range(B_OUT, B_F1):
                split_lo(b + RING)
            for t in range(TT):
                norm_power(TT + 1 + t)
            for f in range(FT):
                b = B_F1 + 2 * f
                split_lo(b + RING)
                split_lo(b + 1 + RING)
                pool.wait_ge(hid_hi, f + 1)
                nc.gpsimd.tensor_tensor(hidl[:, f, :], hid[:, f % 2, :], hidh[:, f, :].bitcast(F32),
                                        ALU.subtract).then_inc(hid_lo, 1)
            for b in range(B_F2, NBLOCKS - RING):
                split_lo(b + RING)
            for t in range(TT):
                norm_power(2 * TT + 1 + t)


def constant_matrices():
    j, i = np.mgrid[0:P, 0:P]
    mats = [j == i, j <= i, j > i, j >= 0]
    for level in range(LEVELS):
        size = 1 << level
        mats.append((i // (2 * size) == j // (2 * size)) & (i // size % 2 == 1) & (j // size % 2 == 0))
    return np.ascontiguousarray(np.stack(mats, 1).astype(np.float32))


def lay_out(a):
    w_in, b_in = a["w_in"][0], a["b_in"][0]
    at = np.cumsum([0, A_HEADS * DH, A_KV * DH, A_KV * DH, GH * DK, GH * DK, GH * DK, GH * DK, GH, GH, D, D])
    aq, ak, av, gq, gk, gv, gz, gb, ga, mga, mgb = at[:-1]
    heads = [8 * pr + 4 * e + i for pr in range(2) for i in range(4) for e in range(2)]
    aq_rows = np.concatenate([np.arange(DH * h, DH * (h + 1)) for h in heads])
    tiles = [np.arange(start + P * i, start + P * (i + 1)) for start in (gk, gv, gq) for i in range(GH)]
    tiles += [np.arange(gb, gb + P)]
    tiles += [np.arange(gz + P * i, gz + P * (i + 1)) for i in range(GH)]
    tiles += [np.arange(start + P * i, start + P * (i + 1)) for start in (ak, av) for i in range(2)]
    tiles += [aq + aq_rows[P * i:P * (i + 1)] for i in range(KT)]
    tiles += [np.arange(start + P * i, start + P * (i + 1)) for start in (mgb, mga) for i in range(KT)]

    def columns(w, which):
        return w[:, which].reshape(KT, P, P).transpose(1, 0, 2).reshape(P, D)

    def rows_of(w, half):
        part = w[:, 512 * half:512 * (half + 1)].reshape(-1, 2, P, 512)
        return list(part.transpose(0, 2, 1, 3).reshape(-1, P, D))

    blocks = [columns(w_in, which) for which in tiles]
    wb, wa = a["w_branch_b"][0], a["w_branch_a"][0][aq_rows]
    for w in (wb, wa):
        blocks += [columns(w, np.arange(P * m, P * (m + 1))) for m in range(KT)]
    for half in range(2):
        blocks += rows_of(a["w_out"][0], half)
    for f in range(FT):
        for start in (0, FFN):
            blocks.append(columns(a["w_ffn_in"][0], np.arange(start + P * f, start + P * (f + 1))))
    for half in range(2):
        blocks += rows_of(a["w_ffn_out"][0], half)
    wstream = np.stack(blocks)
    conv = a["conv_w"][0]
    conv_tiles = [conv[:, start + P * i:start + P * (i + 1)].T
                  for start in (GH * DK, 2 * GH * DK, 0) for i in range(GH)]
    sinks = a["attn_sinks"][0]
    sink_cols = [np.repeat(sinks[4 * (2 * pr + e) + 2 * ip:4 * (2 * pr + e) + 2 * ip + 2], P // 2)
                 for pr in range(2) for e in range(2) for ip in range(2)]
    cols = np.concatenate([np.stack([b_in[which] for which in tiles], 1), *conv_tiles,
                           a["gdn_norm_g"][0][:, None], np.stack(sink_cols, 1)], 1)
    rows = np.stack([a["ln_in_g"], a["ln_in_b"], a["b_out"][0], a["ln1_g"][0], a["ln1_b"][0],
                     a["ln2_g"][0], a["ln2_b"][0]])
    short = np.concatenate([b_in[gb:gb + GH], b_in[ga:ga + GH], a["a_log"][0], a["dt_bias"][0]])
    return {"x": a["x"][0], "meta": a["meta"], "wstream": wstream, "consts": constant_matrices(),
            "cols": cols, "rows": rows, "short": short}


def kernel(**inputs):
    import concourse.bacc as bacc
    from concourse.bass_utils import run_bass_kernel_spmd

    arrays = {k: np.ascontiguousarray(v) for k, v in lay_out({k: np.asarray(v) for k, v in inputs.items()}).items()}
    nc = bacc.Bacc("TRN2", target_bir_lowering=False, num_devices=1, dynamic_dma_scratch_size=1024)
    args = [nc.dram_tensor(f"in_{k}", v.shape, F32, kind="ExternalInput").ap() for k, v in arrays.items()]
    result = nc.dram_tensor("out_0", (SEQ, D), F32, kind="ExternalOutput").ap()
    build(nc, *args, result)
    r = run_bass_kernel_spmd(nc, [{f"in_{k}": v for k, v in arrays.items()}], core_ids=[0])
    return r.results[0]["out_0"].reshape(1, SEQ, D)
```

```python
from contextlib import ExitStack

import numpy as np

import concourse.bass as bass
from concourse import mybir

F32 = mybir.dt.float32
F32R = mybir.dt.float32r
ALU = mybir.AluOpType
ACT = mybir.ActivationFunctionType
AX_X = mybir.AxisListType.X

P = 128
D = 1024
KT = D // P
SEQ = 512
META = 16
NT = META + SEQ
HALF = NT // 2
TT = SEQ // P
ATT_CHUNK = 64
NAC = SEQ // ATT_CHUNK
WIN = 2 * ATT_CHUNK
A_HEADS, A_KV, DH = 16, 4, 64
GH, DK = 8, 128
CONV_K = 4
FFN = -(-8 * D // (3 * 256)) * 256
FT = FFN // P
ALPHA = 2.0 ** 0.25
RING = 3

B_GDN = 0
B_BA = 3 * GH
B_Z = B_BA + 1
B_SIDE = B_Z + GH
SIDE_AKV = 4
SIDE_AQ = SIDE_AKV + KT
SIDE = SIDE_AQ + 2 * KT
B_BB = B_SIDE + SIDE
B_BA2 = B_BB + KT
B_OUT = B_BA2 + KT
B_F1 = B_OUT + KT
B_F2 = B_F1 + 2 * FT
NBLOCKS = B_F2 + FT

C_IDENT, C_INCL, C_GT, C_ONES, C_LEVEL = 0, 1, 2, 3, 4
LEVELS = 7
NCONST = C_LEVEL + LEVELS

COL_BIAS = 0
NBIAS = B_BB
COL_CONV = NBIAS
COL_NORM = COL_CONV + 3 * GH * CONV_K
COL_SINK = COL_NORM + 1
NCOLS = COL_SINK + 8
R_LNIN, R_BOUT, R_LN1, R_LN2, NROWS = 0, 2, 3, 5, 7
S_BIAS, S_ALOG, S_DT, NSHORT = 0, 16, 24, 32
LN_EPS, NORM_EPS = 1e-5, 1e-6


def chunk_of(n):
    return (0, META) if n == 0 else (META + P * (n - 1), P)


def levels_of(n):
    return META.bit_length() - 1 if n == 0 else LEVELS



def bank_uses():
    use, count = {}, [0] * 8

    def add(bank, *key):
        use[key] = (bank, count[bank])
        count[bank] += 1

    for i in range(TT + 1):
        add(2 * (i % 2), "hT", i)
    add(4, "logits")
    add(5, "decays")
    for stage, n, g in delta_order():
        add(4 + g + 2 * WHICH_BANK[stage[0]], stage, n, g)
    for j in range(4):
        add(4 + j, "values", j)
    for a in range(NUNITS):
        add(4 + a % 2, "scores", a)
        add(6 + a % 2, "turn", a)
        if a % 2:
            add(1 + 2 * (a // 2 % 2), "pv", a // 2)
    for t in range(TT):
        add(4 + t, "out", 0, t)
    for t in range(TT):
        add(t, "out", 1, t)
    for t in range(TT):
        add(4 + 2 * (t % 2), "h1T", t)
    for half in range(2):
        for t in range(TT):
            add(t + 4 * (1 - half), "ffn", half, t)
    return use


def filled_before(use, key):
    bank, count = use[key]
    return count - sum(1 for k, (b, c) in use.items()
                       if b == bank and c < count and k[0] in ("out", "ffn") and k[2] == TT - 1)


WHICH_BANK = {"k": 0, "q": 1, "v": 0, "d": 1, "g": 0, "w": 1, "i": 0, "y": 1, "z": 0, "x": 1,
              "s": 0, "p": 1, "r": 0, "o": 1, "t": 0, "f": 1}


OUTPUTS_AFTER = "y2"


def delta_order():
    order = []
    for n in range(TT + 1):
        stages = ["k"] + ["q"] * (n > 0) + ["v", "d", "g"] + ["w"] * (n > 0) + ["i"]
        last = levels_of(n) - 1
        for level in range(1, last + 1):
            stages += [f"y{level}", f"z{level}"] + [f"x{level}"] * (level < last)
        stages += ["s"] * (n > 0) + ["p"] + ["r", "o"] * (n > 0) + ["t"] * (n < TT)
        for stage in stages:
            order += [(stage, n, g) for g in range(2)]
            if stage == OUTPUTS_AFTER and n > 1:
                order += [("f", n - 1, g) for g in range(2)]
    return order + [("f", TT, g) for g in range(2)]


TAIL_BLOCKS = 3
HEAD_BLOCKS = 4
ATT_LAG = 2


def plan():
    todo = [("block", b) for b in range(B_SIDE)]
    todo.insert(B_Z + 2, ("logits",))
    todo.insert(B_Z + 6, ("decays",))
    side = [(b, k) for b in range(B_SIDE, B_BB) for k in range(KT)]

    def step(side, count):
        for _ in range(min(count, len(side))):
            b, k = side.pop(0)
            todo.append(("side", b, k))
            if k == KT - 1:
                todo.append(("sideend", b))

    order = delta_order()
    spread = len(side) - TAIL_BLOCKS * KT
    for m, (stage, n, g) in enumerate(order):
        if (stage, n, g) == ("f", TT, 0):
            step(side, len(side) - KT)
        todo.append(("delta", stage, n, g))
        step(side, spread * (m + 1) // len(order) - spread * m // len(order))
    step(side, len(side))
    todo.append(("reload",))
    branch = [(b, k) for b in range(B_BB, B_BA2) for k in range(KT)]
    step(branch, HEAD_BLOCKS * KT)
    todo.append(("values",))
    for a in range(NUNITS + ATT_LAG + 1):
        todo.append(("att", a))
        step(branch, 1)
    step(branch, len(branch))
    return todo + [("block", b) for b in range(B_BA2, B_OUT)]


NUNITS = NAC * 4


def unit(a):
    return a // 4, a // 2 % 2, a % 2


def build(nc, x, meta, wstream, consts, cols, rows, short, out):
    with ExitStack() as ctx:
        place = {}

        def sb(name, shape, offset, dt=F32):
            place[name] = offset
            return nc.alloc_sbuf_tensor_at(name, shape, dt, offset=offset)

        class Region:

            def __init__(self, at, end):
                self.at, self.end = at, end

            def __call__(self, name, shape, dt=F32):
                t = sb(name, shape, self.at, dt)
                self.at += -(-4 * int(np.prod(shape[1:])) // 32) * 32
                assert self.at <= self.end, (name, self.at, self.end)
                return t

        def sem(name):
            return ctx.enter_context(nc.semaphore(name))

        KB = 1024
        BASE = 2 * KB
        keep = Region(BASE, BASE + 10 * KB)
        cst = keep("cst", [P, NCONST, P])
        col = keep("col", [P, NCOLS])
        halfcol = keep("halfcol", [P, NCOLS])
        srt = keep("srt", [P, NSHORT])
        half = keep("half", [P, GH])
        minus_half = keep("minus_half", [P, GH])
        st6 = keep("st6", [P, TT, 2, 6])
        mv = keep("mv", [P, TT, 2])
        var_eps = keep("var_eps", [P, TT])
        rstd = keep("rstd", [P, TT])
        shift = keep("shift", [P, TT])
        logits = keep("logits", [P, TT + 1, 2 * GH])
        la = keep("la", [P, TT + 1, GH])
        beta = keep("beta", [P, TT + 1, GH])
        soft = keep("soft", [P, TT + 1, GH])
        rho = keep("rho", [P, 2, 4])
        rk2 = keep("rk2", [P, 2, 4])
        kss = keep("kss", [P, 2, 4])
        knorm = keep("knorm", [P, 2, 4])
        qss = keep("qss", [P, 2, 4])
        rq = keep("rq", [P, 2, 4])
        rq2 = keep("rq2", [P, 2, 4])
        oss = keep("oss", [P, 2, 4])
        onorm = keep("onorm", [P, 2, 4])
        neg_a = keep("neg_a", [P, GH])
        eg = keep("eg", [P, TT + 1, 3, GH])
        neg_eg = keep("neg_eg", [P, TT + 1, GH])
        amax = keep("amax", [P, 2, 2])
        neg_amax = keep("neg_amax", [P, 2, 2])
        sink_arg = keep("sink_arg", [P, 2, 2])
        sink_exp = keep("sink_exp", [P, 2, 2])
        asum = keep("asum", [P, 2, 2])
        atot = keep("atot", [P, 2, 2])
        arec = keep("arec", [P, 2, 2])

        RINGS = BASE + 10 * KB
        ring = Region(RINGS, RINGS + 36 * KB)
        wst = ring("wst", [P, RING, D])
        whi = ring("whi", [P, RING, D], F32R)
        wlo = ring("wlo", [P, RING, D], F32R)
        H = RINGS + 36 * KB
        h = sb("h", [P, TT, D], H)
        HT = H + 16 * KB
        ht = Region(HT, HT + 33 * KB)
        hTh = ht("hTh", [P, KT, NT], F32R)
        hTl = ht("hTl", [P, KT, NT], F32R)
        h1h = sb("h1h", [P, KT, SEQ], HT, F32R)
        h1l = sb("h1l", [P, KT, SEQ], HT + 4 * KT * SEQ, F32R)
        G0, GEND = HT + 33 * KB, 224 * KB - 512

        at_norm = Region(G0, GEND)
        xin = at_norm("xin", [P, TT + 1, D])
        lnrow = at_norm("lnrow", [P, 2, D])
        hmeta = at_norm("hmeta", [META, D])

        at_delta = Region(G0, GEND)
        qr = at_delta("qr", [P, GH, NT])
        vr = at_delta("vr", [P, GH, NT])
        kr = at_delta("kr", [P, GH, NT])
        yh = sb("yh", [P, GH, NT], place["qr"], F32R)
        yl = sb("yl", [P, GH, NT], place["vr"], F32R)
        sz = at_delta("sz", [P, GH, SEQ])
        side = at_delta("side", [P, 3, NT])
        work = at_delta.at
        at_conv = Region(work, GEND)
        cbuf = at_conv("cbuf", [P, 2, NT + CONV_K - 1])
        cacc = at_conv("cacc", [P, 2, NT])
        ba_cols = at_conv("ba_cols", [16, NT])
        at_work = Region(work, GEND)
        tri_la = at_work("tri_la", [P, 2, 4, P])
        dec = at_work("dec", [P, 2, 4, P])
        U = at_work("U", [P, 2, 4, P])
        UL = [at_work(f"UL{i}", [P, 2, 4, P]) for i in range(2)]
        AT = at_work("AT", [P, 2, 4, P])
        XT = at_work("XT", [P, 2, 4, P])
        X = at_work("X", [P, 2, 4, P])
        Y = at_work("Y", [P, 2, 4, P])
        ktok = at_work("ktok", [P, 2, 4, P])
        vtok = at_work("vtok", [P, 2, 4, P])
        oraw = at_work("oraw", [P, 2, 4, P])
        state = at_work("state", [P, GH, P])
        vnew, vdec, osq = U, UL[0], Y
        ksq, qsq = Y, X
        youT = dec

        at_att = Region(place["kr"], GEND)
        merged = at_att("merged", [P, KT, SEQ])
        gate = at_att("gate", [P, 2, SEQ])
        yah = at_att("yah", [P, KT, SEQ], F32R)
        yal = at_att("yal", [P, KT, SEQ], F32R)
        kwin = at_att("kwin", [P, 2, NAC, META + WIN])
        vwin = at_att("vwin", [P, NAC - 1, 2, P])
        vmeta = at_att("vmeta", [META, 2, P])
        aqT = at_att("aqT", [P, NAC, KT, ATT_CHUNK])
        prob = at_att("prob", [P, 3, 2, META + WIN])
        pT = at_att("pT", [P, 2, 2, P])
        pTm = at_att("pTm", [META, 2, 2, P])
        avT = sb("avT", [P, 2, NT], place["yah"])
        prod = sb("prod", [P, 2, SEQ], place["aqT"])

        mgh = sb("mgh", [P, KT, SEQ], place["qr"], F32R)
        mgl = sb("mgl", [P, KT, SEQ], place["vr"], F32R)
        orow = sb("orow", [P, 3, D], place["kwin"])
        at_ffn = Region(G0, GEND)
        hidh = at_ffn("hidh", [P, FT, SEQ], F32R)
        hidl = at_ffn("hidl", [P, FT, SEQ], F32R)
        sgate = at_ffn("sgate", [P, 2, SEQ])
        hid = at_ffn("hid", [P, 2, SEQ])
        frow = at_ffn("frow", [P, 2, D])
        res = sb("res", [P, TT, D], HT)

        ps = ctx.enter_context(nc.psum_tensor("ps", [P, 8, 512], F32))
        parked = nc.dram_tensor("parked", (SIDE, P, NT), F32).ap()

        x_landed = [sem(f"x_landed{i}") for i in range(TT + 1)]
        rows_landed = sem("rows_landed")
        const_landed = sem("const_landed")
        w_landed = [sem(f"w_landed{i}") for i in range(RING)]
        w_hi = sem("w_hi")
        w_lo = sem("w_lo")
        w_used = sem("w_used")
        freed = [sem(f"freed{i}") for i in range(2)]
        filled = [sem(f"filled{i}") for i in range(8)]
        taken = [sem(f"taken{i}") for i in range(8)]
        dve_step = sem("dve_step")
        act_step = sem("act_step")
        powers_ready = sem("powers_ready")
        var_ready = sem("var_ready")
        rstd_ready = sem("rstd_ready")
        shift_ready = sem("shift_ready")
        centred = sem("centred")
        gained = sem("gained")
        h_ready = sem("h_ready")
        hT_hi = sem("hT_hi")
        conv_done = sem("conv_done")
        silu_done = sem("silu_done")
        prep = sem("prep")
        prep_act = sem("prep_act")
        tri_ready = sem("tri_ready")
        kss_ready = [sem(f"kss_ready{g}") for g in range(2)]
        knorm_ready = [sem(f"knorm_ready{g}") for g in range(2)]
        qss_ready = [sem(f"qss_ready{g}") for g in range(2)]
        rq_ready = [sem(f"rq_ready{g}") for g in range(2)]
        level_ready = [sem(f"level_ready{g}") for g in range(2)]
        xt_ready = [sem(f"xt_ready{g}") for g in range(2)]
        r_ready = [sem(f"r_ready{g}") for g in range(2)]
        vdec_ready = [sem(f"vdec_ready{g}") for g in range(2)]
        oss_ready = [sem(f"oss_ready{g}") for g in range(2)]
        onorm_ready = [sem(f"onorm_ready{g}") for g in range(2)]
        o_ready = [sem(f"o_ready{g}") for g in range(2)]
        yh_ready = [sem(f"yh_ready{g}") for g in range(2)]
        yl_ready = [sem(f"yl_ready{g}") for g in range(2)]
        side_ready = sem("side_ready")
        side_stored = [sem(f"side_stored{i}") for i in range(3)]
        att_loaded = sem("att_loaded")
        gate_loaded = [sem(f"gate_loaded{i}") for i in range(2)]
        max_ready = sem("max_ready")
        prob_ready = sem("prob_ready")
        ya_hi = sem("ya_hi")
        merged_ready = sem("merged_ready")
        mg_hi = sem("mg_hi")
        mg_lo = sem("mg_lo")
        hid_hi = sem("hid_hi")
        hid_lo = sem("hid_lo")
        out_stored = sem("out_stored")

        steps = plan()
        use = bank_uses()

        def levels_before(n):
            return sum(levels_of(m) for m in range(n))

        def tile_index(b):
            return b if b < B_OUT else b - KT

        def slot_of(b):
            return tile_index(b) % 2, tile_index(b) // 2

        def wait_free(eng, *key):
            bank, before = use[key]
            if before:
                eng.wait_ge(taken[bank], before)

        def wait_filled(eng, *key):
            eng.wait_ge(filled[use[key][0]], filled_before(use, key) + 1)

        def wait_taken(eng, *key):
            bank, before = use[key]
            eng.wait_ge(taken[bank], before + 1)

        def heads(t, g, c, w):
            return t[:c, g, :, :w]

        def bank4(key, c, w):
            return ps[:c, use[key][0], :].rearrange("p (h t) -> p h t", h=4)[:, :, :w]

        def over_heads(i, c):
            return cst[:c, i, :c].unsqueeze(1).to_broadcast([c, 4, c])

        def per_head(t, c, w):
            return t.unsqueeze(2).to_broadcast([c, 4, w])

        def norm_tile(i):
            if i < TT:
                return xin[:, i, :], h[:, i, :], P, lnrow
            if i == TT:
                return xin[:META, i, :], hmeta[:, :], META, lnrow
            if i <= 2 * TT:
                t = i - TT - 1
                return h[:, t, :], h[:, t, :], P, orow[:, 1:3, :]
            t = i - 2 * TT - 1
            return res[:, t, :], res[:, t, :], P, frow

        def window_of(c):
            return META + ATT_CHUNK * max(c - 1, 0), ATT_CHUNK if c == 0 else WIN

        def pair_view(bank):
            return ps[:, bank:bank + 2, :].rearrange("p b (k t) -> p (b k) t", t=P)

        block = ctx.enter_context(nc.Block())

        @block.sync
        def _(sp):
            def load_x(i):
                src = x[P * i:P * (i + 1), :] if i < TT else meta
                sp.dma_start(xin[:src.shape[0], i, :], src).then_inc(x_landed[i], 16)

            load_x(0)
            sp.dma_start(lnrow[:], rows[R_LNIN:R_LNIN + 2, :].partition_broadcast(P)).then_inc(rows_landed, 16)
            for i in range(1, TT + 1):
                load_x(i)
            sp.dma_start(cst[:], consts).then_inc(const_landed, 16)
            sp.dma_start(col[:], cols).then_inc(const_landed, 16)
            sp.dma_start(srt[:], short.partition_broadcast(P)).then_inc(const_landed, 16)
            for b in range(RING):
                sp.dma_start(wst[:, b, :], wstream[b]).then_inc(w_landed[b], 16)
            with sp.Fori(0, (NBLOCKS - RING) // RING) as turn:
                for j in range(RING):
                    sp.wait_ge(w_lo, turn * RING + (j + 1))
                    sp.dma_start(wst[:, j, :], wstream[turn * RING + (RING + j)]).then_inc(w_landed[j], 16)
            for b in range(NBLOCKS - NBLOCKS % RING, NBLOCKS):
                sp.wait_ge(w_lo, b - RING + 1)
                sp.dma_start(wst[:, b % RING, :], wstream[b]).then_inc(w_landed[b % RING], 16)

        @block.tensor
        def _(pe):
            ident = cst[:, C_IDENT, :]

            def tile_step(b, k, inh, inl, first):
                slot, before = slot_of(b)
                if k == 0:
                    pe.wait_ge(w_lo, b + 1)
                    if before:
                        pe.wait_ge(freed[slot], before)
                width = inh.shape[2] - first
                parts = [(0, width)] if width <= 512 else [(0, HALF), (HALF, HALF)]
                s = slice(k * P, (k + 1) * P)
                for m, (w, v) in enumerate(((whi, inh), (whi, inl), (wlo, inh))):
                    for j, (at, n) in enumerate(parts):
                        mm = nc.tensor.matmul(ps[:, 2 * slot + j, 0:n], w[:, b % RING, s],
                                              v[:, k, first + at:first + at + n],
                                              start=(k == 0 and m == 0), stop=(k == KT - 1 and m == 2))
                if k == KT - 1:
                    mm.then_inc(w_used, 1)

            def projection_step(b, k):
                narrow = b > B_BA and not B_SIDE <= b < B_SIDE + SIDE_AKV
                tile_step(b, k, hTh, hTl, META if narrow else 0)

            def branch_step(b, k):
                if b == B_BB and k == 0:
                    for g in range(2):
                        pe.wait_ge(yl_ready[g], TT)
                if b == B_BA2 and k == 0:
                    wait_taken(pe, "pv", NUNITS // 2 - 1)
                    wait_taken(pe, "pv", NUNITS // 2 - 2)
                if b < B_BA2:
                    tile_step(b, k, yh, yl, META)
                else:
                    tile_step(b, k, yah, yal, 0)

            def turn_tile(i, key, src, c):
                pe.wait_ge(h_ready, i + 1)
                wait_free(pe, *key)
                bank = use[key][0]
                for k in range(KT):
                    mm = nc.tensor.transpose(ps[:, bank + k // 4, (k % 4) * P:(k % 4) * P + c],
                                             src[:, k * P:(k + 1) * P], ident[:c, :c])
                mm.then_inc(filled[bank], 1)

            def turn_logits():
                slot, before = slot_of(B_BA)
                pe.wait_ge(freed[slot], before + 1)
                for n in range(TT + 1):
                    t0 = chunk_of(n)[0]
                    mm = nc.tensor.transpose(ps[:, 4, n * 16:n * 16 + 16], ba_cols[:, t0:t0 + P], ident[:16, :16])
                mm.then_inc(filled[4], 1)

            def decays():
                pe.wait_ge(prep, 4)
                for n in range(TT + 1):
                    c = chunk_of(n)[1]
                    for m, mat in enumerate((C_INCL, C_GT, C_ONES)):
                        at = (3 * n + m) * GH
                        mm = nc.tensor.matmul(ps[:, 5, at:at + GH], cst[:c, mat, :], la[:c, n, :],
                                              start=(n == 0 and m == 0), stop=(n == TT and m == 2),
                                              skip_group_check=True)
                mm.then_inc(filled[5], 1)

            def delta(stage, n, g):
                t0, c = chunk_of(n)
                key = (stage, n, g)
                bank = use[key][0]
                last = levels_of(n) - 1
                if key == ("k", 0, 0):
                    pe.wait_ge(silu_done, 3 * GH)
                wait_free(pe, *key)
                toks = slice(t0, t0 + c)
                kind, level = stage[0], int(stage[1:] or 0)
                if kind == "d":
                    pe.wait_ge(tri_ready, 2 * n + g + 1)
                    nc.tensor.matmul(bank4(key, c, c), cst[:c, C_GT, :c], heads(tri_la, g, c, c),
                                     start=True, stop=True).then_inc(filled[bank], 1)
                    return
                if kind == "i":
                    pe.wait_ge(xt_ready[g], n + 1)
                elif kind == "y":
                    pe.wait_ge(level_ready[g], levels_before(n) + level + 1)
                    wait_taken(pe, "i" if level == 1 else f"x{level - 1}", n, g)
                elif kind == "z":
                    wait_taken(pe, f"y{level}", n, g)
                elif kind == "x":
                    wait_taken(pe, f"z{level}", n, g)
                elif kind == "s" or kind == "r":
                    wait_taken(pe, "t", n - 1, g)
                elif kind == "p":
                    wait_taken(pe, f"z{last}", n, g)
                    if n:
                        pe.wait_ge(r_ready[g], n)
                    else:
                        wait_taken(pe, "v", n, g)
                elif kind == "o":
                    wait_taken(pe, "p", n, g)
                    wait_taken(pe, "w", n, g)
                elif kind == "t":
                    pe.wait_ge(vdec_ready[g], n + 1)
                    wait_taken(pe, "k", n, g)
                elif kind == "f":
                    pe.wait_ge(o_ready[g], n)
                for j in range(4):
                    head = 4 * g + j
                    wide = ps[:c, bank, j * P:(j + 1) * P]
                    square = ps[:c, bank, j * P:j * P + c]
                    full = ps[:, bank, j * P:(j + 1) * P]
                    if kind in "kqv":
                        mm = nc.tensor.transpose(wide, {"k": kr, "q": qr, "v": vr}[kind][:, head, toks], ident)
                    elif kind in "ix":
                        mm = nc.tensor.transpose(square, XT[:c, g, j, :c], ident[:c, :c])
                    elif kind == "f":
                        mm = nc.tensor.transpose(full, oraw[:, g, j, :], ident)
                    else:
                        dst, lhs, rhs = {
                            "g": (square, kr[:, head, toks], kr[:, head, toks]),
                            "w": (square, kr[:, head, toks], qr[:, head, toks]),
                            "y": (square, UL[level % 2][:c, g, j, :c], X[:c, g, j, :c]),
                            "z": (square, Y[:c, g, j, :c], XT[:c, g, j, :c]),
                            "s": (wide, kr[:, head, toks], state[:, head, :]),
                            "p": (wide, XT[:c, g, j, :c], vtok[:c, g, j, :]),
                            "r": (wide, qr[:, head, toks], state[:, head, :]),
                            "o": (wide, AT[:c, g, j, :c], vnew[:c, g, j, :]),
                            "t": (full, ktok[:c, g, j, :], vdec[:c, g, j, :]),
                        }[kind]
                        mm = nc.tensor.matmul(dst, lhs, rhs, start=True, stop=True)
                mm.then_inc(filled[bank], 1)

            def values():
                pe.wait_ge(att_loaded, (1 + 2 * (NAC + 1) + NAC) * 16)
                for j in range(4):
                    wait_free(pe, "values", j)
                    for m in range(4):
                        pr, w = divmod(4 * j + m, NAC)
                        rows_ = META if w == NAC - 1 else WIN
                        t0 = 0 if w == NAC - 1 else META + ATT_CHUNK * w
                        mm = nc.tensor.transpose(ps[:rows_, 4 + j, m * P:(m + 1) * P],
                                                 avT[:, pr, t0:t0 + rows_], ident)
                    mm.then_inc(filled[4 + j], 1)

            def scores(a):
                c, pr, e = unit(a)
                t0, w = window_of(c)
                wait_free(pe, "scores", a)
                part = slice(DH * e, DH * (e + 1))
                for ip in range(2):
                    q = aqT[part, c, 4 * pr + 2 * ip:4 * pr + 2 * ip + 2, :].rearrange("p i t -> p (i t)")
                    at = ip * (META + WIN)
                    bank = 4 + a % 2
                    mm = nc.tensor.matmul(ps[:, bank, at:at + META + w], q, kwin[part, pr, c, 0:META + w],
                                          start=(ip == 0), stop=(ip == 1), skip_group_check=True)
                mm.then_inc(filled[bank], 1)

            def turn_probs(a):
                w = window_of(unit(a)[0])[1]
                wait_free(pe, "turn", a)
                pe.wait_ge(prob_ready, a + 1)
                bank, s = 6 + a % 2, a % 3
                for ip in range(2):
                    nc.tensor.transpose(ps[:w, bank, ip * P:(ip + 1) * P], prob[:, s, ip, META:META + w], ident)
                    mm = nc.tensor.transpose(ps[:META, bank, (2 + ip) * P:(3 + ip) * P], prob[:, s, ip, 0:META], ident)
                mm.then_inc(filled[bank], 1)

            def weighted_values(a):
                c, pr, e = unit(a)
                w = window_of(c)[1]
                key = ("pv", a // 2)
                bank = use[key][0]
                if e == 0:
                    wait_free(pe, *key)
                wait_taken(pe, "turn", a)
                dst = ps[DH * e:DH * (e + 1), bank, 0:2 * P]
                part = slice(DH * e, DH * (e + 1))
                nc.tensor.matmul(dst, vwin[:w, max(c - 1, 0), pr, part],
                                 pT[:w, a % 2].rearrange("p i t -> p (i t)"), start=True, stop=False)
                mm = nc.tensor.matmul(dst, vmeta[:, pr, part], pTm[:, a % 2].rearrange("p i t -> p (i t)"),
                                      start=False, stop=True)
                if e:
                    mm.then_inc(filled[bank], 1)

            def output_blocks(first, name, half, blocks, acth, actl, act_ready):
                for kb in range(blocks):
                    b = first + blocks * half + kb
                    pe.wait_ge(w_lo, b + 1)
                    if half == 0:
                        pe.wait_ge(act_ready, 2 * kb + 2)
                    for t in range(TT):
                        bank = use[(name, half, t)][0]
                        if kb == 0:
                            wait_free(pe, name, half, t)
                        toks = slice(P * t, P * (t + 1))
                        for kk in range(2):
                            k = 2 * kb + kk
                            for m, (v, w) in enumerate(((acth, whi), (actl, whi), (acth, wlo))):
                                mm = nc.tensor.matmul(ps[:, bank, :], v[:, k, toks],
                                                      w[:, b % RING, 512 * kk:512 * (kk + 1)],
                                                      start=(k == 0 and m == 0),
                                                      stop=(k == 2 * blocks - 1 and m == 2))
                        if t == TT - 1:
                            mm.then_inc(w_used, 1)
                        elif kb == blocks - 1:
                            mm.then_inc(filled[bank], 1)

            pe.wait_ge(const_landed, 3 * 16)
            for i in range(TT + 1):
                _, src, c, _ = norm_tile(i)
                turn_tile(i, ("hT", i), src, c)
            for i in range(TT + 1):
                wait_taken(pe, "hT", i)
            for what, *at in steps:
                if what == "block":
                    for k in range(KT):
                        (projection_step if at[0] < B_BB else branch_step)(at[0], k)
                elif what == "side":
                    (projection_step if at[0] < B_BB else branch_step)(*at)
                elif what == "logits":
                    turn_logits()
                elif what == "decays":
                    decays()
                elif what == "delta":
                    delta(*at)
                elif what == "values":
                    values()
                elif what == "att":
                    a = at[0]
                    if a < NUNITS:
                        scores(a)
                    if 0 <= a - ATT_LAG < NUNITS:
                        turn_probs(a - ATT_LAG)
                    if 0 <= a - ATT_LAG - 1 < NUNITS:
                        weighted_values(a - ATT_LAG - 1)
            output_blocks(B_OUT, "out", 0, KT // 2, mgh, mgl, mg_lo)
            for s in range(2):
                pe.wait_ge(freed[s], slot_of(B_OUT + KT + s)[1] if slot_of(B_OUT + KT + s)[0] == s
                           else slot_of(B_OUT + KT + 1 - s)[1])
            output_blocks(B_OUT, "out", 1, KT // 2, mgh, mgl, mg_lo)
            for t in range(TT):
                turn_tile(TT + 1 + t, ("h1T", t), h[:, t, :], P)
            for t in range(TT):
                wait_taken(pe, "h1T", t)
            for b in range(B_F1, B_F2):
                for k in range(KT):
                    tile_step(b, k, h1h, h1l, 0)
            output_blocks(B_F2, "ffn", 0, FT // 2, hidh, hidl, hid_lo)
            for s in range(2):
                pe.wait_ge(freed[s], sum(tile_index(b) % 2 == s for b in [*range(B_OUT), *range(B_F1, B_F2)]))
            output_blocks(B_F2, "ffn", 1, FT // 2, hidh, hidl, hid_lo)

        @block.scalar
        def _(act):
            own = [0]

            def step(ins):
                own[0] += 1
                ins.then_inc(act_step, 1)
                act.wait_ge(act_step, own[0])

            def split_hi(b):
                if b >= NBLOCKS:
                    return
                act.wait_ge(w_landed[b % RING], 16 * (b // RING + 1))
                if b >= RING:
                    act.wait_ge(w_used, b - RING + 1)
                nc.scalar.activation(whi[:, b % RING, :], wst[:, b % RING, :], ACT.Copy).then_inc(w_hi, 1)

            def centre(i):
                src, dst, c, _ = norm_tile(i)
                act.wait_ge(shift_ready, i + 1)
                nc.scalar.activation(dst, src, ACT.Identity, scale=rstd[:c, i % TT:i % TT + 1],
                                     bias=shift[:c, i % TT:i % TT + 1]).then_inc(centred, 1)

            def hi_of_tile(i, key, dst, at, c):
                wait_filled(act, *key)
                src = pair_view(use[key][0])[:, :, :c]
                nc.scalar.activation(dst[:, :, at:at + c], src, ACT.Copy).then_inc(hT_hi, 1)

            def projection(b):
                slot, before = slot_of(b)
                act.wait_ge(w_used, b + 1)
                wide = ps[:, 2 * slot:2 * slot + 2, 0:HALF]
                narrow = ps[:, 2 * slot, :]
                bias = col[:, COL_BIAS + b:COL_BIAS + b + 1]
                if b < B_BA:
                    if b >= 2:
                        act.wait_ge(conv_done, b - 1)
                    dst = cbuf[:, b % 2, CONV_K - 1:].rearrange("p (j t) -> p j t", j=2)
                    nc.scalar.activation(dst, wide, ACT.Identity, bias=bias).then_inc(freed[slot], 1)
                elif b == B_BA:
                    dst = ba_cols[:, :].rearrange("p (j t) -> p j t", j=2)
                    nc.scalar.activation(dst, wide[:16], ACT.Copy).then_inc(freed[slot], 1)
                else:
                    nc.scalar.activation(sz[:, b - B_Z, :], narrow, ACT.Silu, bias=bias).then_inc(freed[slot], 1)

            def silu_of_conv(b):
                act.wait_ge(conv_done, b + 1)
                dst = (kr, vr, qr)[b // GH][:, b % GH, :]
                nc.scalar.activation(dst, cacc[:, b % 2, :], ACT.Silu).then_inc(silu_done, 1)

            def log_decay_terms():
                act.wait_ge(prep, 2)
                step(nc.scalar.activation(soft[:], soft[:], ACT.Exp, scale=-1.0))
                step(nc.scalar.activation(soft[:], soft[:], ACT.Ln, bias=1.0))
                step(nc.scalar.activation(neg_a[:], srt[:, S_ALOG:S_ALOG + GH], ACT.Exp))
                nc.scalar.activation(beta[:], logits[:, :, 0:GH], ACT.Tanh, scale=0.5).then_inc(prep_act, 1)

            def decays():
                wait_filled(act, "decays")
                src = ps[:, 5, 0:3 * GH * (TT + 1)].rearrange("p (n m h) -> p n m h", m=3, h=GH)
                nc.scalar.activation(eg[:], src, ACT.Exp).then_inc(taken[5], 1)

            def delta(stage, n, g):
                c = chunk_of(n)[1]
                key = (stage, n, g)
                bank = use[key][0]
                kind = stage[0]
                if kind == "k":
                    wait_filled(act, *key)
                    nc.scalar.activation(heads(ktok, g, c, P), bank4(key, c, P), ACT.Copy)
                    if n > 1:
                        act.wait_ge(oss_ready[g], n - 1)
                    nc.scalar.activation(heads(ksq, g, c, P), bank4(key, c, P), ACT.Square).then_inc(taken[bank], 1)
                elif kind == "q":
                    wait_filled(act, *key)
                    nc.scalar.activation(heads(qsq, g, c, P), bank4(key, c, P), ACT.Square).then_inc(taken[bank], 1)
                elif kind == "d":
                    wait_filled(act, *key)
                    if n > 2:
                        act.wait_ge(yl_ready[g], n - 2)
                    nc.scalar.activation(heads(dec, g, c, c), bank4(key, c, c), ACT.Exp).then_inc(taken[bank], 1)
                elif kind in "ixy":
                    wait_filled(act, *key)
                    dst = Y if kind == "y" else X
                    nc.scalar.activation(heads(dst, g, c, c), bank4(key, c, c), ACT.Copy).then_inc(taken[bank], 1)
                elif kind == "f":
                    wait_taken(act, *key)
                    t0 = chunk_of(n)[0]
                    nc.scalar.activation(yh[:, 4 * g:4 * g + 4, t0:t0 + P], youT[:, g], ACT.Copy).then_inc(yh_ready[g], 1)

            def store_side(j):
                if j < SIDE_AQ:
                    slot, before = slot_of(B_SIDE + j)
                    act.wait_ge(freed[slot], before + 1)
                else:
                    act.wait_ge(side_ready, j - SIDE_AQ + 1)
                w = NT if j < SIDE_AKV else SEQ
                act.dma_start(parked[j, :, 0:w], side[:, j % 3, 0:w]).then_inc(side_stored[j % 3], 16)

            def side_tile(b):
                j = b - B_SIDE
                slot, before = slot_of(b)
                act.wait_ge(w_used, b + 1)
                if j >= 3:
                    act.wait_ge(side_stored[j % 3], 16 * (j // 3))
                if j < SIDE_AKV:
                    dst = side[:, j % 3, :].rearrange("p (j t) -> p j t", j=2)
                    ins = nc.scalar.activation(dst, ps[:, 2 * slot:2 * slot + 2, 0:HALF], ACT.Identity,
                                               bias=col[:, COL_BIAS + b:COL_BIAS + b + 1])
                elif j < SIDE_AQ:
                    ins = nc.scalar.activation(side[:, j % 3, 0:SEQ], ps[:, 2 * slot, :], ACT.Identity,
                                               bias=col[:, COL_BIAS + b:COL_BIAS + b + 1])
                else:
                    ins = nc.scalar.activation(side[:, j % 3, 0:SEQ], ps[:, 2 * slot, :], ACT.Tanh, scale=0.5,
                                               bias=halfcol[:, COL_BIAS + b:COL_BIAS + b + 1])
                ins.then_inc(freed[slot], 1)
                if j:
                    store_side(j - 1)

            def load_gate(m):
                act.dma_start(gate[:, m % 2, :], parked[SIDE_AQ + m, :, 0:SEQ]).then_inc(gate_loaded[m % 2], 16)

            def reload():
                store_side(SIDE - 1)
                for i in range(3):
                    act.wait_ge(side_stored[i], 16 * len(range(i, SIDE, 3)))
                for g in range(2):
                    act.wait_ge(yl_ready[g], TT)
                load_gate(0)
                load_gate(1)
                act.dma_start(avT[:], parked[2:SIDE_AKV].rearrange("i p t -> p i t")).then_inc(att_loaded, 16)
                for pr in range(2):
                    for c in range(NAC):
                        t0 = window_of(c)[0]
                        act.dma_start(kwin[:, pr, c, META:], parked[pr, :, t0:t0 + WIN]).then_inc(att_loaded, 16)
                    act.dma_start(kwin[:, pr, :, 0:META],
                                  parked[pr, :, 0:META].unsqueeze(1).to_broadcast([P, NAC, META])).then_inc(att_loaded, 16)
                for c in range(NAC):
                    src = parked[SIDE_AKV:SIDE_AQ, :, ATT_CHUNK * c:ATT_CHUNK * (c + 1)]
                    act.dma_start(aqT[:, c], src.rearrange("i p t -> p i t")).then_inc(att_loaded, 16)

            def values():
                for j in range(4):
                    wait_filled(act, "values", j)
                    pr, w0 = divmod(4 * j, NAC)
                    n = 3 if w0 else 4
                    src = ps[:, 4 + j, 0:n * P].rearrange("p (w t) -> p w t", w=n)
                    ins = nc.scalar.activation(vwin[:, w0:w0 + n, pr, :], src, ACT.Copy)
                    if w0:
                        ins = nc.scalar.activation(vmeta[:, pr, :], ps[:META, 4 + j, 3 * P:4 * P], ACT.Copy)
                    ins.then_inc(taken[4 + j], 1)

            def attention(a):
                b = a - ATT_LAG
                if 0 <= b < NUNITS:
                    w = window_of(unit(b)[0])[1]
                    wait_filled(act, "turn", b)
                    bank = 6 + b % 2
                    src = ps[:, bank, :].rearrange("p (i t) -> p i t", t=P)
                    nc.scalar.activation(pT[:w, b % 2], src[:w, 0:2], ACT.Copy)
                    nc.scalar.activation(pTm[:, b % 2], src[:META, 2:4], ACT.Copy).then_inc(taken[bank], 1)
                if a < NUNITS:
                    w = META + window_of(unit(a)[0])[1]
                    s = a % 2
                    act.wait_ge(max_ready, a + 1)
                    if a >= 3:
                        wait_filled(act, "turn", a - 3)
                    nc.scalar.activation(sink_exp[:, s, :], sink_arg[:, s, :], ACT.Exp)
                    for ip in range(2):
                        at = ip * (META + WIN)
                        ins = nc.scalar.activation(prob[:, a % 3, ip, 0:w], ps[:, 4 + s, at:at + w], ACT.Exp,
                                                   scale=DH ** -0.5, bias=neg_amax[:, s, ip:ip + 1],
                                                   accum_out=asum[:, s, ip:ip + 1])
                    ins.then_inc(taken[4 + s], 1)
                b = a - ATT_LAG - 1
                if 0 <= b < NUNITS and b % 2:
                    c, pr, _ = unit(b)
                    key = ("pv", b // 2)
                    wait_filled(act, *key)
                    src = ps[:, use[key][0], 0:2 * P].rearrange("p (i t) -> p i t", i=4)
                    nc.scalar.activation(yah[:, 4 * pr:4 * pr + 4, ATT_CHUNK * c:ATT_CHUNK * (c + 1)], src,
                                         ACT.Copy).then_inc(ya_hi, 1)

            def next_gate(m):
                if m + 2 < 2 * KT:
                    slot, before = slot_of(B_BB + m)
                    act.wait_ge(freed[slot], before + 1)
                    load_gate(m + 2)

            def merged_hi(m):
                act.wait_ge(merged_ready, m + 1)
                nc.scalar.activation(mgh[:, m, :], merged[:, m, :], ACT.Copy).then_inc(mg_hi, 1)

            for i in range(TT + 3):
                if i <= TT:
                    centre(i)
                if i >= 2:
                    at, c = (META + P * (i - 2), P) if i - 2 < TT else (0, META)
                    hi_of_tile(i - 2, ("hT", i - 2), hTh, at, c)
                if 2 <= i < 2 + RING:
                    split_hi(i - 2)
            for what, *at in steps:
                if what == "block":
                    b = at[0]
                    if b < B_BB:
                        projection(b)
                        split_hi(b + RING)
                        if 1 <= b <= B_BA:
                            silu_of_conv(b - 1)
                    else:
                        split_hi(b + RING)
                        merged_hi(b - B_BA2)
                        next_gate(b - B_BB)
                elif what == "sideend":
                    b = at[0]
                    if b < B_BB:
                        side_tile(b)
                    split_hi(b + RING)
                    if b >= B_BB:
                        next_gate(b - B_BB)
                elif what == "logits":
                    log_decay_terms()
                elif what == "decays":
                    decays()
                elif what == "delta":
                    delta(*at)
                elif what == "reload":
                    reload()
                elif what == "values":
                    values()
                elif what == "att":
                    attention(at[0])
                    if at[0] == NUNITS + ATT_LAG:
                        act.dma_start(orow[:], rows[R_BOUT:R_BOUT + 3, :].partition_broadcast(P)).then_inc(rows_landed, 16)
            for b in range(B_OUT, B_F1):
                split_hi(b + RING)
            for t in range(TT + 2):
                if t < TT:
                    centre(TT + 1 + t)
                if t >= 2:
                    hi_of_tile(TT - 1 + t, ("h1T", t - 2), h1h, P * (t - 2), P)
            for f in range(FT):
                b = B_F1 + 2 * f
                slot, before = slot_of(b)
                act.wait_ge(w_used, b + 1)
                nc.scalar.activation(sgate[:, f % 2, :], ps[:, 2 * slot, :], ACT.Silu).then_inc(freed[slot], 1)
                split_hi(b + RING)
                split_hi(b + 1 + RING)
                up, upbefore = slot_of(b + 1)
                act.wait_ge(freed[up], upbefore + 1)
                nc.scalar.activation(hidh[:, f, :], hid[:, f % 2, :], ACT.Copy).then_inc(hid_hi, 1)
                if f == 0:
                    act.dma_start(frow[:], rows[R_LN2:R_LN2 + 2, :].partition_broadcast(P)).then_inc(rows_landed, 16)
            for b in range(B_F2, NBLOCKS - RING):
                split_hi(b + RING)
            for t in range(TT):
                centre(2 * TT + 1 + t)
            for t in range(TT):
                act.wait_ge(h_ready, 2 * TT + 2 + t)
                act.dma_start(out[P * t:P * (t + 1), :], res[:, t, :]).then_inc(out_stored, 16)
            act.wait_ge(out_stored, 16 * TT)

        @block.vector
        def _(dve):
            own = [0]

            def step(ins):
                own[0] += 1
                ins.then_inc(dve_step, 1)
                dve.wait_ge(dve_step, own[0])

            def tell(ins, semaphore, value):
                ins.then_inc(semaphore, 1)
                dve.wait_ge(semaphore, value)

            def take(ins, *key):
                bank, before = use[key]
                tell(ins, taken[bank], before + 1)

            def free_slot(ins, b):
                slot, before = slot_of(b)
                tell(ins, freed[slot], before + 1)

            def half_stats(i, j):
                src, _, c, _ = norm_tile(i)
                step(nc.vector.bn_stats(st6[:c, i % TT, j, :], src[:, 512 * j:512 * (j + 1)]))

            def variance(i):
                _, _, c, _ = norm_tile(i)
                m = i % TT
                step(nc.vector.bn_aggr(mv[:c, m, :], st6[:c, m, :, :]))
                tell(nc.vector.tensor_scalar(var_eps[:c, m:m + 1], mv[:c, m, 1:2], LN_EPS, None, ALU.add),
                     var_ready, i + 1)

            def offset(i):
                _, _, c, _ = norm_tile(i)
                m = i % TT
                dve.wait_ge(rstd_ready, i + 1)
                tell(nc.vector.scalar_tensor_tensor(out=shift[:c, m:m + 1], in0=mv[:c, m, 0:1], scalar=-1.0,
                                                    in1=rstd[:c, m:m + 1], op0=ALU.mult, op1=ALU.mult),
                     shift_ready, i + 1)

            def gain_tile(i):
                _, dst, c, gain = norm_tile(i)
                dve.wait_ge(centred, i + 1)
                tell(nc.vector.tensor_tensor(dst, dst, gain[:c, 0, :], ALU.mult), gained, i + 1)

            def lo_of_tile(i, key, hi, lo, at, c, n):
                dve.wait_ge(hT_hi, n + 1)
                src = pair_view(use[key][0])[:, :, :c]
                s = slice(at, at + c)
                ins = nc.vector.tensor_tensor(lo[:, :, s], src, hi[:, :, s].bitcast(F32), ALU.subtract)
                bank, before = use[key]
                ins.then_inc(taken[bank], 1)
                dve.wait_ge(taken[bank], before + 1)

            def convolve(b):
                slot, before = slot_of(b)
                dve.wait_ge(freed[slot], before + 1)
                if b >= 2:
                    dve.wait_ge(silu_done, b - 1)
                acc = cacc[:, b % 2, :]
                for i in range(CONV_K):
                    tap = col[:, COL_CONV + CONV_K * b + i:COL_CONV + CONV_K * b + i + 1]
                    src = cbuf[:, b % 2, i:i + NT]
                    if i == 0:
                        step(nc.vector.tensor_scalar(acc, src, tap, None, ALU.mult))
                        continue
                    ins = nc.vector.scalar_tensor_tensor(out=acc, in0=src, scalar=tap, in1=acc,
                                                         op0=ALU.mult, op1=ALU.add)
                    if i < CONV_K - 1:
                        step(ins)
                    else:
                        tell(ins, conv_done, b + 1)

            def decay_logits():
                wait_filled(dve, "logits")
                n = TT + 1
                src = ps[:, 4, 0:16 * n].rearrange("p (n m) -> p n m", m=16)
                row = lambda at, w: srt[:, at:at + w].unsqueeze(1).to_broadcast([P, n, w])
                take(nc.vector.tensor_tensor(logits[:], src, row(S_BIAS, 16), ALU.add), "logits")
                tell(nc.vector.tensor_tensor(la[:], logits[:, :, GH:], row(S_DT, GH), ALU.add), prep, 1)
                tell(nc.vector.scalar_tensor_tensor(out=soft[:], in0=la[:], scalar=-1.0, in1=la[:],
                                                    op0=ALU.mult, op1=ALU.max), prep, 2)
                dve.wait_ge(prep_act, 1)
                step(nc.vector.scalar_tensor_tensor(out=la[:], in0=la[:], scalar=0.0, in1=soft[:],
                                                    op0=ALU.max, op1=ALU.add))
                step(nc.vector.tensor_scalar(neg_a[:], neg_a[:], -1.0, None, ALU.mult))
                tell(nc.vector.tensor_scalar(beta[:], beta[:], 0.5, 0.5, ALU.mult, ALU.add), prep, 3)
                tell(nc.vector.tensor_tensor(la[:], la[:], neg_a[:, :].unsqueeze(1).to_broadcast([P, n, GH]),
                                             ALU.mult), prep, 4)

            def delta(stage, n, g):
                t0, c = chunk_of(n)
                key = (stage, n, g)
                kind = stage[0]
                hs = slice(4 * g, 4 * g + 4)
                tt = nc.vector.tensor_tensor
                if kind == "k":
                    if n > 1:
                        scale_output(n - 1, g)
                    step_la = per_head(la[:c, n, hs], c, c)
                    tell(tt(heads(tri_la, g, c, c), over_heads(C_INCL, c), step_la, ALU.mult), tri_ready, 2 * n + g + 1)
                    wait_taken(dve, *key)
                    step(nc.vector.tensor_reduce(kss[:c, g, :], heads(ksq, g, c, P), AX_X, ALU.add))
                    tell(nc.vector.tensor_scalar(kss[:c, g, :], kss[:c, g, :], NORM_EPS, None, ALU.add),
                         kss_ready[g], n + 1)
                    step(nc.vector.reciprocal(rk2[:c, g, :], kss[:c, g, :]))
                    step(tt(rho[:c, g, :], rk2[:c, g, :], beta[:c, n, hs], ALU.mult))
                elif kind == "q":
                    wait_taken(dve, *key)
                    step(nc.vector.tensor_reduce(qss[:c, g, :], heads(qsq, g, c, P), AX_X, ALU.add))
                    tell(nc.vector.tensor_scalar(qss[:c, g, :], qss[:c, g, :], NORM_EPS, None, ALU.add),
                         qss_ready[g], n)
                elif kind == "v":
                    wait_filled(dve, *key)
                    dve.wait_ge(knorm_ready[g], n + 1)
                    take(tt(heads(vtok, g, c, P), bank4(key, c, P), per_head(knorm[:c, g, :], c, P), ALU.mult), *key)
                elif kind == "g":
                    wait_filled(dve, *key)
                    take(tt(heads(U, g, c, c), bank4(key, c, c), heads(dec, g, c, c), ALU.mult), *key)
                    step(tt(heads(U, g, c, c), heads(U, g, c, c), per_head(rho[:c, g, :], c, c), ALU.mult))
                    mask_level(n, g, c, 0)
                    tell(tt(heads(XT, g, c, c), over_heads(C_IDENT, c), heads(UL[0], g, c, c), ALU.subtract),
                         xt_ready[g], n + 1)
                elif kind == "w":
                    wait_filled(dve, *key)
                    take(tt(heads(AT, g, c, c), bank4(key, c, c), heads(dec, g, c, c), ALU.mult), *key)
                elif kind == "d":
                    wait_taken(dve, *key)
                    step(tt(heads(dec, g, c, c), heads(dec, g, c, c), over_heads(C_INCL, c), ALU.mult))
                elif kind == "i":
                    mask_level(n, g, c, 1)
                elif kind == "y":
                    if int(stage[1:]) + 1 < levels_of(n):
                        mask_level(n, g, c, int(stage[1:]) + 1)
                elif kind == "z":
                    wait_filled(dve, *key)
                    take(tt(heads(XT, g, c, c), heads(XT, g, c, c), bank4(key, c, c), ALU.subtract), *key)
                elif kind == "s":
                    wait_filled(dve, *key)
                    take(tt(heads(Y, g, c, P), bank4(key, c, P), per_head(neg_eg[:c, n, hs], c, P), ALU.mult), *key)
                    tell(tt(heads(vtok, g, c, P), heads(vtok, g, c, P), heads(Y, g, c, P), ALU.add), r_ready[g], n)
                elif kind == "p":
                    wait_filled(dve, *key)
                    take(tt(heads(vnew, g, c, P), bank4(key, c, P), per_head(rho[:c, g, :], c, P), ALU.mult), *key)
                elif kind == "r":
                    wait_filled(dve, *key)
                    take(tt(heads(oraw, g, c, P), bank4(key, c, P), per_head(eg[:c, n, 0, hs], c, P), ALU.mult), *key)
                elif kind == "o":
                    wait_filled(dve, *key)
                    take(tt(heads(oraw, g, c, P), heads(oraw, g, c, P), bank4(key, c, P), ALU.add), *key)
                    dve.wait_ge(rq_ready[g], n)
                    step(nc.vector.tensor_scalar(rq[:, g, :], rq[:, g, :], DK ** -0.5, None, ALU.mult))
                    step(tt(rq2[:, g, :], rq[:, g, :], rq[:, g, :], ALU.mult))
                    step(tt(osq[:, g], oraw[:, g], oraw[:, g], ALU.mult))
                    step(nc.vector.tensor_reduce(oss[:, g, :], osq[:, g], AX_X, ALU.add))
                    step(nc.vector.scalar_tensor_tensor(out=oss[:, g, :], in0=oss[:, g, :], scalar=1.0 / DK,
                                                        in1=rq2[:, g, :], op0=ALU.mult, op1=ALU.mult))
                    tell(nc.vector.tensor_scalar(oss[:, g, :], oss[:, g, :], NORM_EPS, None, ALU.add), oss_ready[g], n)
                    if n == TT:
                        scale_output(n, g)
                elif kind == "t":
                    s = state[:, hs, :]
                    if n:
                        step(tt(s, s, per_head(eg[:, n, 2, hs], P, P), ALU.mult))
                    wait_filled(dve, *key)
                    if n:
                        take(tt(s, s, bank4(key, P, P), ALU.add), *key)
                    else:
                        take(nc.vector.tensor_copy(s, bank4(key, P, P)), *key)
                elif kind == "f":
                    wait_filled(dve, *key)
                    gated = sz[:, hs, t0 - META:t0 - META + P]
                    take(nc.vector.scalar_tensor_tensor(out=youT[:, g], in0=bank4(key, P, P),
                                                        scalar=col[:, COL_NORM:COL_NORM + 1], in1=gated,
                                                        op0=ALU.mult, op1=ALU.mult), *key)

            def mask_level(n, g, c, level):
                tell(nc.vector.tensor_tensor(heads(UL[level % 2], g, c, c), heads(U, g, c, c),
                                             over_heads(C_LEVEL + level, c), ALU.mult),
                     level_ready[g], levels_before(n) + level + 1)

            def scale_output(n, g):
                dve.wait_ge(onorm_ready[g], n)
                step(nc.vector.tensor_tensor(onorm[:, g, :], onorm[:, g, :], rq[:, g, :], ALU.mult))
                tell(nc.vector.tensor_tensor(oraw[:, g], oraw[:, g], per_head(onorm[:, g, :], P, P), ALU.mult),
                     o_ready[g], n)

            def gate_of_side(b):
                j = b - B_SIDE
                if j < SIDE_AQ:
                    return
                slot, before = slot_of(b)
                dve.wait_ge(freed[slot], before + 1)
                s = side[:, j % 3, 0:SEQ]
                tell(nc.vector.tensor_scalar(s, s, 0.5, 0.5, ALU.mult, ALU.add), side_ready, j - SIDE_AQ + 1)

            def branch(b):
                m = b - B_BB
                slot, _ = slot_of(b)
                dve.wait_ge(w_used, b + 1)
                dve.wait_ge(gate_loaded[m % 2], 16 * (m // 2 + 1))
                src = ps[:, 2 * slot, :]
                if m < KT:
                    free_slot(nc.vector.tensor_tensor(merged[:, m, :], src, gate[:, m % 2, :], ALU.mult), b)
                    return
                free_slot(nc.vector.tensor_tensor(prod[:, m % 2, :], src, gate[:, m % 2, :], ALU.mult), b)
                if m == KT:
                    dve.wait_ge(rows_landed, 2 * 16)
                if m < KT + TT:
                    t = m - KT
                    step(nc.vector.scalar_tensor_tensor(out=h[:, t, :], in0=h[:, t, :], scalar=ALPHA,
                                                        in1=orow[:, 0, :], op0=ALU.mult, op1=ALU.add))
                dst = merged[:, m - KT, :]
                tell(nc.vector.tensor_tensor(dst, dst, prod[:, m % 2, :], ALU.add), merged_ready, m - KT + 1)

            def attention(a):
                if a < NUNITS:
                    w = META + window_of(unit(a)[0])[1]
                    s, group = a % 2, a % 4
                    wait_filled(dve, "scores", a)
                    src = ps[:, 4 + s, 0:2 * (META + WIN)].rearrange("p (i t) -> p i t", i=2)[:, :, 0:w]
                    step(nc.vector.tensor_reduce(amax[:, s, :], src, AX_X, ALU.max))
                    sink = col[:, COL_SINK + 2 * group:COL_SINK + 2 * group + 2]
                    step(nc.vector.scalar_tensor_tensor(out=amax[:, s, :], in0=amax[:, s, :], scalar=DH ** -0.5,
                                                        in1=sink, op0=ALU.mult, op1=ALU.max))
                    step(nc.vector.tensor_scalar(neg_amax[:, s, :], amax[:, s, :], -1.0, None, ALU.mult))
                    tell(nc.vector.tensor_tensor(sink_arg[:, s, :], sink, amax[:, s, :], ALU.subtract),
                         max_ready, a + 1)
                if 1 <= a <= NUNITS:
                    b = a - 1
                    w = META + window_of(unit(b)[0])[1]
                    s = b % 2
                    wait_taken(dve, "scores", b)
                    step(nc.vector.tensor_tensor(atot[:, s, :], asum[:, s, :], sink_exp[:, s, :], ALU.add))
                    step(nc.vector.reciprocal(arec[:, s, :], atot[:, s, :]))
                    pr_ = prob[:, b % 3, :, 0:w]
                    tell(nc.vector.tensor_tensor(pr_, pr_, arec[:, s, :].unsqueeze(2).to_broadcast([P, 2, w]),
                                                 ALU.mult), prob_ready, b + 1)
                b = a - ATT_LAG - 1
                if 0 <= b < NUNITS and b % 2:
                    c, pr, _ = unit(b)
                    key = ("pv", b // 2)
                    dve.wait_ge(ya_hi, b // 2 + 1)
                    src = ps[:, use[key][0], 0:2 * P].rearrange("p (i t) -> p i t", i=4)
                    at = (slice(None), slice(4 * pr, 4 * pr + 4), slice(ATT_CHUNK * c, ATT_CHUNK * (c + 1)))
                    take(nc.vector.tensor_tensor(yal[at], src, yah[at].bitcast(F32), ALU.subtract), *key)

            def wait_half(name, half, t, last_block):
                if t < TT - 1:
                    wait_filled(dve, name, half, t)
                else:
                    dve.wait_ge(w_used, last_block + 1)

            def add_mixer(half, t):
                wait_half("out", half, t, B_OUT + KT // 2 * (half + 1) - 1)
                dst = h[:, t, 512 * half:512 * (half + 1)]
                take(nc.vector.tensor_tensor(dst, dst, ps[:, use[("out", half, t)][0], :], ALU.add), "out", half, t)
                half_stats(TT + 1 + t, half)

            def add_ffn(half, t):
                wait_half("ffn", half, t, B_F2 + FT // 2 * (half + 1) - 1)
                cs = slice(512 * half, 512 * (half + 1))
                take(nc.vector.scalar_tensor_tensor(out=res[:, t, cs], in0=h[:, t, cs], scalar=ALPHA,
                                                    in1=ps[:, use[("ffn", half, t)][0], :],
                                                    op0=ALU.mult, op1=ALU.add), "ffn", half, t)
                half_stats(2 * TT + 1 + t, half)

            step(nc.vector.memset(cbuf[:, :, 0:CONV_K - 1], 0.0))
            step(nc.vector.memset(half[:], 0.5))
            tell(nc.vector.memset(minus_half[:], -0.5), powers_ready, 1)
            for i in range(TT + 5):
                if i <= TT:
                    dve.wait_ge(x_landed[i], 16)
                    half_stats(i, 0)
                    half_stats(i, 1)
                    variance(i)
                if 1 <= i <= TT + 1:
                    offset(i - 1)
                if i == 2:
                    dve.wait_ge(rows_landed, 16)
                if 2 <= i <= TT + 2:
                    gain_tile(i - 2)
                if i >= 4:
                    j = i - 4
                    at, c = (META + P * j, P) if j < TT else (0, META)
                    lo_of_tile(j, ("hT", j), hTh, hTl, at, c, j)
            dve.wait_ge(const_landed, 3 * 16)
            step(nc.vector.tensor_scalar(halfcol[:], col[:], 0.5, None, ALU.mult))
            for what, *at in steps:
                if what == "block" and at[0] < B_BA:
                    convolve(at[0])
                elif what == "block" and at[0] >= B_BB or what == "sideend" and at[0] >= B_BB:
                    branch(at[0])
                elif what == "sideend":
                    gate_of_side(at[0])
                elif what == "logits":
                    decay_logits()
                elif what == "decays":
                    wait_taken(dve, "decays")
                    step(nc.vector.tensor_scalar(neg_eg[:], eg[:, :, 0, :], -1.0, None, ALU.mult))
                elif what == "delta":
                    delta(*at)
                elif what == "att":
                    attention(at[0])
            for t in range(TT):
                add_mixer(0, t)
            for t in range(TT + 3):
                if t < TT:
                    add_mixer(1, t)
                    variance(TT + 1 + t)
                if 1 <= t <= TT:
                    offset(TT + t)
                    gain_tile(TT + t)
                if t >= 3:
                    lo_of_tile(t - 3, ("h1T", t - 3), h1h, h1l, P * (t - 3), P, TT - 2 + t)
            for f in range(FT):
                b = B_F1 + 2 * f + 1
                gslot, gbefore = slot_of(b - 1)
                dve.wait_ge(w_used, b + 1)
                dve.wait_ge(freed[gslot], gbefore + 1)
                if f >= 2:
                    dve.wait_ge(hid_lo, f - 1)
                free_slot(nc.vector.tensor_tensor(hid[:, f % 2, :], ps[:, 2 * slot_of(b)[0], :],
                                                  sgate[:, f % 2, :], ALU.mult), b)
            dve.wait_ge(rows_landed, 3 * 16)
            for t in range(TT):
                add_ffn(0, t)
            for t in range(TT + 1):
                if t < TT:
                    add_ffn(1, t)
                    variance(2 * TT + 1 + t)
                if t:
                    offset(2 * TT + t)
                    gain_tile(2 * TT + t)

        @block.gpsimd
        def _(pool):
            def split_lo(b):
                if b >= NBLOCKS:
                    return
                s = b % RING
                pool.wait_ge(w_hi, b + 1)
                if b >= RING:
                    pool.wait_ge(w_used, b - RING + 1)
                nc.gpsimd.tensor_tensor(wlo[:, s, :], wst[:, s, :], whi[:, s, :].bitcast(F32),
                                        ALU.subtract).then_inc(w_lo, 1)

            def power(dst, src, exponent, semaphore, wait, value):
                pool.wait_ge(wait, value)
                nc.gpsimd.tensor_tensor(dst, src, exponent, ALU.pow).then_inc(semaphore, 1)

            def norm_power(i):
                c = META if i == TT else P
                m = slice(i % TT, i % TT + 1)
                power(rstd[:c, m], var_eps[:c, m], minus_half[:c, 0:1], rstd_ready, var_ready, i + 1)

            def add_offset(i):
                _, dst, c, gain = norm_tile(i)
                pool.wait_ge(gained, i + 1)
                nc.gpsimd.tensor_tensor(dst, dst, gain[:c, 1, :], ALU.add).then_inc(h_ready, 1)

            def delta(stage, n, g):
                c = chunk_of(n)[1]
                kind = stage[0]
                hs = slice(4 * g, 4 * g + 4)
                tt = nc.gpsimd.tensor_tensor
                small = (slice(0, c), g)
                if kind == "k":
                    power(knorm[small], kss[small], half[:c, 0:4], knorm_ready[g], kss_ready[g], n + 1)
                elif kind == "q":
                    power(rq[small], qss[small], minus_half[:c, 0:4], rq_ready[g], qss_ready[g], n)
                elif kind == "p" and n < TT:
                    wait_taken(pool, stage, n, g)
                    tt(heads(vdec, g, c, P), heads(vnew, g, c, P), per_head(eg[:c, n, 1, hs], c, P),
                       ALU.mult).then_inc(vdec_ready[g], 1)
                elif kind == "o":
                    power(onorm[small], oss[small], minus_half[:c, 0:4], onorm_ready[g], oss_ready[g], n)
                elif kind == "f":
                    t0 = chunk_of(n)[0]
                    pool.wait_ge(yh_ready[g], n)
                    at = (slice(None), hs, slice(t0, t0 + P))
                    tt(yl[at], youT[:, g], yh[at].bitcast(F32), ALU.subtract).then_inc(yl_ready[g], 1)

            pool.wait_ge(powers_ready, 1)
            for i in range(TT + 3):
                if i <= TT:
                    norm_power(i)
                if i >= 2:
                    add_offset(i - 2)
                if 2 <= i < 2 + RING:
                    split_lo(i - 2)
            for what, *at in steps:
                if what in ("block", "sideend"):
                    b = at[0]
                    split_lo(b + RING)
                    if b >= B_BA2:
                        m = b - B_BA2
                        pool.wait_ge(mg_hi, m + 1)
                        nc.gpsimd.tensor_tensor(mgl[:, m, :], merged[:, m, :], mgh[:, m, :].bitcast(F32),
                                                ALU.subtract).then_inc(mg_lo, 1)
                elif what == "delta":
                    delta(*at)
            for b in range(B_OUT, B_F1):
                split_lo(b + RING)
            for t in range(TT + 1):
                if t < TT:
                    norm_power(TT + 1 + t)
                if t:
                    add_offset(TT + t)
            for f in range(FT):
                b = B_F1 + 2 * f
                split_lo(b + RING)
                split_lo(b + 1 + RING)
                pool.wait_ge(hid_hi, f + 1)
                nc.gpsimd.tensor_tensor(hidl[:, f, :], hid[:, f % 2, :], hidh[:, f, :].bitcast(F32),
                                        ALU.subtract).then_inc(hid_lo, 1)
            for b in range(B_F2, NBLOCKS - RING):
                split_lo(b + RING)
            for t in range(TT + 1):
                if t < TT:
                    norm_power(2 * TT + 1 + t)
                if t:
                    add_offset(2 * TT + t)


def constant_matrices():
    j, i = np.mgrid[0:P, 0:P]
    mats = [j == i, j <= i, j > i, j >= 0]
    for level in range(LEVELS):
        size = 1 << level
        mats.append((i // (2 * size) == j // (2 * size)) & (i // size % 2 == 1) & (j // size % 2 == 0))
    return np.ascontiguousarray(np.stack(mats, 1).astype(np.float32))


def lay_out(a):
    w_in, b_in = a["w_in"][0], a["b_in"][0]
    at = np.cumsum([0, A_HEADS * DH, A_KV * DH, A_KV * DH, GH * DK, GH * DK, GH * DK, GH * DK, GH, GH, D, D])
    aq, ak, av, gq, gk, gv, gz, gb, ga, mga, mgb = at[:-1]
    heads = [8 * pr + 4 * e + i for pr in range(2) for i in range(4) for e in range(2)]
    aq_rows = np.concatenate([np.arange(DH * h, DH * (h + 1)) for h in heads])
    tiles = [np.arange(start + P * i, start + P * (i + 1)) for start in (gk, gv, gq) for i in range(GH)]
    tiles += [np.arange(gb, gb + P)]
    tiles += [np.arange(gz + P * i, gz + P * (i + 1)) for i in range(GH)]
    tiles += [np.arange(start + P * i, start + P * (i + 1)) for start in (ak, av) for i in range(2)]
    tiles += [aq + aq_rows[P * i:P * (i + 1)] for i in range(KT)]
    tiles += [np.arange(start + P * i, start + P * (i + 1)) for start in (mgb, mga) for i in range(KT)]

    def columns(w, which):
        return w[:, which].reshape(KT, P, P).transpose(1, 0, 2).reshape(P, D)

    def rows_of(w, half):
        part = w[:, 512 * half:512 * (half + 1)].reshape(-1, 2, P, 512)
        return list(part.transpose(0, 2, 1, 3).reshape(-1, P, D))

    blocks = [columns(w_in, which) for which in tiles]
    wb, wa = a["w_branch_b"][0], a["w_branch_a"][0][aq_rows]
    for w in (wb, wa):
        blocks += [columns(w, np.arange(P * m, P * (m + 1))) for m in range(KT)]
    for half in range(2):
        blocks += rows_of(a["w_out"][0], half)
    for f in range(FT):
        for start in (0, FFN):
            blocks.append(columns(a["w_ffn_in"][0], np.arange(start + P * f, start + P * (f + 1))))
    for half in range(2):
        blocks += rows_of(a["w_ffn_out"][0], half)
    wstream = np.stack(blocks)
    conv = a["conv_w"][0]
    conv_tiles = [conv[:, start + P * i:start + P * (i + 1)].T
                  for start in (GH * DK, 2 * GH * DK, 0) for i in range(GH)]
    sinks = a["attn_sinks"][0]
    sink_cols = [np.repeat(sinks[4 * (2 * pr + e) + 2 * ip:4 * (2 * pr + e) + 2 * ip + 2], P // 2)
                 for pr in range(2) for e in range(2) for ip in range(2)]
    cols = np.concatenate([np.stack([b_in[which] for which in tiles], 1), *conv_tiles,
                           a["gdn_norm_g"][0][:, None], np.stack(sink_cols, 1)], 1)
    rows = np.stack([a["ln_in_g"], a["ln_in_b"], a["b_out"][0], a["ln1_g"][0], a["ln1_b"][0],
                     a["ln2_g"][0], a["ln2_b"][0]])
    short = np.concatenate([b_in[gb:gb + GH], b_in[ga:ga + GH], a["a_log"][0], a["dt_bias"][0]])
    return {"x": a["x"][0], "meta": a["meta"], "wstream": wstream, "consts": constant_matrices(),
            "cols": cols, "rows": rows, "short": short}


def kernel(**inputs):
    import concourse.bacc as bacc
    from concourse.bass_utils import run_bass_kernel_spmd

    arrays = {k: np.ascontiguousarray(v) for k, v in lay_out({k: np.asarray(v) for k, v in inputs.items()}).items()}
    nc = bacc.Bacc("TRN2", target_bir_lowering=False, num_devices=1, dynamic_dma_scratch_size=1024)
    args = [nc.dram_tensor(f"in_{k}", v.shape, F32, kind="ExternalInput").ap() for k, v in arrays.items()]
    result = nc.dram_tensor("out_0", (SEQ, D), F32, kind="ExternalOutput").ap()
    build(nc, *args, result)
    r = run_bass_kernel_spmd(nc, [{f"in_{k}": v for k, v in arrays.items()}], core_ids=[0])
    return r.results[0]["out_0"].reshape(1, SEQ, D)
```

```python
from contextlib import ExitStack

import numpy as np

import concourse.bass as bass
from concourse import mybir

F32 = mybir.dt.float32
F32R = mybir.dt.float32r
ALU = mybir.AluOpType
ACT = mybir.ActivationFunctionType
AX_X = mybir.AxisListType.X

P = 128
D = 1024
KT = D // P
SEQ = 512
META = 16
NT = META + SEQ
HALF = NT // 2
TT = SEQ // P
ATT_CHUNK = 64
NAC = SEQ // ATT_CHUNK
WIN = 2 * ATT_CHUNK
A_HEADS, A_KV, DH = 16, 4, 64
GH, DK = 8, 128
CONV_K = 4
FFN = -(-8 * D // (3 * 256)) * 256
FT = FFN // P
ALPHA = 2.0 ** 0.25
PEELED = 4
TURN = 3
NORMS = TT + 1
LATE = 3
RING = 3

B_BA = 3 * GH
B_Z = B_BA + 1
B_SIDE = B_Z + GH
SIDE_AKV = 4
SIDE_AQ = SIDE_AKV + KT
SIDE = SIDE_AQ + 2 * KT
B_BB = B_SIDE + SIDE
B_BA2 = B_BB + KT
B_OUT = B_BA2 + KT
B_F1 = B_OUT + KT
B_F2 = B_F1 + 2 * FT
NBLOCKS = B_F2 + FT

C_IDENT, C_INCL, C_GT, C_ONES, C_LEVEL = 0, 1, 2, 3, 4
LEVELS = 7
NCONST = C_LEVEL + LEVELS

COL_BIAS = 0
NBIAS = B_BB
COL_CONV = NBIAS
COL_NORM = COL_CONV + 3 * GH * CONV_K
COL_SINK = COL_NORM + 1
NCOLS = COL_SINK + 8
R_LNIN, R_BOUT, R_LN1, R_LN2, NROWS = 0, 2, 3, 5, 7
S_BIAS, S_ALOG, S_DT, NSHORT = 0, 16, 24, 32
LN_EPS, NORM_EPS = 1e-5, 1e-6


def chunk_of(n):
    return (0, META) if n == 0 else (META + P * (n - 1), P)


INPUT_TILES = [0, 1, TT, *range(2, TT)]


def token_span(i):
    t = INPUT_TILES[i]
    return (0, META) if t == TT else (META + P * t, P)


def on_vector(i):
    return i == 1 or i == TT or i > TT + 1 and i != 2 * TT + 1


def levels_of(n):
    return META.bit_length() - 1 if n == 0 else LEVELS



def bank_uses():
    use, count = {}, [0] * 8

    def add(bank, *key):
        use[key] = (bank, count[bank])
        count[bank] += 1

    for i in range(TT + 1):
        add((4, 6, 2, 4, 6)[i], "hT", i)
    add(4, "logits")
    add(5, "decays")
    for stage, n, g in delta_order():
        add(4 + g + 2 * WHICH_BANK[stage[0]], stage, n, g)
    for j in range(4):
        add(4 + j, "values", j)
    for a in range(NUNITS):
        add(4 + a % 2, "scores", a)
        add(6 + a % 2, "turn", a)
        if a % 2:
            add(1 + 2 * (a // 2 % 2), "pv", a // 2)
    for t in range(TT):
        add(4 + t, "out", 0, t)
    for t in range(TT):
        add(t, "out", 1, t)
    for t in range(TT):
        add((4, 6, 0, 4)[t], "h1T", t)
    for half in range(2):
        for t in range(TT):
            add(t + 4 * (1 - half), "ffn", half, t)
    return use


def filled_before(use, key):
    bank, count = use[key]
    return count - sum(1 for k, (b, c) in use.items()
                       if b == bank and c < count and k[0] in ("out", "ffn") and k[2] == TT - 1)


WHICH_BANK = {"k": 0, "q": 1, "v": 0, "d": 1, "g": 0, "w": 1, "i": 0, "y": 1, "z": 0, "x": 0,
              "s": 0, "p": 1, "r": 0, "o": 1, "t": 0, "f": 1}


OUTPUTS_AFTER = "y2"


def delta_order():
    order = []
    for n in range(TT + 1):
        stages = ["k"] + ["q"] * (n > 0) + ["v", "d", "g"] + ["w"] * (n > 0) + ["i"]
        last = levels_of(n) - 1
        for level in range(1, last + 1):
            stages += [f"y{level}"] + [f"x{level - 1}"] * (level > 1) + [f"z{level}"]
        stages += ["s"] * (n > 0) + ["p"] + ["r", "o"] * (n > 0) + ["t"] * (n < TT)
        for stage in stages:
            order += [(stage, n, g) for g in range(2)]
            if stage == OUTPUTS_AFTER and n > 1:
                order += [("f", n - 1, g) for g in range(2)]
    return order + [("f", TT, g) for g in range(2)]


BEHIND = {("t", 1): 18, ("d", 1): 10, ("w", 1): 5, ("i", 0): 8, ("i", 1): 8}
TAIL_BLOCKS = 2
HEAD_BLOCKS = 4
ATT_LAG = 3


def plan():
    todo = [("block", b) for b in range(B_BA, B_SIDE)]
    todo.insert(B_Z - B_BA + 2, ("logits",))
    todo.insert(B_Z - B_BA + 6, ("decays",))
    side = [(b, k) for b in range(B_SIDE, B_BB) for k in range(KT)]

    def step(side, count):
        for _ in range(min(count, len(side))):
            b, k = side.pop(0)
            todo.append(("side", b, k))
            if k == KT - 1:
                todo.append(("sideend", b))

    order = delta_order()
    spread = len(side) - TAIL_BLOCKS * KT
    shares = np.cumsum([0] + [BEHIND.get((stage, g), 2) for stage, n, g in order])
    for m, (stage, n, g) in enumerate(order):
        if (stage, n, g) == ("f", TT, 0):
            step(side, len(side) - KT)
        todo.append(("delta", stage, n, g))
        step(side, int(spread * shares[m + 1] // shares[-1] - spread * shares[m] // shares[-1]))
    step(side, len(side))
    todo.append(("reload",))
    branch = [(b, k) for b in range(B_BB, B_BA2) for k in range(KT)]
    step(branch, HEAD_BLOCKS * KT)
    todo.append(("values",))
    for a in range(NUNITS + ATT_LAG + 1):
        todo.append(("att", a))
        step(branch, 1)
    step(branch, len(branch))
    return todo + [("block", b) for b in range(B_BA2, B_OUT)]


NUNITS = NAC * 4


def unit(a):
    return a // 4, a // 2 % 2, a % 2


def build(nc, x, meta, wstream, consts, cols, rows, short, out):
    with ExitStack() as ctx:
        place = {}

        def sb(name, shape, offset, dt=F32):
            place[name] = offset
            return nc.alloc_sbuf_tensor_at(name, shape, dt, offset=offset)

        class Region:

            def __init__(self, at, end):
                self.at, self.end = at, end

            def __call__(self, name, shape, dt=F32):
                t = sb(name, shape, self.at, dt)
                self.at += -(-4 * int(np.prod(shape[1:])) // 32) * 32
                assert self.at <= self.end, (name, self.at, self.end)
                return t

        def sem(name):
            return ctx.enter_context(nc.semaphore(name))

        KB = 1024
        BASE = 2 * KB
        keep = Region(BASE, BASE + 10 * KB)
        cst = keep("cst", [P, NCONST, P])
        col = keep("col", [P, NCOLS])
        halfcol = keep("halfcol", [P, NCOLS])
        srt = keep("srt", [P, NSHORT])
        half = keep("half", [P, GH])
        minus_half = keep("minus_half", [P, GH])
        st6 = keep("st6", [P, NORMS, 2, 6])
        mv = keep("mv", [P, NORMS, 2])
        var_eps = keep("var_eps", [P, NORMS])
        rstd = keep("rstd", [P, NORMS])
        logits = keep("logits", [P, TT + 1, 2 * GH])
        la = keep("la", [P, TT + 1, GH])
        beta = keep("beta", [P, TT + 1, GH])
        soft = keep("soft", [P, TT + 1, GH])
        rho = keep("rho", [P, 2, 4])
        rk2 = keep("rk2", [P, 2, 4])
        kss = keep("kss", [P, 2, 4])
        knorm = keep("knorm", [P, 2, 4])
        qss = keep("qss", [P, 2, 4])
        rq = keep("rq", [P, 2, 4])
        rq2 = keep("rq2", [P, 2, 4])
        oss = keep("oss", [P, 2, 4])
        onorm = keep("onorm", [P, 2, 4])
        neg_a = keep("neg_a", [P, GH])
        eg = keep("eg", [P, TT + 1, 3, GH])
        neg_eg = keep("neg_eg", [P, TT + 1, GH])
        amax = keep("amax", [P, 2, 2])
        neg_amax = keep("neg_amax", [P, 2, 2])
        sink_arg = keep("sink_arg", [P, 2, 2])
        sink_exp = keep("sink_exp", [P, 2, 2])
        asum = keep("asum", [P, 2, 2])
        atot = keep("atot", [P, 2, 2])
        arec = keep("arec", [P, 4, 2])
        minus_sinks = keep("minus_sinks", [P, 8])

        RINGS = BASE + 10 * KB
        ring = Region(RINGS, RINGS + 36 * KB)
        wst = ring("wst", [P, RING, D])
        whi = ring("whi", [P, RING, D], F32R)
        wlo = ring("wlo", [P, RING, D], F32R)
        H = RINGS + 36 * KB
        h = sb("h", [P, TT, D], H)
        HT = H + 16 * KB
        ht = Region(HT, HT + 33 * KB)
        hTh = ht("hTh", [P, KT, NT], F32R)
        hTl = ht("hTl", [P, KT, NT], F32R)
        h1h = sb("h1h", [P, KT, SEQ], HT, F32R)
        h1l = sb("h1l", [P, KT, SEQ], HT + 4 * KT * SEQ, F32R)
        G0, GEND = HT + 33 * KB, 224 * KB - 512

        at_norm = Region(G0, GEND)
        xin = at_norm("xin", [P, TT + 1, D])
        lnrow = at_norm("lnrow", [P, 2, D])
        hmeta = at_norm("hmeta", [META, D])

        at_delta = Region(G0, GEND)
        kvq = at_delta("kvq", [P, 3 * GH, NT])
        kr, vr, qr = (kvq[:, GH * i:GH * (i + 1), :] for i in range(3))
        yh = sb("yh", [P, GH, NT], G0, F32R)
        yl = sb("yl", [P, GH, NT], G0 + 4 * GH * NT, F32R)
        sz = at_delta("sz", [P, GH, SEQ])
        side = at_delta("side", [P, 3, NT])
        work = at_delta.at
        at_conv = Region(work, GEND)
        cbuf = at_conv("cbuf", [P, 2, NT + CONV_K - 1])
        cacc = at_conv("cacc", [P, 2, NT])
        ba_cols = at_conv("ba_cols", [16, NT])
        at_work = Region(work, GEND)
        tri_la = at_work("tri_la", [P, 2, 4, P])
        dec = at_work("dec", [P, 2, 4, P])
        U = at_work("U", [P, 2, 4, P])
        UL = [at_work(f"UL{i}", [P, 2, 4, P]) for i in range(2)]
        AT = at_work("AT", [P, 2, 4, P])
        XT = at_work("XT", [P, 2, 4, P])
        X = at_work("X", [P, 2, 4, P])
        Y = at_work("Y", [P, 2, 4, P])
        ktok = at_work("ktok", [P, 2, 4, P])
        vtok = at_work("vtok", [P, 2, 4, P])
        oraw = at_work("oraw", [P, 2, 4, P])
        state = at_work("state", [P, GH, P])
        vnew, vdec, osq = U, UL[0], Y
        ksq, qsq = Y, X
        youT = dec

        at_att = Region(G0 + 2 * 4 * GH * NT, GEND)
        merged = at_att("merged", [P, KT, SEQ])
        gate = at_att("gate", [P, 2, SEQ])
        yah = at_att("yah", [P, KT, SEQ], F32R)
        yal = at_att("yal", [P, KT, SEQ], F32R)
        kwin = at_att("kwin", [P, 2, NAC, META + WIN])
        vwin = at_att("vwin", [P, NAC - 1, 2, P])
        vmeta = at_att("vmeta", [META, 2, P])
        aqT = at_att("aqT", [P, NAC, KT, ATT_CHUNK])
        prob = at_att("prob", [P, 4, 2, META + WIN])
        pT = at_att("pT", [P, 2, 2, P])
        pTm = at_att("pTm", [META, 2, 2, P])
        avT = sb("avT", [P, 2, NT], place["yah"])
        prod = sb("prod", [P, 2, SEQ], place["aqT"])

        mgh = sb("mgh", [P, KT, SEQ], G0, F32R)
        mgl = sb("mgl", [P, KT, SEQ], G0 + 4 * GH * NT, F32R)
        orow = sb("orow", [P, 3, D], place["kwin"])
        at_ffn = Region(G0, GEND)
        hidh = at_ffn("hidh", [P, FT, SEQ], F32R)
        hidl = at_ffn("hidl", [P, FT, SEQ], F32R)
        sgate = at_ffn("sgate", [P, TURN, SEQ])
        hid = at_ffn("hid", [P, TURN, SEQ])
        frow = at_ffn("frow", [P, 2, D])
        res = sb("res", [P, TT, D], HT)

        ps = ctx.enter_context(nc.psum_tensor("ps", [P, 8, 512], F32))
        k_windows = nc.dram_tensor("k_windows", (P, 2, NAC, META + WIN), F32).ap()
        v_rows = nc.dram_tensor("v_rows", (P, 2, NT), F32).ap()
        q_rows = nc.dram_tensor("q_rows", (P, NAC, KT, ATT_CHUNK), F32).ap()
        gates = nc.dram_tensor("gates", (2 * KT, P, SEQ), F32).ap()

        x_landed = [sem(f"x_landed{i}") for i in range(TT + 1)]
        rows_landed = sem("rows_landed")
        ident_landed = sem("ident_landed")
        const_landed = sem("const_landed")
        w_landed = [sem(f"w_landed{i}") for i in range(RING)]
        w_hi = sem("w_hi")
        w_lo = sem("w_lo")
        w_used = sem("w_used")
        freed = [sem(f"freed{i}") for i in range(2)]
        filled = [sem(f"filled{i}") for i in range(8)]
        taken = [sem(f"taken{i}") for i in range(8)]
        dve_step = sem("dve_step")
        act_step = sem("act_step")
        powers_ready = sem("powers_ready")
        var_ready = sem("var_ready")
        rstd_ready = sem("rstd_ready")
        gained = sem("gained")
        scaled = sem("scaled")
        normed_by_pool = sem("normed_by_pool")
        normed_by_vector = sem("normed_by_vector")
        hT_hi = sem("hT_hi")
        conv_step = sem("conv_step")
        conv_done = sem("conv_done")
        silu_done = sem("silu_done")
        prep = sem("prep")
        prep_act = sem("prep_act")
        tri_ready = sem("tri_ready")
        kss_ready = [sem(f"kss_ready{g}") for g in range(2)]
        knorm_ready = [sem(f"knorm_ready{g}") for g in range(2)]
        qss_ready = [sem(f"qss_ready{g}") for g in range(2)]
        rq_ready = [sem(f"rq_ready{g}") for g in range(2)]
        level_ready = [sem(f"level_ready{g}") for g in range(2)]
        xt_ready = [sem(f"xt_ready{g}") for g in range(2)]
        r_ready = [sem(f"r_ready{g}") for g in range(2)]
        vdec_ready = [sem(f"vdec_ready{g}") for g in range(2)]
        oss_ready = [sem(f"oss_ready{g}") for g in range(2)]
        onorm_ready = [sem(f"onorm_ready{g}") for g in range(2)]
        o_ready = [sem(f"o_ready{g}") for g in range(2)]
        yh_ready = [sem(f"yh_ready{g}") for g in range(2)]
        yl_ready = [sem(f"yl_ready{g}") for g in range(2)]
        side_ready = sem("side_ready")
        side_stored = [sem(f"side_stored{i}") for i in range(3)]
        av_loaded = sem("av_loaded")
        kq_loaded = sem("kq_loaded")
        gate_loaded = [sem(f"gate_loaded{i}") for i in range(2)]
        max_ready = sem("max_ready")
        sink_ready = sem("sink_ready")
        arec_ready = sem("arec_ready")
        prob_ready = sem("prob_ready")
        ya_hi = sem("ya_hi")
        merged_ready = sem("merged_ready")
        mg_hi = sem("mg_hi")
        mg_lo = sem("mg_lo")
        hid_hi = sem("hid_hi")
        hid_lo = sem("hid_lo")
        out_stored = sem("out_stored")

        steps = plan()
        use = bank_uses()

        def levels_before(n):
            return sum(levels_of(m) for m in range(n))

        def later(value, turn, per_turn):
            return value if turn is None else turn * per_turn + value

        def gdn_tiles(eng, tile):
            assert (3 * GH) % (2 * TURN) == 0 and 2 * TURN % 2 == 0
            for b in range(2 * TURN):
                tile(b, None)
            with eng.Fori(0, 3 * GH // (2 * TURN) - 1) as turn:
                for b in range(2 * TURN, 4 * TURN):
                    tile(b, turn)

        def hidden_tiles(eng, tile):
            assert 2 * TURN % RING == 0 and (FT - PEELED) % TURN == 0
            for f in range(PEELED):
                tile(f, None)
            with eng.Fori(0, (FT - PEELED) // TURN) as turn:
                for f in range(PEELED, PEELED + TURN):
                    tile(f, turn)

        def last_splits(eng, split):
            first = B_F2 + RING
            turns = (NBLOCKS - first) // RING
            with eng.Fori(0, turns) as turn:
                for b in range(first, first + RING):
                    split(b, turn, RING)
            for b in range(first + turns * RING, NBLOCKS):
                split(b)

        def tile_index(b):
            return b if b < B_OUT else b - KT

        def slot_of(b):
            return tile_index(b) % 2, tile_index(b) // 2

        def wait_free(eng, *key):
            bank, before = use[key]
            if before:
                eng.wait_ge(taken[bank], before)

        def wait_filled(eng, *key):
            eng.wait_ge(filled[use[key][0]], filled_before(use, key) + 1)

        def wait_taken(eng, *key):
            bank, before = use[key]
            eng.wait_ge(taken[bank], before + 1)

        def heads(t, g, c, w):
            return t[:c, g, :, :w]

        def bank4(key, c, w):
            return ps[:c, use[key][0], :].rearrange("p (h t) -> p h t", h=4)[:, :, :w]

        def even(t, level):
            return t.rearrange("p (b two s) -> p b two s", two=2, s=1 << level)[:, :, 0]

        def over_heads(i, c):
            return cst[:c, i, :c].unsqueeze(1).to_broadcast([c, 4, c])

        def per_head(t, c, w):
            return t.unsqueeze(2).to_broadcast([c, 4, w])

        def norm_tile(i):
            if i <= TT:
                t = INPUT_TILES[i]
                if t == TT:
                    return xin[:META, i, :], hmeta[:, :], META, lnrow
                return xin[:, i, :], h[:, t, :], P, lnrow
            if i <= 2 * TT:
                t = i - TT - 1
                return h[:, t, :], h[:, t, :], P, orow[:, 1:3, :]
            t = i - 2 * TT - 1
            return res[:, t, :], res[:, t, :], P, frow

        def normed_before(i):
            return sum(on_vector(m) == on_vector(i) for m in range(i))

        def wait_normed(eng, i):
            eng.wait_ge(normed_by_vector if on_vector(i) else normed_by_pool, normed_before(i) + 1)

        def stored_before(j):
            return sum(16 * (4 if i < 2 else 1) for i in range(j % 3, min(j, SIDE), 3))

        def window_of(c):
            return META + ATT_CHUNK * max(c - 1, 0), ATT_CHUNK if c == 0 else WIN

        def pair_view(bank):
            return ps[:, bank:bank + 2, :].rearrange("p b (k t) -> p (b k) t", t=P)

        block = ctx.enter_context(nc.Block())

        @block.sync
        def _(sp):
            def load_x(i):
                t = INPUT_TILES[i]
                src = x[P * t:P * (t + 1), :] if t < TT else meta
                sp.dma_start(xin[:src.shape[0], i, :], src).then_inc(x_landed[i], 16)

            for i in range(3):
                load_x(i)
            for j in range(2):
                sp.dma_start(lnrow[:, j, :], rows[R_LNIN + j].partition_broadcast(P)).then_inc(rows_landed, 16)
            sp.dma_start(cst[:, C_IDENT, :], consts[:, C_IDENT, :]).then_inc(ident_landed, 16)
            load_x(3)
            sp.dma_start(wst[:, 0, :], wstream[0]).then_inc(w_landed[0], 16)
            load_x(4)
            for b in range(1, RING):
                sp.dma_start(wst[:, b, :], wstream[b]).then_inc(w_landed[b], 16)
            sp.dma_start(col[:], cols).then_inc(const_landed, 16)
            sp.dma_start(srt[:], short.partition_broadcast(P)).then_inc(const_landed, 16)
            sp.dma_start(cst[:, C_INCL:, :], consts[:, C_INCL:, :]).then_inc(const_landed, 16)
            with sp.Fori(0, (NBLOCKS - RING) // RING) as turn:
                for j in range(RING):
                    sp.wait_ge(w_lo, turn * RING + (j + 1))
                    sp.dma_start(wst[:, j, :], wstream[turn * RING + (RING + j)]).then_inc(w_landed[j], 16)
            for b in range(NBLOCKS - NBLOCKS % RING, NBLOCKS):
                sp.wait_ge(w_lo, b - RING + 1)
                sp.dma_start(wst[:, b % RING, :], wstream[b]).then_inc(w_landed[b % RING], 16)
            for t in range(TT):
                wait_normed(sp, 2 * TT + 1 + t)
                sp.dma_start(out[P * t:P * (t + 1), :], res[:, t, :]).then_inc(out_stored, 16)
            sp.wait_ge(out_stored, 16 * TT)

        @block.tensor
        def _(pe):
            ident = cst[:, C_IDENT, :]

            def tile_step(b, k, inh, inl, first, turn=None):
                slot, before = slot_of(b)
                if k == 0:
                    pe.wait_ge(w_lo, later(b + 1, turn, 2 * TURN))
                    if before:
                        pe.wait_ge(freed[slot], later(before, turn, TURN))
                width = inh.shape[2] - first
                parts = [(0, width)] if width <= 512 else [(0, HALF), (HALF, HALF)]
                s = slice(k * P, (k + 1) * P)
                for m, (w, v) in enumerate(((whi, inh), (whi, inl), (wlo, inh))):
                    for j, (at, n) in enumerate(parts):
                        mm = nc.tensor.matmul(ps[:, 2 * slot + j, 0:n], w[:, b % RING, s],
                                              v[:, k, first + at:first + at + n],
                                              start=(k == 0 and m == 0), stop=(k == KT - 1 and m == 2))
                if k == KT - 1:
                    mm.then_inc(w_used, 1)

            def tile_part(b, part, ks, inh, inl, n, bank, col0):
                slot, before = slot_of(b)
                if part == 0 and ks[0] == 0:
                    pe.wait_ge(w_lo, b + 1)
                    if before:
                        pe.wait_ge(freed[slot], before)
                for k in ks:
                    for m, (w, v) in enumerate(((whi, inh), (whi, inl), (wlo, inh))):
                        mm = nc.tensor.matmul(ps[:, bank, col0:col0 + n], w[:, b % RING, k * P:(k + 1) * P],
                                              v[:, k, n * part:n * (part + 1)], start=(k == 0 and m == 0 and col0 == 0),
                                              stop=(k == KT - 1 and m == 2), skip_group_check=True)
                if part == 1 and ks[-1] == KT - 1:
                    mm.then_inc(w_used, 1)

            def projection_step(b, k):
                narrow = b > B_BA and not B_SIDE <= b < B_SIDE + SIDE_AKV
                tile_step(b, k, hTh, hTl, META if narrow else 0)

            def branch_step(b, k):
                if b == B_BB and k == 0:
                    for g in range(2):
                        pe.wait_ge(yl_ready[g], TT)
                if b == B_BA2 and k == 0:
                    wait_taken(pe, "pv", NUNITS // 2 - 1)
                    wait_taken(pe, "pv", NUNITS // 2 - 2)
                if b < B_BA2:
                    tile_step(b, k, yh, yl, META)
                else:
                    tile_step(b, k, yah, yal, 0)

            def turn_tile(i, key, src, c):
                wait_normed(pe, i)
                wait_free(pe, *key)
                bank = use[key][0]
                for k in range(KT):
                    mm = nc.tensor.transpose(ps[:, bank + k // 4, (k % 4) * P:(k % 4) * P + c],
                                             src[:, k * P:(k + 1) * P], ident[:c, :c])
                mm.then_inc(filled[bank], 1)

            def turn_logits():
                slot, before = slot_of(B_BA)
                pe.wait_ge(freed[slot], before + 1)
                for n in range(TT + 1):
                    t0 = chunk_of(n)[0]
                    mm = nc.tensor.transpose(ps[:, 4, n * 16:n * 16 + 16], ba_cols[:, t0:t0 + P], ident[:16, :16])
                mm.then_inc(filled[4], 1)

            def decays():
                pe.wait_ge(const_landed, 3 * 16)
                pe.wait_ge(prep, 4)
                for n in range(TT + 1):
                    c = chunk_of(n)[1]
                    for m, mat in enumerate((C_INCL, C_GT, C_ONES)):
                        at = (3 * n + m) * GH
                        mm = nc.tensor.matmul(ps[:, 5, at:at + GH], cst[:c, mat, :], la[:c, n, :],
                                              start=(n == 0 and m == 0), stop=(n == TT and m == 2),
                                              skip_group_check=True)
                mm.then_inc(filled[5], 1)

            def delta(stage, n, g):
                t0, c = chunk_of(n)
                key = (stage, n, g)
                bank = use[key][0]
                last = levels_of(n) - 1
                if key == ("k", 0, 0):
                    pe.wait_ge(silu_done, 3 * GH)
                wait_free(pe, *key)
                toks = slice(t0, t0 + c)
                kind, level = stage[0], int(stage[1:] or 0)
                if kind == "d":
                    pe.wait_ge(tri_ready, 2 * n + g + 1)
                    nc.tensor.matmul(bank4(key, c, c), cst[:c, C_GT, :c], heads(tri_la, g, c, c),
                                     start=True, stop=True).then_inc(filled[bank], 1)
                    return
                if kind == "i":
                    pe.wait_ge(xt_ready[g], n + 1)
                elif kind == "y":
                    pe.wait_ge(level_ready[g], levels_before(n) + level + 1)
                    wait_taken(pe, "i" if level == 1 else f"z{level - 1}", n, g)
                elif kind == "z":
                    wait_taken(pe, f"y{level}", n, g)
                    if level > 1:
                        wait_taken(pe, f"x{level - 1}", n, g)
                elif kind == "x":
                    wait_taken(pe, f"z{level}", n, g)
                elif kind == "s" or kind == "r":
                    wait_taken(pe, "t", n - 1, g)
                elif kind == "p":
                    wait_taken(pe, f"z{last}", n, g)
                    if n:
                        pe.wait_ge(r_ready[g], n)
                    else:
                        wait_taken(pe, "v", n, g)
                elif kind == "o":
                    wait_taken(pe, "p", n, g)
                    wait_taken(pe, "w", n, g)
                elif kind == "t":
                    pe.wait_ge(vdec_ready[g], n + 1)
                    wait_taken(pe, "k", n, g)
                elif kind == "f":
                    pe.wait_ge(o_ready[g], n)
                for j in range(4):
                    head = 4 * g + j
                    wide = ps[:c, bank, j * P:(j + 1) * P]
                    square = ps[:c, bank, j * P:j * P + c]
                    h2 = c // 2
                    left = square[:, 0:h2]
                    half_rows = slice(h2 if c == P else 0, c)
                    full = ps[:, bank, j * P:(j + 1) * P]
                    if kind in "kqv":
                        mm = nc.tensor.transpose(wide, {"k": kr, "q": qr, "v": vr}[kind][:, head, toks], ident)
                    elif kind in "ix":
                        src = (XT if kind == "i" else X)[:c, g, j, :c]
                        mm = nc.tensor.transpose(square, src, ident[:c, :c])
                    elif kind == "f":
                        mm = nc.tensor.transpose(full, oraw[:, g, j, :], ident)
                    else:
                        dst, lhs, rhs = {
                            "g": (square, kr[:, head, toks], kr[:, head, toks]),
                            "w": (square, kr[:, head, toks], qr[:, head, toks]),
                            "y": (left, UL[level % 2][:c, g, j, :c], even(X[:c, g, j, :c], level))
                                 if level < LEVELS - 1 else
                                 (left[h2:c], UL[level % 2][:h2, g, j, h2:c], X[:h2, g, j, :h2]),
                            "z": (left, XT[:c, g, j, :c], Y[:c, g, j, :h2]) if level < last else
                                 (left[:h2], Y[half_rows, g, j, :h2], XT[half_rows, g, j, h2:c]),
                            "s": (wide, kr[:, head, toks], state[:, head, :]),
                            "p": (wide, XT[:c, g, j, :c], vtok[:c, g, j, :]),
                            "r": (wide, qr[:, head, toks], state[:, head, :]),
                            "o": (wide, AT[:c, g, j, :c], vnew[:c, g, j, :]),
                            "t": (full, ktok[:c, g, j, :], vdec[:c, g, j, :]),
                        }[kind]
                        mm = nc.tensor.matmul(dst, lhs, rhs, start=True, stop=True)
                mm.then_inc(filled[bank], 1)

            def values():
                pe.wait_ge(av_loaded, 16)
                for j in range(4):
                    wait_free(pe, "values", j)
                    for m in range(4):
                        pr, w = divmod(4 * j + m, NAC)
                        rows_ = META if w == NAC - 1 else WIN
                        t0 = 0 if w == NAC - 1 else META + ATT_CHUNK * w
                        mm = nc.tensor.transpose(ps[:rows_, 4 + j, m * P:(m + 1) * P],
                                                 avT[:, pr, t0:t0 + rows_], ident)
                    mm.then_inc(filled[4 + j], 1)

            def scores(a):
                c, pr, e = unit(a)
                w = window_of(c)[1]
                if a == 0:
                    pe.wait_ge(kq_loaded, (1 + NAC // 2) * 16)
                wait_free(pe, "scores", a)
                part = slice(DH * e, DH * (e + 1))
                for ip in range(2):
                    q = aqT[part, c, 4 * pr + 2 * ip:4 * pr + 2 * ip + 2, :].rearrange("p i t -> p (i t)")
                    at = ip * (META + WIN)
                    bank = 4 + a % 2
                    mm = nc.tensor.matmul(ps[:, bank, at:at + META + w], q, kwin[part, pr, c, 0:META + w],
                                          start=(ip == 0), stop=(ip == 1), skip_group_check=True)
                mm.then_inc(filled[bank], 1)

            def turn_probs(a):
                w = window_of(unit(a)[0])[1]
                wait_free(pe, "turn", a)
                pe.wait_ge(prob_ready, a + 1)
                bank, s = 6 + a % 2, a % 4
                for ip in range(2):
                    nc.tensor.transpose(ps[:w, bank, ip * P:(ip + 1) * P], prob[:, s, ip, META:META + w], ident)
                    mm = nc.tensor.transpose(ps[:META, bank, (2 + ip) * P:(3 + ip) * P], prob[:, s, ip, 0:META], ident)
                mm.then_inc(filled[bank], 1)

            def weighted_values(a):
                c, pr, e = unit(a)
                w = window_of(c)[1]
                key = ("pv", a // 2)
                bank = use[key][0]
                if e == 0:
                    wait_free(pe, *key)
                wait_taken(pe, "turn", a)
                dst = ps[DH * e:DH * (e + 1), bank, 0:2 * P]
                part = slice(DH * e, DH * (e + 1))
                nc.tensor.matmul(dst, vwin[:w, max(c - 1, 0), pr, part],
                                 pT[:w, a % 2].rearrange("p i t -> p (i t)"), start=True, stop=False)
                mm = nc.tensor.matmul(dst, vmeta[:, pr, part], pTm[:, a % 2].rearrange("p i t -> p (i t)"),
                                      start=False, stop=True)
                if e:
                    mm.then_inc(filled[bank], 1)

            def output_blocks(first, name, half, blocks, acth, actl, act_ready):
                early = blocks - (LATE if half else 0)
                order = [(kb, t) for kb in range(early) for t in range(TT)]
                order += [(kb, t) for t in range(TT) for kb in range(early, blocks)]
                for kb, t in order:
                    b = first + blocks * half + kb
                    if t == 0:
                        pe.wait_ge(w_lo, b + 1)
                        if half == 0:
                            pe.wait_ge(act_ready, 2 * kb + 2)
                    bank = use[(name, half, t)][0]
                    if kb == 0:
                        wait_free(pe, name, half, t)
                    toks = slice(P * t, P * (t + 1))
                    for kk in range(2):
                        k = 2 * kb + kk
                        for m, (v, w) in enumerate(((acth, whi), (actl, whi), (acth, wlo))):
                            mm = nc.tensor.matmul(ps[:, bank, :], v[:, k, toks],
                                                  w[:, b % RING, 512 * kk:512 * (kk + 1)],
                                                  start=(k == 0 and m == 0),
                                                  stop=(k == 2 * blocks - 1 and m == 2))
                    if t == TT - 1:
                        mm.then_inc(w_used, 1)
                    elif kb == blocks - 1:
                        mm.then_inc(filled[bank], 1)

            pe.wait_ge(ident_landed, 16)
            def turn_input(i):
                _, src, c, _ = norm_tile(i)
                turn_tile(i, ("hT", i), src, c)

            def first_part(b, part, ks):
                tile_part(b, part, ks, hTh, hTl, HALF, 2 * b + part, 0)

            for i in range(3):
                turn_input(i)
            for i in range(3):
                wait_taken(pe, "hT", i)
            first_part(0, 0, range(KT))
            turn_input(3)
            first_part(1, 0, range(KT // 2))
            turn_input(4)
            first_part(1, 0, range(KT // 2, KT))
            for i in (3, 4):
                wait_taken(pe, "hT", i)
            for b in range(2):
                first_part(b, 1, range(KT))

            def gdn_product(b, turn):
                if b > 1:
                    for k in range(KT):
                        tile_step(b, k, hTh, hTl, 0, turn)

            gdn_tiles(pe, gdn_product)
            for what, *at in steps:
                if what == "block":
                    for k in range(KT):
                        (projection_step if at[0] < B_BB else branch_step)(at[0], k)
                elif what == "side":
                    (projection_step if at[0] < B_BB else branch_step)(*at)
                elif what == "logits":
                    turn_logits()
                elif what == "decays":
                    decays()
                elif what == "delta":
                    delta(*at)
                elif what == "values":
                    values()
                elif what == "att":
                    a = at[0]
                    if a < NUNITS:
                        scores(a)
                    if 0 <= a - ATT_LAG < NUNITS:
                        turn_probs(a - ATT_LAG)
                    if 0 <= a - ATT_LAG - 1 < NUNITS:
                        weighted_values(a - ATT_LAG - 1)
            output_blocks(B_OUT, "out", 0, KT // 2, mgh, mgl, mg_lo)
            for s in range(2):
                pe.wait_ge(freed[s], slot_of(B_OUT + KT + s)[1] if slot_of(B_OUT + KT + s)[0] == s
                           else slot_of(B_OUT + KT + 1 - s)[1])
            output_blocks(B_OUT, "out", 1, KT // 2, mgh, mgl, mg_lo)
            def turn_h1(t):
                turn_tile(TT + 1 + t, ("h1T", t), h[:, t, :], P)

            def ffn_part(b, part, ks):
                tile_part(b, part, ks, h1h, h1l, 2 * P, 2 * slot_of(b)[0], 2 * P * part)

            for t in range(3):
                turn_h1(t)
            for t in range(2):
                wait_taken(pe, "h1T", t)
            ffn_part(B_F1, 0, range(KT))
            wait_taken(pe, "h1T", 2)
            ffn_part(B_F1 + 1, 0, range(KT // 2))
            turn_h1(3)
            ffn_part(B_F1 + 1, 0, range(KT // 2, KT))
            wait_taken(pe, "h1T", 3)
            for b in range(B_F1, B_F1 + 2):
                ffn_part(b, 1, range(KT))
            def gate_and_up(f, turn):
                for b in (B_F1 + 2 * f, B_F1 + 2 * f + 1):
                    if f:
                        for k in range(KT):
                            tile_step(b, k, h1h, h1l, 0, turn)

            hidden_tiles(pe, gate_and_up)
            output_blocks(B_F2, "ffn", 0, FT // 2, hidh, hidl, hid_lo)
            for s in range(2):
                pe.wait_ge(freed[s], sum(tile_index(b) % 2 == s for b in [*range(B_OUT), *range(B_F1, B_F2)]))
            output_blocks(B_F2, "ffn", 1, FT // 2, hidh, hidl, hid_lo)

        @block.scalar
        def _(act):
            own = [0]

            def step(ins):
                own[0] += 1
                ins.then_inc(act_step, 1)
                act.wait_ge(act_step, own[0])

            def split_hi(b, turn=None, blocks=2 * TURN):
                if b >= NBLOCKS:
                    return
                act.wait_ge(w_landed[b % RING], later(16 * (b // RING + 1), turn, 16 * (blocks // RING)))
                if b >= RING:
                    act.wait_ge(w_used, later(b - RING + 1, turn, blocks))
                nc.scalar.activation(whi[:, b % RING, :], wst[:, b % RING, :], ACT.Copy).then_inc(w_hi, 1)

            def scale_tile(i):
                _, dst, c, _ = norm_tile(i)
                act.wait_ge(gained, i + 1)
                act.wait_ge(rstd_ready, i + 1)
                m = i % NORMS
                nc.scalar.activation(dst, dst, ACT.Identity, scale=rstd[:c, m:m + 1]).then_inc(scaled, 1)

            def hi_of_tile(key, dst, at, c):
                wait_filled(act, *key)
                src = pair_view(use[key][0])[:, :, :c]
                nc.scalar.activation(dst[:, :, at:at + c], src, ACT.Copy).then_inc(hT_hi, 1)

            def projection(b, turn=None):
                slot, before = slot_of(b)
                act.wait_ge(w_used, later(b + 1, turn, 2 * TURN))
                wide = ps[:, 2 * slot:2 * slot + 2, 0:HALF]
                narrow = ps[:, 2 * slot, :]
                at = later(COL_BIAS + b, turn, 2 * TURN)
                bias = col[:, bass.ds(at, 1)]
                if b < B_BA:
                    if b >= 2:
                        act.wait_ge(conv_done, later(b - 1, turn, 2 * TURN))
                    dst = cbuf[:, b % 2, CONV_K - 1:].rearrange("p (j t) -> p j t", j=2)
                    nc.scalar.activation(dst, wide, ACT.Identity, bias=bias).then_inc(freed[slot], 1)
                elif b == B_BA:
                    dst = ba_cols[:, :].rearrange("p (j t) -> p j t", j=2)
                    nc.scalar.activation(dst, wide[:16], ACT.Copy).then_inc(freed[slot], 1)
                else:
                    nc.scalar.activation(sz[:, b - B_Z, :], narrow, ACT.Silu, bias=bias).then_inc(freed[slot], 1)

            def silu_of_conv(b, turn=None):
                act.wait_ge(conv_done, later(b + 1, turn, 2 * TURN))
                nc.scalar.activation(kvq[:, later(b, turn, 2 * TURN), :], cacc[:, b % 2, :],
                                     ACT.Silu).then_inc(silu_done, 1)

            def gdn_tile(b, turn):
                projection(b, turn)
                split_hi(b + RING, turn)
                if b:
                    silu_of_conv(b - 1, turn)

            def log_decay_terms():
                act.wait_ge(prep, 2)
                step(nc.scalar.activation(soft[:], soft[:], ACT.Exp, scale=-1.0))
                step(nc.scalar.activation(soft[:], soft[:], ACT.Ln, bias=1.0))
                step(nc.scalar.activation(neg_a[:], srt[:, S_ALOG:S_ALOG + GH], ACT.Exp))
                nc.scalar.activation(beta[:], logits[:, :, 0:GH], ACT.Tanh, scale=0.5).then_inc(prep_act, 1)

            def decays():
                wait_filled(act, "decays")
                src = ps[:, 5, 0:3 * GH * (TT + 1)].rearrange("p (n m h) -> p n m h", m=3, h=GH)
                nc.scalar.activation(eg[:], src, ACT.Exp).then_inc(taken[5], 1)

            def delta(stage, n, g):
                c = chunk_of(n)[1]
                key = (stage, n, g)
                bank = use[key][0]
                kind = stage[0]
                if kind == "k":
                    wait_filled(act, *key)
                    nc.scalar.activation(heads(ktok, g, c, P), bank4(key, c, P), ACT.Copy)
                    if n > 1:
                        act.wait_ge(oss_ready[g], n - 1)
                    nc.scalar.activation(heads(ksq, g, c, P), bank4(key, c, P), ACT.Square).then_inc(taken[bank], 1)
                elif kind == "q":
                    wait_filled(act, *key)
                    nc.scalar.activation(heads(qsq, g, c, P), bank4(key, c, P), ACT.Square).then_inc(taken[bank], 1)
                elif kind == "d":
                    wait_filled(act, *key)
                    if n > 2:
                        act.wait_ge(yl_ready[g], n - 2)
                    nc.scalar.activation(heads(dec, g, c, c), bank4(key, c, c), ACT.Exp).then_inc(taken[bank], 1)
                elif kind in "ixy":
                    wait_filled(act, *key)
                    dst = {"i": X, "x": XT, "y": Y}[kind]
                    w = c // 2 if kind == "y" else c
                    r = slice(c // 2 if stage == f"y{LEVELS - 1}" else 0, c)
                    nc.scalar.activation(heads(dst, g, c, w)[r], bank4(key, c, w)[r], ACT.Copy).then_inc(taken[bank], 1)
                elif kind == "f":
                    wait_taken(act, *key)
                    t0 = chunk_of(n)[0]
                    nc.scalar.activation(yh[:, 4 * g:4 * g + 4, t0:t0 + P], youT[:, g], ACT.Copy).then_inc(yh_ready[g], 1)

            def store_side(j):
                if j < SIDE_AQ:
                    slot, before = slot_of(B_SIDE + j)
                    act.wait_ge(freed[slot], before + 1)
                else:
                    act.wait_ge(side_ready, j - SIDE_AQ + 1)
                src, stored = side[:, j % 3, :], side_stored[j % 3]
                frames = src[:, META:]
                if j < 2:
                    behind = frames[:, 0:SEQ - ATT_CHUNK].rearrange("p (c t) -> p c t", t=ATT_CHUNK)
                    own_chunk = frames[:, ATT_CHUNK:].rearrange("p (c t) -> p c t", t=ATT_CHUNK)
                    to = k_windows[:, j]
                    act.dma_start(to[:, :, 0:META],
                                  src[:, 0:META].unsqueeze(1).to_broadcast([P, NAC, META])).then_inc(stored, 16)
                    act.dma_start(to[:, 0, META:], frames[:, 0:WIN]).then_inc(stored, 16)
                    act.dma_start(to[:, 1:, META:META + ATT_CHUNK], behind).then_inc(stored, 16)
                    act.dma_start(to[:, 1:, META + ATT_CHUNK:], own_chunk).then_inc(stored, 16)
                elif j < SIDE_AKV:
                    act.dma_start(v_rows[:, j - 2, :], src).then_inc(stored, 16)
                elif j < SIDE_AQ:
                    chunks = src[:, 0:SEQ].rearrange("p (c t) -> p c t", t=ATT_CHUNK)
                    act.dma_start(q_rows[:, :, j - SIDE_AKV, :], chunks).then_inc(stored, 16)
                else:
                    act.dma_start(gates[j - SIDE_AQ], src[:, 0:SEQ]).then_inc(stored, 16)

            def side_tile(b):
                j = b - B_SIDE
                slot, before = slot_of(b)
                act.wait_ge(w_used, b + 1)
                if j >= 3:
                    act.wait_ge(side_stored[j % 3], stored_before(j))
                if j < SIDE_AKV:
                    dst = side[:, j % 3, :].rearrange("p (j t) -> p j t", j=2)
                    ins = nc.scalar.activation(dst, ps[:, 2 * slot:2 * slot + 2, 0:HALF], ACT.Identity,
                                               bias=col[:, COL_BIAS + b:COL_BIAS + b + 1])
                elif j < SIDE_AQ:
                    ins = nc.scalar.activation(side[:, j % 3, 0:SEQ], ps[:, 2 * slot, :], ACT.Identity,
                                               bias=col[:, COL_BIAS + b:COL_BIAS + b + 1])
                else:
                    ins = nc.scalar.activation(side[:, j % 3, 0:SEQ], ps[:, 2 * slot, :], ACT.Tanh, scale=0.5,
                                               bias=halfcol[:, COL_BIAS + b:COL_BIAS + b + 1])
                ins.then_inc(freed[slot], 1)
                if j:
                    store_side(j - 1)

            def load_gate(m):
                act.dma_start(gate[:, m % 2, :], gates[m]).then_inc(gate_loaded[m % 2], 16)

            def reload():
                store_side(SIDE - 1)
                for j in range(SIDE, SIDE + 3):
                    act.wait_ge(side_stored[j % 3], stored_before(j))
                for g in range(2):
                    act.wait_ge(yl_ready[g], TT)
                act.dma_start(avT[:], v_rows).then_inc(av_loaded, 16)
                load_gate(0)
                act.dma_start(kwin[:], k_windows).then_inc(kq_loaded, 16)
                for c in range(0, NAC, 2):
                    act.dma_start(aqT[:, c:c + 2], q_rows[:, c:c + 2]).then_inc(kq_loaded, 16)
                    if c == 0:
                        load_gate(1)

            def values():
                for j in range(4):
                    wait_filled(act, "values", j)
                    pr, w0 = divmod(4 * j, NAC)
                    n = 3 if w0 else 4
                    src = ps[:, 4 + j, 0:n * P].rearrange("p (w t) -> p w t", w=n)
                    ins = nc.scalar.activation(vwin[:, w0:w0 + n, pr, :], src, ACT.Copy)
                    if w0:
                        ins = nc.scalar.activation(vmeta[:, pr, :], ps[:META, 4 + j, 3 * P:4 * P], ACT.Copy)
                    ins.then_inc(taken[4 + j], 1)

            def attention(a):
                b = a - ATT_LAG
                if 0 <= b < NUNITS:
                    w = window_of(unit(b)[0])[1]
                    wait_filled(act, "turn", b)
                    bank = 6 + b % 2
                    src = ps[:, bank, :].rearrange("p (i t) -> p i t", t=P)
                    nc.scalar.activation(pT[:w, b % 2], src[:w, 0:2], ACT.Copy)
                    nc.scalar.activation(pTm[:, b % 2], src[:META, 2:4], ACT.Copy).then_inc(taken[bank], 1)
                if a < NUNITS:
                    w = META + window_of(unit(a)[0])[1]
                    s = a % 2
                    act.wait_ge(max_ready, a + 1)
                    if a >= 4:
                        wait_filled(act, "turn", a - 4)
                    for ip in range(2):
                        at = ip * (META + WIN)
                        nc.scalar.activation(prob[:, a % 4, ip, 0:w], ps[:, 4 + s, at:at + w], ACT.Exp,
                                             scale=DH ** -0.5, bias=neg_amax[:, s, ip:ip + 1],
                                             accum_out=asum[:, s, ip:ip + 1])
                    act.wait_ge(sink_ready, a + 1)
                    nc.scalar.activation(sink_exp[:, s, :], sink_arg[:, s, :], ACT.Exp).then_inc(taken[4 + s], 1)
                b = a - ATT_LAG - 1
                if 0 <= b < NUNITS and b % 2:
                    c, pr, _ = unit(b)
                    key = ("pv", b // 2)
                    wait_filled(act, *key)
                    src = ps[:, use[key][0], 0:2 * P].rearrange("p (i t) -> p i t", i=4)
                    nc.scalar.activation(yah[:, 4 * pr:4 * pr + 4, ATT_CHUNK * c:ATT_CHUNK * (c + 1)], src,
                                         ACT.Copy).then_inc(ya_hi, 1)

            def next_gate(m):
                if m + 2 < 2 * KT:
                    slot, before = slot_of(B_BB + m)
                    act.wait_ge(freed[slot], before + 1)
                    load_gate(m + 2)

            def merged_hi(m):
                act.wait_ge(merged_ready, m + 1)
                nc.scalar.activation(mgh[:, m, :], merged[:, m, :], ACT.Copy).then_inc(mg_hi, 1)

            scale_tile(0)
            scale_tile(2)
            split_hi(0)
            split_hi(1)
            for i in range(3):
                hi_of_tile(("hT", i), hTh, *token_span(i))
            scale_tile(3)
            split_hi(2)
            for i in range(3, TT + 1):
                hi_of_tile(("hT", i), hTh, *token_span(i))
            act.wait_ge(const_landed, 3 * 16)
            gdn_tiles(act, gdn_tile)
            for what, *at in steps:
                if what == "block":
                    b = at[0]
                    if b < B_BB:
                        projection(b)
                        split_hi(b + RING)
                        if b == B_BA:
                            silu_of_conv(b - 1)
                    else:
                        split_hi(b + RING)
                        merged_hi(b - B_BA2)
                        next_gate(b - B_BB)
                elif what == "sideend":
                    b = at[0]
                    if b < B_BB:
                        side_tile(b)
                    split_hi(b + RING)
                    if b >= B_BB:
                        next_gate(b - B_BB)
                elif what == "logits":
                    log_decay_terms()
                elif what == "decays":
                    decays()
                elif what == "delta":
                    delta(*at)
                elif what == "reload":
                    reload()
                elif what == "values":
                    values()
                elif what == "att":
                    attention(at[0])
                    if at[0] == NUNITS + ATT_LAG:
                        act.dma_start(orow[:], rows[R_BOUT:R_BOUT + 3, :].partition_broadcast(P)).then_inc(rows_landed, 16)
            for b in range(B_OUT, B_F1 - RING):
                split_hi(b + RING)
            scale_tile(TT + 1)
            split_hi(B_F1)
            split_hi(B_F1 + 1)
            for t in range(TT):
                hi_of_tile(("h1T", t), h1h, P * t, P)
                if t == 1:
                    split_hi(B_F1 + 2)
            def silu_of_gate(f, turn):
                b = B_F1 + 2 * f
                slot, up = slot_of(b)[0], slot_of(b + 1)
                act.wait_ge(w_used, later(b + 1, turn, 2 * TURN))
                nc.scalar.activation(sgate[:, f % TURN, :], ps[:, 2 * slot, :], ACT.Silu).then_inc(freed[slot], 1)
                split_hi(b + RING, turn)
                split_hi(b + 1 + RING, turn)
                act.wait_ge(freed[up[0]], later(up[1] + 1, turn, TURN))
                nc.scalar.activation(hidh[:, later(f, turn, TURN), :], hid[:, f % TURN, :], ACT.Copy).then_inc(hid_hi, 1)
                if f == 0:
                    act.dma_start(frow[:], rows[R_LN2:R_LN2 + 2, :].partition_broadcast(P)).then_inc(rows_landed, 16)

            hidden_tiles(act, silu_of_gate)
            last_splits(act, split_hi)
            scale_tile(2 * TT + 1)

        @block.vector
        def _(dve):
            own = [0]

            def step(ins):
                own[0] += 1
                ins.then_inc(dve_step, 1)
                dve.wait_ge(dve_step, own[0])

            def tell(ins, semaphore, value):
                ins.then_inc(semaphore, 1)
                dve.wait_ge(semaphore, value)

            def take(ins, *key):
                bank, before = use[key]
                tell(ins, taken[bank], before + 1)

            def free_slot(ins, b):
                slot, before = slot_of(b)
                tell(ins, freed[slot], before + 1)

            def half_stats(i, j):
                src, _, c, _ = norm_tile(i)
                step(nc.vector.bn_stats(st6[:c, i % NORMS, j, :], src[:, 512 * j:512 * (j + 1)]))

            def variance(i):
                _, _, c, _ = norm_tile(i)
                m = i % NORMS
                step(nc.vector.bn_aggr(mv[:c, m, :], st6[:c, m, :, :]))
                tell(nc.vector.tensor_scalar(var_eps[:c, m:m + 1], mv[:c, m, 1:2], LN_EPS, None, ALU.add),
                     var_ready, i + 1)

            def gain_tile(i):
                src, dst, c, rows_ = norm_tile(i)
                mean = mv[:c, i % NORMS, 0:1]
                tell(nc.vector.scalar_tensor_tensor(out=dst, in0=src, scalar=mean, in1=rows_[:c, 0, :],
                                                    op0=ALU.subtract, op1=ALU.mult), gained, i + 1)

            def finish_tile(i):
                _, dst, c, rows_ = norm_tile(i)
                dve.wait_ge(rstd_ready, i + 1)
                m = i % NORMS
                tell(nc.vector.scalar_tensor_tensor(out=dst, in0=dst, scalar=rstd[:c, m:m + 1], in1=rows_[:c, 1, :],
                                                    op0=ALU.mult, op1=ALU.add), normed_by_vector, normed_before(i) + 1)

            def lo_of_tile(key, hi, lo, at, c, n):
                dve.wait_ge(hT_hi, n + 1)
                src = pair_view(use[key][0])[:, :, :c]
                s = slice(at, at + c)
                ins = nc.vector.tensor_tensor(lo[:, :, s], src, hi[:, :, s].bitcast(F32), ALU.subtract)
                bank, before = use[key]
                ins.then_inc(taken[bank], 1)
                dve.wait_ge(taken[bank], before + 1)

            def convolve(b, turn):
                slot, before = slot_of(b)
                dve.wait_ge(freed[slot], later(before + 1, turn, TURN))
                if b >= 2:
                    dve.wait_ge(silu_done, later(b - 1, turn, 2 * TURN))
                acc = cacc[:, b % 2, :]
                for i in range(CONV_K):
                    at = later(COL_CONV + CONV_K * b + i, turn, CONV_K * 2 * TURN)
                    tap = col[:, bass.ds(at, 1)]
                    src = cbuf[:, b % 2, i:i + NT]
                    if i == 0:
                        nc.vector.tensor_scalar(acc, src, tap, None, ALU.mult).then_inc(conv_step, 1)
                        dve.wait_ge(conv_step, later((CONV_K - 1) * b + i + 1, turn, (CONV_K - 1) * 2 * TURN))
                        continue
                    ins = nc.vector.scalar_tensor_tensor(out=acc, in0=src, scalar=tap, in1=acc,
                                                         op0=ALU.mult, op1=ALU.add)
                    if i < CONV_K - 1:
                        ins.then_inc(conv_step, 1)
                        dve.wait_ge(conv_step, later((CONV_K - 1) * b + i + 1, turn, (CONV_K - 1) * 2 * TURN))
                    else:
                        ins.then_inc(conv_done, 1)

            def decay_logits():
                wait_filled(dve, "logits")
                n = TT + 1
                src = ps[:, 4, 0:16 * n].rearrange("p (n m) -> p n m", m=16)
                row = lambda at, w: srt[:, at:at + w].unsqueeze(1).to_broadcast([P, n, w])
                take(nc.vector.tensor_tensor(logits[:], src, row(S_BIAS, 16), ALU.add), "logits")
                tell(nc.vector.tensor_tensor(la[:], logits[:, :, GH:], row(S_DT, GH), ALU.add), prep, 1)
                tell(nc.vector.scalar_tensor_tensor(out=soft[:], in0=la[:], scalar=-1.0, in1=la[:],
                                                    op0=ALU.mult, op1=ALU.max), prep, 2)
                dve.wait_ge(prep_act, 1)
                step(nc.vector.scalar_tensor_tensor(out=la[:], in0=la[:], scalar=0.0, in1=soft[:],
                                                    op0=ALU.max, op1=ALU.add))
                step(nc.vector.tensor_scalar(neg_a[:], neg_a[:], -1.0, None, ALU.mult))
                tell(nc.vector.tensor_scalar(beta[:], beta[:], 0.5, 0.5, ALU.mult, ALU.add), prep, 3)
                tell(nc.vector.tensor_tensor(la[:], la[:], neg_a[:, :].unsqueeze(1).to_broadcast([P, n, GH]),
                                             ALU.mult), prep, 4)

            def delta(stage, n, g):
                t0, c = chunk_of(n)
                key = (stage, n, g)
                kind = stage[0]
                hs = slice(4 * g, 4 * g + 4)
                tt = nc.vector.tensor_tensor
                if kind == "k":
                    if n > 1:
                        scale_output(n - 1, g)
                    step_la = per_head(la[:c, n, hs], c, c)
                    tell(tt(heads(tri_la, g, c, c), over_heads(C_INCL, c), step_la, ALU.mult), tri_ready, 2 * n + g + 1)
                    wait_taken(dve, *key)
                    step(nc.vector.tensor_reduce(kss[:c, g, :], heads(ksq, g, c, P), AX_X, ALU.add))
                    tell(nc.vector.tensor_scalar(kss[:c, g, :], kss[:c, g, :], NORM_EPS, None, ALU.add),
                         kss_ready[g], n + 1)
                    step(nc.vector.reciprocal(rk2[:c, g, :], kss[:c, g, :]))
                    step(tt(rho[:c, g, :], rk2[:c, g, :], beta[:c, n, hs], ALU.mult))
                elif kind == "q":
                    wait_taken(dve, *key)
                    step(nc.vector.tensor_reduce(qss[:c, g, :], heads(qsq, g, c, P), AX_X, ALU.add))
                    tell(nc.vector.tensor_scalar(qss[:c, g, :], qss[:c, g, :], NORM_EPS, None, ALU.add),
                         qss_ready[g], n)
                elif kind == "v":
                    wait_filled(dve, *key)
                    dve.wait_ge(knorm_ready[g], n + 1)
                    take(tt(heads(vtok, g, c, P), bank4(key, c, P), per_head(knorm[:c, g, :], c, P), ALU.mult), *key)
                elif kind == "g":
                    wait_filled(dve, *key)
                    take(tt(heads(U, g, c, c), bank4(key, c, c), heads(dec, g, c, c), ALU.mult), *key)
                    step(tt(heads(U, g, c, c), heads(U, g, c, c), per_head(rho[:c, g, :], c, c), ALU.mult))
                    mask_level(n, g, c, 0)
                    tell(tt(heads(XT, g, c, c), over_heads(C_IDENT, c), heads(UL[0], g, c, c), ALU.subtract),
                         xt_ready[g], n + 1)
                elif kind == "w":
                    wait_filled(dve, *key)
                    take(tt(heads(AT, g, c, c), bank4(key, c, c), heads(dec, g, c, c), ALU.mult), *key)
                elif kind == "d":
                    wait_taken(dve, *key)
                    step(tt(heads(dec, g, c, c), heads(dec, g, c, c), over_heads(C_INCL, c), ALU.mult))
                elif kind == "i":
                    mask_level(n, g, c, 1)
                elif kind == "y":
                    if int(stage[1:]) + 1 < levels_of(n):
                        mask_level(n, g, c, int(stage[1:]) + 1)
                elif kind == "z":
                    wait_filled(dve, *key)
                    level, h2 = int(stage[1:]), c // 2
                    if level < levels_of(n) - 1:
                        size = 1 << level
                        old = heads(X, g, c, c).rearrange("p h (b two s) -> p h b two s", two=2, s=size)[:, :, :, 0]
                        new = bank4(key, c, h2).rearrange("p h (b s) -> p h b s", s=size)
                    else:
                        old, new = XT[:h2, g, :, h2:c], bank4(key, h2, h2)
                    take(tt(old, old, new, ALU.subtract), *key)
                elif kind == "s":
                    wait_filled(dve, *key)
                    take(tt(heads(Y, g, c, P), bank4(key, c, P), per_head(neg_eg[:c, n, hs], c, P), ALU.mult), *key)
                    tell(tt(heads(vtok, g, c, P), heads(vtok, g, c, P), heads(Y, g, c, P), ALU.add), r_ready[g], n)
                elif kind == "p":
                    wait_filled(dve, *key)
                    take(tt(heads(vnew, g, c, P), bank4(key, c, P), per_head(rho[:c, g, :], c, P), ALU.mult), *key)
                elif kind == "r":
                    wait_filled(dve, *key)
                    take(tt(heads(oraw, g, c, P), bank4(key, c, P), per_head(eg[:c, n, 0, hs], c, P), ALU.mult), *key)
                elif kind == "o":
                    wait_filled(dve, *key)
                    take(tt(heads(oraw, g, c, P), heads(oraw, g, c, P), bank4(key, c, P), ALU.add), *key)
                    dve.wait_ge(rq_ready[g], n)
                    step(nc.vector.tensor_scalar(rq[:, g, :], rq[:, g, :], DK ** -0.5, None, ALU.mult))
                    step(tt(rq2[:, g, :], rq[:, g, :], rq[:, g, :], ALU.mult))
                    step(tt(osq[:, g], oraw[:, g], oraw[:, g], ALU.mult))
                    step(nc.vector.tensor_reduce(oss[:, g, :], osq[:, g], AX_X, ALU.add))
                    step(nc.vector.scalar_tensor_tensor(out=oss[:, g, :], in0=oss[:, g, :], scalar=1.0 / DK,
                                                        in1=rq2[:, g, :], op0=ALU.mult, op1=ALU.mult))
                    tell(nc.vector.tensor_scalar(oss[:, g, :], oss[:, g, :], NORM_EPS, None, ALU.add), oss_ready[g], n)
                    if n == TT:
                        scale_output(n, g)
                elif kind == "t":
                    s = state[:, hs, :]
                    if n:
                        step(tt(s, s, per_head(eg[:, n, 2, hs], P, P), ALU.mult))
                    wait_filled(dve, *key)
                    if n:
                        take(tt(s, s, bank4(key, P, P), ALU.add), *key)
                    else:
                        take(nc.vector.tensor_copy(s, bank4(key, P, P)), *key)
                elif kind == "f":
                    wait_filled(dve, *key)
                    gated = sz[:, hs, t0 - META:t0 - META + P]
                    take(nc.vector.scalar_tensor_tensor(out=youT[:, g], in0=bank4(key, P, P),
                                                        scalar=col[:, COL_NORM:COL_NORM + 1], in1=gated,
                                                        op0=ALU.mult, op1=ALU.mult), *key)

            def mask_level(n, g, c, level):
                tell(nc.vector.tensor_tensor(heads(UL[level % 2], g, c, c), heads(U, g, c, c),
                                             over_heads(C_LEVEL + level, c), ALU.mult),
                     level_ready[g], levels_before(n) + level + 1)

            def scale_output(n, g):
                dve.wait_ge(onorm_ready[g], n)
                step(nc.vector.tensor_tensor(onorm[:, g, :], onorm[:, g, :], rq[:, g, :], ALU.mult))
                tell(nc.vector.tensor_tensor(oraw[:, g], oraw[:, g], per_head(onorm[:, g, :], P, P), ALU.mult),
                     o_ready[g], n)

            def gate_of_side(b):
                j = b - B_SIDE
                if j < SIDE_AQ:
                    return
                slot, before = slot_of(b)
                dve.wait_ge(freed[slot], before + 1)
                s = side[:, j % 3, 0:SEQ]
                tell(nc.vector.tensor_scalar(s, s, 0.5, 0.5, ALU.mult, ALU.add), side_ready, j - SIDE_AQ + 1)

            def branch(b):
                m = b - B_BB
                slot, _ = slot_of(b)
                dve.wait_ge(w_used, b + 1)
                dve.wait_ge(gate_loaded[m % 2], 16 * (m // 2 + 1))
                src = ps[:, 2 * slot, :]
                if m < KT:
                    free_slot(nc.vector.tensor_tensor(merged[:, m, :], src, gate[:, m % 2, :], ALU.mult), b)
                    return
                free_slot(nc.vector.tensor_tensor(prod[:, m % 2, :], src, gate[:, m % 2, :], ALU.mult), b)
                if m == KT:
                    dve.wait_ge(rows_landed, 3 * 16)
                if m < KT + TT:
                    t = m - KT
                    step(nc.vector.scalar_tensor_tensor(out=h[:, t, :], in0=h[:, t, :], scalar=ALPHA,
                                                        in1=orow[:, 0, :], op0=ALU.mult, op1=ALU.add))
                dst = merged[:, m - KT, :]
                tell(nc.vector.tensor_tensor(dst, dst, prod[:, m % 2, :], ALU.add), merged_ready, m - KT + 1)

            def attention(a):
                if a < NUNITS:
                    w = META + window_of(unit(a)[0])[1]
                    s, group = a % 2, a % 4
                    wait_filled(dve, "scores", a)
                    src = ps[:, 4 + s, 0:2 * (META + WIN)].rearrange("p (i t) -> p i t", i=2)[:, :, 0:w]
                    step(nc.vector.tensor_reduce(amax[:, s, :], src, AX_X, ALU.max))
                    sink = col[:, COL_SINK + 2 * group:COL_SINK + 2 * group + 2]
                    minus_sink = minus_sinks[:, 2 * group:2 * group + 2]
                    tell(nc.vector.scalar_tensor_tensor(out=neg_amax[:, s, :], in0=amax[:, s, :], scalar=-DH ** -0.5,
                                                        in1=minus_sink, op0=ALU.mult, op1=ALU.min), max_ready, a + 1)
                    nc.vector.tensor_tensor(sink_arg[:, s, :], sink, neg_amax[:, s, :], ALU.add).then_inc(sink_ready, 1)
                if 1 <= a <= NUNITS:
                    b = a - 1
                    s = b % 2
                    wait_taken(dve, "scores", b)
                    step(nc.vector.tensor_tensor(atot[:, s, :], asum[:, s, :], sink_exp[:, s, :], ALU.add))
                    if b >= 4:
                        dve.wait_ge(prob_ready, b - 3)
                    nc.vector.reciprocal(arec[:, b % 4, :], atot[:, s, :]).then_inc(arec_ready, 1)
                b = a - ATT_LAG - 1
                if 0 <= b < NUNITS and b % 2:
                    c, pr, _ = unit(b)
                    key = ("pv", b // 2)
                    dve.wait_ge(ya_hi, b // 2 + 1)
                    src = ps[:, use[key][0], 0:2 * P].rearrange("p (i t) -> p i t", i=4)
                    at = (slice(None), slice(4 * pr, 4 * pr + 4), slice(ATT_CHUNK * c, ATT_CHUNK * (c + 1)))
                    take(nc.vector.tensor_tensor(yal[at], src, yah[at].bitcast(F32), ALU.subtract), *key)

            def wait_half(name, half, t, last_block):
                if t < TT - 1:
                    wait_filled(dve, name, half, t)
                else:
                    dve.wait_ge(w_used, last_block + 1)

            def add_mixer(half, t):
                wait_half("out", half, t, B_OUT + KT // 2 * (half + 1) - 1)
                dst = h[:, t, 512 * half:512 * (half + 1)]
                take(nc.vector.tensor_tensor(dst, dst, ps[:, use[("out", half, t)][0], :], ALU.add), "out", half, t)
                half_stats(TT + 1 + t, half)

            def add_ffn(half, t):
                wait_half("ffn", half, t, B_F2 + FT // 2 * (half + 1) - 1)
                cs = slice(512 * half, 512 * (half + 1))
                take(nc.vector.scalar_tensor_tensor(out=res[:, t, cs], in0=h[:, t, cs], scalar=ALPHA,
                                                    in1=ps[:, use[("ffn", half, t)][0], :],
                                                    op0=ALU.mult, op1=ALU.add), "ffn", half, t)
                half_stats(2 * TT + 1 + t, half)

            step(nc.vector.memset(cbuf[:, :, 0:CONV_K - 1], 0.0))
            step(nc.vector.memset(half[:], 0.5))
            tell(nc.vector.memset(minus_half[:], -0.5), powers_ready, 1)
            def input_stats(i):
                dve.wait_ge(x_landed[i], 16)
                half_stats(i, 0)
                half_stats(i, 1)
                variance(i)

            def input_lo(i):
                lo_of_tile(("hT", i), hTh, hTl, *token_span(i), i)

            input_stats(0)
            input_stats(1)
            input_stats(2)
            dve.wait_ge(rows_landed, 2 * 16)
            gain_tile(0)
            gain_tile(1)
            gain_tile(2)
            finish_tile(1)
            input_stats(3)
            gain_tile(3)
            for i in range(3):
                input_lo(i)
            input_stats(4)
            gain_tile(4)
            finish_tile(4)
            input_lo(3)
            input_lo(4)
            dve.wait_ge(const_landed, 3 * 16)
            step(nc.vector.tensor_scalar(halfcol[:], col[:], 0.5, None, ALU.mult))
            step(nc.vector.tensor_scalar(minus_sinks[:], col[:, COL_SINK:COL_SINK + 8], -1.0, None, ALU.mult))
            gdn_tiles(dve, convolve)
            for what, *at in steps:
                if what == "block" and at[0] >= B_BB or what == "sideend" and at[0] >= B_BB:
                    branch(at[0])
                elif what == "sideend":
                    gate_of_side(at[0])
                elif what == "logits":
                    decay_logits()
                elif what == "decays":
                    wait_taken(dve, "decays")
                    step(nc.vector.tensor_scalar(neg_eg[:], eg[:, :, 0, :], -1.0, None, ALU.mult))
                elif what == "delta":
                    delta(*at)
                elif what == "att":
                    attention(at[0])
            for t in range(TT):
                add_mixer(0, t)
            def h1_lo(t):
                lo_of_tile(("h1T", t), h1h, h1l, P * t, P, TT + 1 + t)

            for t in range(TT):
                i = TT + 1 + t
                add_mixer(1, t)
                variance(i)
                if t == TT - 1:
                    for before in range(t):
                        h1_lo(before)
                gain_tile(i)
                if on_vector(i):
                    finish_tile(i)
            h1_lo(TT - 1)

            def hidden(f, turn):
                b = B_F1 + 2 * f + 1
                (gslot, gbefore), (slot, before) = slot_of(b - 1), slot_of(b)
                dve.wait_ge(w_used, later(b + 1, turn, 2 * TURN))
                dve.wait_ge(freed[gslot], later(gbefore + 1, turn, TURN))
                if f >= TURN:
                    dve.wait_ge(hid_lo, later(f - TURN + 1, turn, TURN))
                nc.vector.tensor_tensor(hid[:, f % TURN, :], ps[:, 2 * slot, :], sgate[:, f % TURN, :],
                                        ALU.mult).then_inc(freed[slot], 1)

            hidden_tiles(dve, hidden)
            dve.wait_ge(rows_landed, 4 * 16)
            for t in range(TT):
                add_ffn(0, t)
            for t in range(TT):
                i = 2 * TT + 1 + t
                add_ffn(1, t)
                variance(i)
                gain_tile(i)
                if on_vector(i):
                    finish_tile(i)

        @block.gpsimd
        def _(pool):
            def split_lo(b, turn=None, blocks=2 * TURN):
                if b >= NBLOCKS:
                    return
                s = b % RING
                pool.wait_ge(w_hi, later(b + 1, turn, blocks))
                if b >= RING:
                    pool.wait_ge(w_used, later(b - RING + 1, turn, blocks))
                nc.gpsimd.tensor_tensor(wlo[:, s, :], wst[:, s, :], whi[:, s, :].bitcast(F32),
                                        ALU.subtract).then_inc(w_lo, 1)

            def power(dst, src, exponent, semaphore, wait, value):
                pool.wait_ge(wait, value)
                nc.gpsimd.tensor_tensor(dst, src, exponent, ALU.pow).then_inc(semaphore, 1)

            def norm_power(i):
                c = norm_tile(i)[2]
                m = slice(i % NORMS, i % NORMS + 1)
                power(rstd[:c, m], var_eps[:c, m], minus_half[:c, 0:1], rstd_ready, var_ready, i + 1)

            def add_offset(i):
                _, dst, c, rows_ = norm_tile(i)
                pool.wait_ge(scaled, normed_before(i) + 1)
                nc.gpsimd.tensor_tensor(dst, dst, rows_[:c, 1, :], ALU.add).then_inc(normed_by_pool, 1)

            def delta(stage, n, g):
                c = chunk_of(n)[1]
                kind = stage[0]
                hs = slice(4 * g, 4 * g + 4)
                tt = nc.gpsimd.tensor_tensor
                small = (slice(0, c), g)
                if kind == "k":
                    power(knorm[small], kss[small], half[:c, 0:4], knorm_ready[g], kss_ready[g], n + 1)
                elif kind == "q":
                    power(rq[small], qss[small], minus_half[:c, 0:4], rq_ready[g], qss_ready[g], n)
                elif kind == "p" and n < TT:
                    wait_taken(pool, stage, n, g)
                    tt(heads(vdec, g, c, P), heads(vnew, g, c, P), per_head(eg[:c, n, 1, hs], c, P),
                       ALU.mult).then_inc(vdec_ready[g], 1)
                elif kind == "o":
                    power(onorm[small], oss[small], minus_half[:c, 0:4], onorm_ready[g], oss_ready[g], n)
                elif kind == "f":
                    t0 = chunk_of(n)[0]
                    pool.wait_ge(yh_ready[g], n)
                    at = (slice(None), hs, slice(t0, t0 + P))
                    tt(yl[at], youT[:, g], yh[at].bitcast(F32), ALU.subtract).then_inc(yl_ready[g], 1)

            def normalise_probs(a):
                if 0 <= a < NUNITS:
                    w = META + window_of(unit(a)[0])[1]
                    pr_ = prob[:, a % 4, :, 0:w]
                    pool.wait_ge(arec_ready, a + 1)
                    nc.gpsimd.tensor_tensor(pr_, pr_, arec[:, a % 4, :].unsqueeze(2).to_broadcast([P, 2, w]),
                                            ALU.mult).then_inc(prob_ready, 1)

            def norms(first):
                norm_power(first)
                add_offset(first)
                for i in (1, 2):
                    norm_power(first + i)

            pool.wait_ge(powers_ready, 1)
            norm_power(0)
            norm_power(1)
            norm_power(2)
            add_offset(0)
            add_offset(2)
            split_lo(0)
            norm_power(3)
            split_lo(1)
            norm_power(4)
            add_offset(3)
            split_lo(2)
            gdn_tiles(pool, lambda b, turn: split_lo(b + RING, turn))
            for what, *at in steps:
                if what in ("block", "sideend"):
                    b = at[0]
                    split_lo(b + RING)
                    if b >= B_BA2:
                        m = b - B_BA2
                        pool.wait_ge(mg_hi, m + 1)
                        nc.gpsimd.tensor_tensor(mgl[:, m, :], merged[:, m, :], mgh[:, m, :].bitcast(F32),
                                                ALU.subtract).then_inc(mg_lo, 1)
                elif what == "delta":
                    delta(*at)
                elif what == "att":
                    normalise_probs(at[0] - 1)
            for b in range(B_OUT, B_F1 - RING):
                split_lo(b + RING)
            norms(TT + 1)
            split_lo(B_F1)
            split_lo(B_F1 + 1)
            norm_power(2 * TT)
            split_lo(B_F1 + 2)
            def hidden_lo(f, turn):
                split_lo(B_F1 + 2 * f + RING, turn)
                split_lo(B_F1 + 2 * f + 1 + RING, turn)
                pool.wait_ge(hid_hi, later(f + 1, turn, TURN))
                at = later(f, turn, TURN)
                nc.gpsimd.tensor_tensor(hidl[:, at, :], hid[:, f % TURN, :], hidh[:, at, :].bitcast(F32),
                                        ALU.subtract).then_inc(hid_lo, 1)

            hidden_tiles(pool, hidden_lo)
            last_splits(pool, split_lo)
            norms(2 * TT + 1)
            norm_power(3 * TT)


def constant_matrices():
    j, i = np.mgrid[0:P, 0:P]
    mats = [j == i, j <= i, j > i, j >= 0]
    for level in range(LEVELS):
        size = 1 << level
        mats.append((i // (2 * size) == j // (2 * size)) & (i // size % 2 == 1) & (j // size % 2 == 0))
    return np.ascontiguousarray(np.stack(mats, 1).astype(np.float32))


def lay_out(a):
    w_in, b_in = a["w_in"][0], a["b_in"][0]
    at = np.cumsum([0, A_HEADS * DH, A_KV * DH, A_KV * DH, GH * DK, GH * DK, GH * DK, GH * DK, GH, GH, D, D])
    aq, ak, av, gq, gk, gv, gz, gb, ga, mga, mgb = at[:-1]
    heads = [8 * pr + 4 * e + i for pr in range(2) for i in range(4) for e in range(2)]
    aq_rows = np.concatenate([np.arange(DH * h, DH * (h + 1)) for h in heads])
    tiles = [np.arange(start + P * i, start + P * (i + 1)) for start in (gk, gv, gq) for i in range(GH)]
    tiles += [np.arange(gb, gb + P)]
    tiles += [np.arange(gz + P * i, gz + P * (i + 1)) for i in range(GH)]
    tiles += [np.arange(start + P * i, start + P * (i + 1)) for start in (ak, av) for i in range(2)]
    tiles += [aq + aq_rows[P * i:P * (i + 1)] for i in range(KT)]
    tiles += [np.arange(start + P * i, start + P * (i + 1)) for start in (mgb, mga) for i in range(KT)]

    def columns(w, which):
        return w[:, which].reshape(KT, P, P).transpose(1, 0, 2).reshape(P, D)

    def rows_of(w, half):
        part = w[:, 512 * half:512 * (half + 1)].reshape(-1, 2, P, 512)
        return list(part.transpose(0, 2, 1, 3).reshape(-1, P, D))

    blocks = [columns(w_in, which) for which in tiles]
    wb, wa = a["w_branch_b"][0], a["w_branch_a"][0][aq_rows]
    for w in (wb, wa):
        blocks += [columns(w, np.arange(P * m, P * (m + 1))) for m in range(KT)]
    for half in range(2):
        blocks += rows_of(a["w_out"][0], half)
    for f in range(FT):
        for start in (0, FFN):
            blocks.append(columns(a["w_ffn_in"][0], np.arange(start + P * f, start + P * (f + 1))))
    for half in range(2):
        blocks += rows_of(a["w_ffn_out"][0], half)
    wstream = np.stack(blocks)
    conv = a["conv_w"][0]
    conv_tiles = [conv[:, start + P * i:start + P * (i + 1)].T
                  for start in (GH * DK, 2 * GH * DK, 0) for i in range(GH)]
    sinks = a["attn_sinks"][0]
    sink_cols = [np.repeat(sinks[4 * (2 * pr + e) + 2 * ip:4 * (2 * pr + e) + 2 * ip + 2], P // 2)
                 for pr in range(2) for e in range(2) for ip in range(2)]
    cols = np.concatenate([np.stack([b_in[which] for which in tiles], 1), *conv_tiles,
                           a["gdn_norm_g"][0][:, None], np.stack(sink_cols, 1)], 1)
    rows = np.stack([a["ln_in_g"], a["ln_in_b"], a["b_out"][0], a["ln1_g"][0], a["ln1_b"][0],
                     a["ln2_g"][0], a["ln2_b"][0]])
    short = np.concatenate([b_in[gb:gb + GH], b_in[ga:ga + GH], a["a_log"][0], a["dt_bias"][0]])
    return {"x": a["x"][0], "meta": a["meta"], "wstream": wstream, "consts": constant_matrices(),
            "cols": cols, "rows": rows, "short": short}


def kernel(**inputs):
    import concourse.bacc as bacc
    from concourse.bass_utils import run_bass_kernel_spmd

    arrays = {k: np.ascontiguousarray(v) for k, v in lay_out({k: np.asarray(v) for k, v in inputs.items()}).items()}
    nc = bacc.Bacc("TRN2", target_bir_lowering=False, num_devices=1, dynamic_dma_scratch_size=1024)
    args = [nc.dram_tensor(f"in_{k}", v.shape, F32, kind="ExternalInput").ap() for k, v in arrays.items()]
    result = nc.dram_tensor("out_0", (SEQ, D), F32, kind="ExternalOutput").ap()
    build(nc, *args, result)
    r = run_bass_kernel_spmd(nc, [{f"in_{k}": v for k, v in arrays.items()}], core_ids=[0])
    return r.results[0]["out_0"].reshape(1, SEQ, D)
```
